# Optimizing a Trainium2 kernel written in Bass

```python
import math
import jax, jax.numpy as jnp
from jax import lax
import numpy as np

'''One inference step of a hybrid decoder layer stack (Hymba-style parallel head groups).

Each layer: RMSNorm -> ONE combined q/k/v projection whose columns are split between
  head group A: differential attention (4 heads, q/k halves of 64, value width 128,
                learned lambda, headwise RMSNorm * (1 - lambda_init), T5 relative bias)
  head group B: stick-breaking attention (8 heads of 64, no positional encoding,
                strictly causal, log-space stick-breaking weights)
-> concat (1024) -> ONE output projection -> residual add;
RMSNorm -> hierarchical MoE (top-1 of 4 expert groups, then top-2 of 4 SwiGLU experts) -> residual add.
Final RMSNorm.

Inputs:
  x_prompt      (BATCH, SEQ, D_MODEL)        new sequences, positions 0..SEQ-1
  x_sample      (DEC_BATCH, DEC_SEQ, D_MODEL) new tokens at positions PAST_LEN..PAST_LEN+DEC_SEQ-1
  cache_kv_diff (N_POOL, PAGE_SIZE, DEPTH, 2, H_DIFF, 2*HEAD_DIM)  paged [k1|k2] and v rows of group A
  cache_kv_sb   (N_POOL, PAGE_SIZE, DEPTH, 2, H_SB, HEAD_DIM)      paged k and v rows of group B
  page_table    (DEC_BATCH, N_PAGES) int32, N_PAGES = PAST_LEN // PAGE_SIZE
  weights (per-layer arrays carry a leading DEPTH axis; rel_bias is shared by all layers)
Outputs (tuple):
  y_prompt           (BATCH, SEQ, D_MODEL)
  y_sample           (DEC_BATCH, DEC_SEQ, D_MODEL)
  new_kv_diff_prompt (BATCH, SEQ, DEPTH, 2, H_DIFF, 2*HEAD_DIM)
  new_kv_sb_prompt   (BATCH, SEQ, DEPTH, 2, H_SB, HEAD_DIM)
  new_kv_diff_sample (DEC_BATCH, DEC_SEQ, DEPTH, 2, H_DIFF, 2*HEAD_DIM)
  new_kv_sb_sample   (DEC_BATCH, DEC_SEQ, DEPTH, 2, H_SB, HEAD_DIM)
'''

D_MODEL = 1024
BATCH = 1
SEQ = 1024
DEPTH = 1
DEC_BATCH = 8
DEC_SEQ = 8
PAST_LEN = 2048
PAGE_SIZE = 128

HEAD_DIM = 64
H_DIFF = 4
H_SB = 8
DIFF_W = H_DIFF * 2 * HEAD_DIM
SB_W = H_SB * HEAD_DIM
MIX_W = DIFF_W + SB_W
N_BUCKETS = 32
MAX_DISTANCE = 128
N_GROUPS = 4
EXPERTS_PER_GROUP = 4
TOP_K_INNER = 2
D_EXPERT = 256
Q_BLOCK = 128
NORM_EPS = 1e-6
SUBLN_EPS = 1e-5

kernel_name = 'hymba_diffattn_stickbreak_hmoe_step'

def lambda_init(layer):
    return 0.8 - 0.6 * math.exp(-0.3 * layer)

def rms_norm(x, g, eps=NORM_EPS):
    xf = x.astype(jnp.float32)
    y = xf * lax.rsqrt(jnp.mean(xf * xf, axis=-1, keepdims=True) + eps)
    return (y * g.astype(jnp.float32)).astype(x.dtype)

def project(h, w_in):
    B, T, _ = h.shape
    p = h @ w_in
    qd, kd, vd, qs, ks, vs = jnp.split(
        p, [DIFF_W, 2 * DIFF_W, 3 * DIFF_W, 3 * DIFF_W + SB_W, 3 * DIFF_W + 2 * SB_W], axis=-1)
    rd = lambda a: a.reshape(B, T, H_DIFF, 2 * HEAD_DIM)
    rs = lambda a: a.reshape(B, T, H_SB, HEAD_DIM)
    return rd(qd), rd(kd), rd(vd), rs(qs), rs(ks), rs(vs)

def rel_bucket(rel):
    n = jnp.maximum(-rel, 0)
    max_exact = N_BUCKETS // 2
    nf = jnp.maximum(n, 1).astype(jnp.float32)
    large = max_exact + (jnp.log(nf / max_exact) / math.log(MAX_DISTANCE / max_exact)
                         * (N_BUCKETS - max_exact)).astype(jnp.int32)
    large = jnp.minimum(large, N_BUCKETS - 1)
    return jnp.where(n < max_exact, n, large)

def diff_attention(q, k, v, q_pos, k_pos, rel_bias, lam, subln_g, lam_init):
    B, Tq, H, _ = q.shape
    Tk = k.shape[1]
    qf = q.astype(jnp.float32).reshape(B, Tq, H, 2, HEAD_DIM)
    kf = k.astype(jnp.float32).reshape(B, Tk, H, 2, HEAD_DIM)
    s = jnp.einsum('bqhcd,bkhcd->bchqk', qf, kf) * (HEAD_DIM ** -0.5)
    bias = jnp.transpose(rel_bias.astype(jnp.float32)[rel_bucket(k_pos[None, :] - q_pos[:, None])],
                         (2, 0, 1))
    mask = k_pos[None, :] <= q_pos[:, None]
    s = jnp.where(mask, s + bias, -jnp.inf)
    p = jax.nn.softmax(s, axis=-1)
    w = p[:, 0] - lam * p[:, 1]
    o = jnp.einsum('bhqk,bkhe->bqhe', w, v.astype(jnp.float32))
    o = o * lax.rsqrt(jnp.mean(o * o, axis=-1, keepdims=True) + SUBLN_EPS)
    o = o * subln_g.astype(jnp.float32) * (1.0 - lam_init)
    return o.reshape(B, Tq, H * 2 * HEAD_DIM)

def stick_breaking_attention(q, k, v, q_pos, k_pos):
    B, Tq, H, _ = q.shape
    z = jnp.einsum('bqhd,bkhd->bhqk', q.astype(jnp.float32), k.astype(jnp.float32)) * (HEAD_DIM ** -0.5)
    mask = k_pos[None, :] < q_pos[:, None]
    log_beta = jax.nn.log_sigmoid(z)
    log_rest = jnp.where(mask, jax.nn.log_sigmoid(-z), 0.0)
    suffix = lax.cumsum(log_rest, axis=3, reverse=True) - log_rest
    a = jnp.where(mask, jnp.exp(log_beta + suffix), 0.0)
    o = jnp.einsum('bhqk,bkhd->bqhd', a, v.astype(jnp.float32))
    return o.reshape(B, Tq, H * HEAD_DIM)

def mix(qd, qs, q_pos, kd, vd, ks, vs, k_pos, rel_bias, lam, subln_g, lam_init):
    od = diff_attention(qd, kd, vd, q_pos, k_pos, rel_bias, lam, subln_g, lam_init)
    osb = stick_breaking_attention(qs, ks, vs, q_pos, k_pos)
    return jnp.concatenate([od, osb], axis=-1)

def hmoe(x, w_group, b_group, w_erouter, b_erouter, w_gate, w_up, w_down):
    B, T, D = x.shape
    xt = x.reshape(B * T, D)
    xf = xt.astype(jnp.float32)
    gl = xf @ w_group.astype(jnp.float32) + b_group.astype(jnp.float32)
    pg = jax.nn.softmax(gl, axis=-1)
    g = jnp.argmax(gl, axis=-1)
    pg_sel = jnp.take_along_axis(pg, g[:, None], axis=1)[:, 0]
    el = jnp.einsum('nd,dge->nge', xf, w_erouter.astype(jnp.float32)) + b_erouter.astype(jnp.float32)
    el_g = jnp.take_along_axis(el, g[:, None, None], axis=1)[:, 0]
    tv, ti = lax.top_k(el_g, TOP_K_INNER)
    wi = jax.nn.softmax(tv, axis=-1)
    inner = jnp.einsum('nk,nke->ne', wi, jax.nn.one_hot(ti, EXPERTS_PER_GROUP, dtype=jnp.float32))
    gates = pg_sel[:, None, None] * jax.nn.one_hot(g, N_GROUPS, dtype=jnp.float32)[:, :, None] * inner[:, None, :]
    a = jax.nn.silu(jnp.einsum('nd,gedf->ngef', xt, w_gate)) * jnp.einsum('nd,gedf->ngef', xt, w_up)
    y = jnp.einsum('ngef,gefd->nd', a * gates[..., None].astype(a.dtype), w_down)
    return y.reshape(B, T, D).astype(x.dtype)

def setup_inputs(seed: int = 0) -> dict:
    key = jax.random.key(seed)
    ks = jax.random.split(key, 24)
    n_pages = PAST_LEN // PAGE_SIZE
    n_pool = (DEC_BATCH * n_pages * 5) // 4
    nrm = lambda k, s, sc: jax.random.normal(k, s, jnp.float32) * sc
    page_table = jax.random.permutation(ks[0], n_pool)[:DEC_BATCH * n_pages].reshape(DEC_BATCH, n_pages).astype(jnp.int32)
    return {
        'x_prompt': nrm(ks[1], (BATCH, SEQ, D_MODEL), 1.0),
        'x_sample': nrm(ks[2], (DEC_BATCH, DEC_SEQ, D_MODEL), 1.0),
        'cache_kv_diff': nrm(ks[3], (n_pool, PAGE_SIZE, DEPTH, 2, H_DIFF, 2 * HEAD_DIM), 1.0),
        'cache_kv_sb': nrm(ks[4], (n_pool, PAGE_SIZE, DEPTH, 2, H_SB, HEAD_DIM), 1.0),
        'page_table': page_table,
        'rel_bias': nrm(ks[5], (N_BUCKETS, H_DIFF), 0.5),
        'g_mix': 1.0 + nrm(ks[6], (DEPTH, D_MODEL), 0.02),
        'w_in': nrm(ks[7], (DEPTH, D_MODEL, 3 * MIX_W), D_MODEL ** -0.5),
        'lambda_q1': nrm(ks[8], (DEPTH, HEAD_DIM), 0.1),
        'lambda_k1': nrm(ks[9], (DEPTH, HEAD_DIM), 0.1),
        'lambda_q2': nrm(ks[10], (DEPTH, HEAD_DIM), 0.1),
        'lambda_k2': nrm(ks[11], (DEPTH, HEAD_DIM), 0.1),
        'subln_g': 1.0 + nrm(ks[12], (DEPTH, 2 * HEAD_DIM), 0.02),
        'w_out': nrm(ks[13], (DEPTH, MIX_W, D_MODEL), MIX_W ** -0.5),
        'g_ffn': 1.0 + nrm(ks[14], (DEPTH, D_MODEL), 0.02),
        'w_group': nrm(ks[15], (DEPTH, D_MODEL, N_GROUPS), D_MODEL ** -0.5),
        'b_group': nrm(ks[16], (DEPTH, N_GROUPS), 0.01),
        'w_erouter': nrm(ks[17], (DEPTH, D_MODEL, N_GROUPS, EXPERTS_PER_GROUP), D_MODEL ** -0.5),
        'b_erouter': nrm(ks[18], (DEPTH, N_GROUPS, EXPERTS_PER_GROUP), 0.01),
        'w_gate': nrm(ks[19], (DEPTH, N_GROUPS, EXPERTS_PER_GROUP, D_MODEL, D_EXPERT), D_MODEL ** -0.5),
        'w_up': nrm(ks[20], (DEPTH, N_GROUPS, EXPERTS_PER_GROUP, D_MODEL, D_EXPERT), D_MODEL ** -0.5),
        'w_down': nrm(ks[21], (DEPTH, N_GROUPS, EXPERTS_PER_GROUP, D_EXPERT, D_MODEL), D_EXPERT ** -0.5),
        'g_final': 1.0 + nrm(ks[22], (D_MODEL,), 0.02),
    }

def reference(x_prompt, x_sample, cache_kv_diff, cache_kv_sb, page_table, rel_bias, g_mix, w_in,
              lambda_q1, lambda_k1, lambda_q2, lambda_k2, subln_g, w_out, g_ffn, w_group, b_group,
              w_erouter, b_erouter, w_gate, w_up, w_down, g_final):
    xp, xs = x_prompt, x_sample
    B, S, _ = xp.shape
    DB, T, _ = xs.shape
    P = page_table.shape[1] * cache_kv_diff.shape[1]
    nb = S // Q_BLOCK
    p_pos = jnp.arange(S)
    s_qpos = P + jnp.arange(T)
    s_kpos = jnp.arange(P + T)
    kvd_p, kvs_p, kvd_s, kvs_s = [], [], [], []
    to_blocks = lambda a: jnp.moveaxis(a.reshape(B, nb, Q_BLOCK, *a.shape[2:]), 1, 0)
    for l in range(DEPTH):
        li = lambda_init(l)
        f32 = lambda a: a.astype(jnp.float32)
        lam = (jnp.exp(jnp.sum(f32(lambda_q1[l]) * f32(lambda_k1[l])))
               - jnp.exp(jnp.sum(f32(lambda_q2[l]) * f32(lambda_k2[l]))) + li)
        h = rms_norm(xp, g_mix[l])
        qd, kd, vd, qs, ks_, vs = project(h, w_in[l])

        def one_block(args, kd=kd, vd=vd, ks_=ks_, vs=vs, lam=lam, l=l, li=li):
            qdb, qsb, pb = args
            return mix(qdb, qsb, pb, kd, vd, ks_, vs, p_pos, rel_bias, lam, subln_g[l], li)

        o = lax.map(one_block, (to_blocks(qd), to_blocks(qs), p_pos.reshape(nb, Q_BLOCK)))
        o = jnp.moveaxis(o, 0, 1).reshape(B, S, MIX_W)
        xp = xp + o.astype(xp.dtype) @ w_out[l]
        xp = xp + hmoe(rms_norm(xp, g_ffn[l]), w_group[l], b_group[l], w_erouter[l], b_erouter[l],
                       w_gate[l], w_up[l], w_down[l])
        kvd_p.append(jnp.stack([kd, vd], axis=2))
        kvs_p.append(jnp.stack([ks_, vs], axis=2))
        h = rms_norm(xs, g_mix[l])
        qd, kd, vd, qs, ks_, vs = project(h, w_in[l])
        new_d = jnp.stack([kd, vd], axis=2)
        new_s = jnp.stack([ks_, vs], axis=2)
        past_d = cache_kv_diff[:, :, l][page_table].reshape(DB, P, 2, H_DIFF, 2 * HEAD_DIM)
        past_s = cache_kv_sb[:, :, l][page_table].reshape(DB, P, 2, H_SB, HEAD_DIM)
        all_d = jnp.concatenate([past_d, new_d.astype(past_d.dtype)], axis=1)
        all_s = jnp.concatenate([past_s, new_s.astype(past_s.dtype)], axis=1)
        o = mix(qd, qs, s_qpos, all_d[:, :, 0], all_d[:, :, 1], all_s[:, :, 0], all_s[:, :, 1],
                s_kpos, rel_bias, lam, subln_g[l], li)
        xs = xs + o.astype(xs.dtype) @ w_out[l]
        xs = xs + hmoe(rms_norm(xs, g_ffn[l]), w_group[l], b_group[l], w_erouter[l], b_erouter[l],
                       w_gate[l], w_up[l], w_down[l])
        kvd_s.append(new_d)
        kvs_s.append(new_s)
    y_prompt = rms_norm(xp, g_final)
    y_sample = rms_norm(xs, g_final)
    new_kv_diff_prompt = jnp.stack(kvd_p, axis=2)
    new_kv_sb_prompt = jnp.stack(kvs_p, axis=2)
    new_kv_diff_sample = jnp.stack(kvd_s, axis=2)
    new_kv_sb_sample = jnp.stack(kvs_s, axis=2)
    return (y_prompt, y_sample, new_kv_diff_prompt, new_kv_sb_prompt, new_kv_diff_sample, new_kv_sb_sample)


_drawn_inputs = setup_inputs


def setup_inputs(seed=0):
    import zlib

    import numpy as np

    out = dict(_drawn_inputs(seed))
    spreads = {}
    factors = {'lambda_k1': 6.469,
     'lambda_q2': 6.595,
     'subln_g': 10.841,
     'b_group': 19.628,
     'b_erouter': 27.828,
     'g_final': 7.972,
     'g_ffn': 3.515}
    for name, (base, spread) in spreads.items():
        noise = np.random.default_rng([zlib.crc32(name.encode()), seed]).standard_normal(out[name].shape)
        drawn = base * np.exp(spread * noise) if base else spread * noise
        out[name] = __import__('jax').numpy.asarray(drawn.astype(out[name].dtype))
    for name, factor in factors.items():
        out[name] = (out[name] * factor).astype(out[name].dtype)
    return out
```

```python
import math
from contextlib import ExitStack

import numpy as np
import concourse.bass as bass
from concourse import mybir
from concourse.alu_op_type import AluOpType as ALU

ACT = mybir.ActivationFunctionType
AX = mybir.AxisListType
F32 = mybir.dt.float32
I32 = mybir.dt.int32

D_MODEL = 1024
SEQ = 1024
DEC_BATCH, DEC_SEQ = 8, 8
PAST_LEN, PAGE = 2048, 128
N_PAGES = PAST_LEN // PAGE
HEAD = 64
H_DIFF, H_SB = 4, 8
HALF_W = H_DIFF * 2 * HEAD
MIX_W = 2 * HALF_W
N_BUCKETS, MAX_DISTANCE = 32, 128
N_GROUPS, PER_GROUP = 4, 4
N_EXPERTS = N_GROUPS * PER_GROUP
TOP_K = 2
D_EXPERT = 256
NORM_EPS, SUBLN_EPS = 1e-6, 1e-5
LAMBDA_INIT = 0.8 - 0.6 * math.exp(-0.3 * 0)

P = 128
KC = D_MODEL // P
N_SAMPLE = DEC_BATCH * DEC_SEQ
PT = SEQ // P
TILES = PT + 1
BANK = 512
PROJ_G = 3 * MIX_W // BANK
BLOCKS = MIX_W // P
NEAR = 2 * P
DIST = 3 * P
NEG = -1e30
MOE_TILES = (TOP_K * (SEQ + N_SAMPLE) + N_EXPERTS * (P - 1)) // P


class Count:

    def __init__(self, sem, per):
        self.sem, self.per = sem, per

    def after(self, turn, k):
        assert -self.per <= k < self.per
        return turn * self.per + (self.per + k + 1)



def constants(nc, ctx, t):
    t.ident = ctx.enter_context(nc.sbuf_tensor("ident", [P, P], F32))
    t.ones = ctx.enter_context(nc.sbuf_tensor("ones", [P, P], F32))
    t.neg_half = ctx.enter_context(nc.sbuf_tensor("neg_half", [P, 1], F32))
    t.waits_passed = ctx.enter_context(nc.semaphore("waits_passed"))
    t.const_ready = ctx.enter_context(nc.semaphore("const_ready"))
    with nc.Block() as block:

        @block.sync
        def _(sp):
            sp.dma_start(t.ident[:, :], t.eye).then_inc(t.const_ready, 16)

        @block.gpsimd
        def _(pool):
            pool.memset(t.neg_half[:, :], -0.5)
            pool.memset(t.ones[:, :], 1.0)


def own_wait(engine, t):
    engine.sem_inc(t.waits_passed, 1)


def clear(nc, sems):
    with nc.Block() as block:

        @block.gpsimd
        def _(pool):
            for one in sems:
                pool.sem_clear(one)


def project(nc, t):
    with ExitStack() as ctx:
        sems = []

        def sb(name, shape, dt=F32):
            return ctx.enter_context(nc.sbuf_tensor(name, shape, dt))

        def ps(name, shape):
            return ctx.enter_context(nc.psum_tensor(name, shape, F32))

        def sem(name):
            sems.append(ctx.enter_context(nc.semaphore(name)))
            return sems[-1]

        w_in = sb("w_in", [P, KC, PROJ_G, BANK])
        g_row = sb("g_mix_row", [P, D_MODEL])
        x = sb("x_tile", [P, 2, D_MODEL])
        h = sb("h_tile", [P, 2, D_MODEL])
        square = sb("square", [P, D_MODEL])
        hT = sb("h_transposed", [P, 2, KC, P])
        proj = sb("proj_rows", [P, 2, PROJ_G, BANK])
        qkT = sb("qk_transposed", [P, 2, 2, BLOCKS, P])
        ss = sb("sum_squares", [P, 2, 3])
        hT_ps = ps("hT_ps", [P, 2, BANK])
        pj_ps = ps("proj_ps", [P, 2, BANK])
        tr_ps = ps("qkT_ps", [P, 2, BANK])

        w_in_loaded = [sem(f"w_in_loaded{g}") for g in range(PROJ_G)]
        g_loaded = sem("g_mix_loaded")
        x_loaded = [sem(f"x_loaded{u}") for u in range(2)]
        rows_stored = [sem(f"rows_stored{u}") for u in range(2)]
        squares = Count(sem("squares_done"), 2)
        rstd = Count(sem("rstd_done"), 2)
        rstd_step = Count(sem("rstd_step"), 2)
        h_done = Count(sem("h_done"), 2)
        hT_done = Count(sem("hT_in_psum"), 4)
        hT_kept = Count(sem("hT_kept"), 4)
        pj_done = Count(sem("proj_in_psum"), 2 * PROJ_G)
        pj_kept = Count(sem("proj_kept"), 2 * PROJ_G)
        tr_done = Count(sem("qkT_in_psum"), 8)
        tr_kept = Count(sem("qkT_kept"), 8)
        setup = sem("p1_setup")
        QK = [0, 1, 3, 4]

        w_view = t.w_in.rearrange("(k p) (g n) -> p k g n", p=P, n=BANK)

        def row_tile(dram, tile):
            return dram[bass.ds(tile * P, P), :]

        with nc.Block() as block:

            @block.sync
            def _(sp):
                sp.dma_start(x[:, 0, :], row_tile(t.x, 0)).then_inc(x_loaded[0], 16)
                sp.dma_start(g_row[:, :], t.g_mix.partition_broadcast(P)).then_inc(g_loaded, 16)
                for g in range(PROJ_G):
                    sp.dma_start(w_in[:, :, g, :], w_view[:, :, g, :]).then_inc(w_in_loaded[g], 16)
                for u in range(2):
                    sp.sem_inc(rows_stored[u], 64)

                def store(it, u):
                    tile = it * 2 + u
                    sp.wait_ge(pj_kept.sem, pj_kept.after(it, u * PROJ_G + 2))
                    sp.dma_start(row_tile(t.new_kvd, tile), proj[:, u, 1:3, :]).then_inc(rows_stored[u], 16)
                    sp.wait_ge(pj_kept.sem, pj_kept.after(it, u * PROJ_G + 5))
                    sp.dma_start(row_tile(t.new_kvs, tile), proj[:, u, 4:6, :]).then_inc(rows_stored[u], 16)
                    sp.wait_ge(tr_kept.sem, tr_kept.after(it, u * 4 + 3))
                    own_wait(sp, t)
                    for n, dst in enumerate((t.qT, t.kT)):
                        sp.dma_start(dst[:, :, bass.ds(tile * P, P)], qkT[:, u, n, :, :])\
                          .then_inc(rows_stored[u], 16)

                with sp.Fori(0, PT // 2) as it:
                    for u in range(2):
                        sp.wait_ge(h_done.sem, h_done.after(it, u - 1))
                        own_wait(sp, t)
                        sp.dma_start(x[:, 1 - u, :], row_tile(t.x, it * 2 + u + 1))\
                          .then_inc(x_loaded[1 - u], 16)
                        store(it, u)
                store(PT // 2, 0)
                sp.wait_ge(rows_stored[0], 64 * (2 + PT // 2))
                sp.wait_ge(rows_stored[1], 64 * (1 + PT // 2))

            def loop(engine, tile):
                with engine.Fori(0, PT // 2) as it:
                    for u in range(2):
                        tile(it, u)
                tile(PT // 2, 0)

            @block.gpsimd
            def _(pool):
                pool.sem_inc(rstd.sem, rstd.per)
                pool.sem_inc(rstd_step.sem, rstd_step.per)

                def tile(it, u):
                    pool.wait_ge(squares.sem, squares.after(it, u))
                    own_wait(pool, t)
                    pool.tensor_scalar(ss[:, u, 1:2], ss[:, u, 0:1], 1.0 / D_MODEL, NORM_EPS, ALU.mult, ALU.add)\
                        .then_inc(rstd_step.sem, 1)
                    pool.wait_ge(rstd_step.sem, rstd_step.after(it, u))
                    pool.tensor_tensor(ss[:, u, 2:3], ss[:, u, 1:2], t.neg_half[:, :], ALU.pow)\
                        .then_inc(rstd.sem, 1)

                loop(pool, tile)

            @block.tensor
            def _(pe):
                pe.sem_inc(hT_done.sem, hT_done.per)
                pe.sem_inc(pj_done.sem, pj_done.per)
                pe.sem_inc(tr_done.sem, tr_done.per)

                def turn_h(it, u):
                    pe.wait_ge(h_done.sem, h_done.after(it, u))
                    for half in range(2):
                        pe.wait_ge(hT_kept.sem, hT_kept.after(it, 2 * u + half - 2))
                        for k in range(4):
                            last = pe.transpose(hT_ps[:, half, k * P:(k + 1) * P],
                                                h[:, u, (4 * half + k) * P:(4 * half + k + 1) * P], t.ident[:, :])
                        last.then_inc(hT_done.sem, 1)

                def turn_qk(it, u, n):
                    g = QK[n]
                    pe.wait_ge(pj_kept.sem, pj_kept.after(it, u * PROJ_G + g))
                    pe.wait_ge(tr_kept.sem, tr_kept.after(it, 4 * u + n - 2))
                    for b in range(4):
                        last = pe.transpose(tr_ps[:, n % 2, b * P:(b + 1) * P], proj[:, u, g, b * P:(b + 1) * P],
                                            t.ident[:, :])
                    last.then_inc(tr_done.sem, 1)

                def tile(it, u, final=False):
                    pe.wait_ge(hT_kept.sem, hT_kept.after(it, 2 * u + 1))
                    for g in range(PROJ_G):
                        pe.wait_ge(w_in_loaded[g], 16)
                        pe.wait_ge(pj_kept.sem, pj_kept.after(it, u * PROJ_G + g - 2))
                        for k in range(KC):
                            last = pe.matmul(pj_ps[:, g % 2, :], hT[:, u, k, :], w_in[:, k, g, :],
                                             start=(k == 0), stop=(k == KC - 1))
                        last.then_inc(pj_done.sem, 1)
                        if g == 3 and not final:
                            turn_h(it + u, 1 - u)
                        if g >= 1 and g - 1 in QK:
                            turn_qk(it, u, QK.index(g - 1))

                pe.wait_ge(t.const_ready, 16)
                turn_h(0, 0)
                with pe.Fori(0, PT // 2) as it:
                    for u in range(2):
                        tile(it, u)
                tile(PT // 2, 0, final=True)

            @block.vector
            def _(dve):
                dve.sem_inc(h_done.sem, h_done.per)
                dve.sem_inc(hT_kept.sem, hT_kept.per)
                dve.sem_inc(tr_kept.sem, tr_kept.per)
                dve.wait_ge(g_loaded, 16)

                def norm(it, u):
                    dve.wait_ge(rstd.sem, rstd.after(it, u))
                    dve.wait_ge(hT_done.sem, hT_done.after(it, 2 * u - 3))
                    dve.scalar_tensor_tensor(h[:, u, :], x[:, u, :], ss[:, u, 2:3], g_row[:, :], ALU.mult, ALU.mult)\
                       .then_inc(h_done.sem, 1)

                def keep_h(it, u):
                    for half in range(2):
                        dve.wait_ge(hT_done.sem, hT_done.after(it, 2 * u + half))
                        dve.wait_ge(pj_done.sem, pj_done.after(it, (u - 1) * PROJ_G - 1))
                        dve.tensor_copy(hT[:, u, 4 * half:4 * half + 4, :], hT_ps[:, half, :])\
                           .then_inc(hT_kept.sem, 1)

                def keep_qk(it, u, n):
                    dve.wait_ge(tr_done.sem, tr_done.after(it, 4 * u + n))
                    dve.wait_ge(rows_stored[u], it * 64 + 64)
                    dve.tensor_copy(qkT[:, u, n % 2, n // 2 * 4:n // 2 * 4 + 4, :], tr_ps[:, n % 2, :])\
                       .then_inc(tr_kept.sem, 1)

                def tile(it, u, final=False):
                    keep_qk(it, u, 0)
                    keep_qk(it, u, 1)
                    if not final:
                        norm(it + u, 1 - u)
                        keep_h(it + u, 1 - u)
                    keep_qk(it, u, 2)
                    keep_qk(it, u, 3)

                norm(0, 0)
                keep_h(0, 0)
                with dve.Fori(0, PT // 2) as it:
                    for u in range(2):
                        tile(it, u)
                tile(PT // 2, 0, final=True)

            @block.scalar
            def _(act):
                act.sem_inc(squares.sem, squares.per)
                act.sem_inc(pj_kept.sem, pj_kept.per)

                def square_sum(it, u):
                    act.wait_ge(x_loaded[u], it * 16 + 16)
                    act.wait_ge(squares.sem, squares.after(it, u - 1))
                    act.activation(square[:, :], x[:, u, :], ACT.Square, accum_out=ss[:, u, 0:1])\
                       .then_inc(squares.sem, 1)

                def tile(it, u, final=False):
                    if not final:
                        square_sum(it + u, 1 - u)
                    for g in range(PROJ_G):
                        act.wait_ge(pj_done.sem, pj_done.after(it, u * PROJ_G + g))
                        if g == 0:
                            act.wait_ge(rows_stored[u], it * 64 + 64)
                        scale = HEAD ** -0.5 if g in (0, 3) else 1.0
                        act.activation(proj[:, u, g, :], pj_ps[:, g % 2, :], ACT.Copy, scale=scale)\
                           .then_inc(pj_kept.sem, 1)

                square_sum(0, 0)
                with act.Fori(0, PT // 2) as it:
                    for u in range(2):
                        tile(it, u)
                tile(PT // 2, 0, final=True)

        clear(nc, sems)


def tables(nc, ctx, t):
    def keep(name, shape, dt=F32):
        return ctx.enter_context(nc.sbuf_tensor(name, shape, dt))

    t.q_heads = keep("sample_q_by_head", [P, DEC_BATCH, BLOCKS, 2, DEC_SEQ])
    t.near_dec = keep("near_bias_sample", [P, PAGE + DEC_SEQ])
    t.neg_lambda = keep("neg_lambda", [P, 1])
    t.row_factor = keep("row_factor", [P, 1])
    t.sub_g = keep("sub_g", [P, 1])
    t.pages = keep("page_ids", [1, DEC_BATCH * N_PAGES], I32)
    with ExitStack() as own:
        sems = []

        def sb(name, shape, dt=F32):
            return own.enter_context(nc.sbuf_tensor(name, shape, dt))

        def sem(name):
            sems.append(own.enter_context(nc.semaphore(name)))
            return sems[-1]

        rb = sb("rel_bias_rows", [N_BUCKETS + 2, H_DIFF + 1])
        buckets = sb("buckets", [N_BUCKETS + 2, DIST])
        rb_wide = sb("rel_bias_wide", [N_BUCKETS + 2, H_DIFF + 1, P])
        by_distance = sb("bias_by_distance", [P, H_DIFF + 1, DIST])
        lam_in = sb("lambda_in", [P, 4, HEAD])
        lam_mul = sb("lambda_products", [P, 2, HEAD])
        lam_sum = sb("lambda_sums", [P, 2])
        lam_exp = sb("lambda_exps", [P, 2])
        halves = sb("map_of_halves", [P, 2])
        g_in = sb("subln_in", [P, 1])
        q_in = sb("sample_qT", [P, BLOCKS, N_SAMPLE])
        bias_ps = own.enter_context(nc.psum_tensor("bias_ps", [P, H_DIFF + 1, BANK], F32))
        zeroed, rb_loaded, lam_loaded, q_loaded = sem("zeroed"), sem("rb_loaded"), sem("lam_loaded"), sem("q_loaded")
        bias_done, bias_kept, bias_stored = sem("bias_done"), sem("bias_kept"), sem("bias_stored")
        near_loaded, pages_loaded = sem("near_loaded"), sem("pages_loaded")
        widened = sem("rel_bias_widened")
        step, exps = sem("lambda_step"), sem("lambda_exps_done")

        with nc.Block() as block:

            @block.sync
            def _(sp):
                sp.dma_start(buckets[:, :], t.bucket_table).then_inc(rb_loaded, 16)
                sp.dma_start(rb[N_BUCKETS:N_BUCKETS + 2, :], t.mask_rows).then_inc(rb_loaded, 16)
                sp.wait_ge(zeroed, 1)
                sp.dma_start(rb[0:N_BUCKETS, 0:H_DIFF], t.rel_bias).then_inc(rb_loaded, 16)
                for n, v in enumerate((t.lambda_q1, t.lambda_k1, t.lambda_q2, t.lambda_k2)):
                    sp.dma_start(lam_in[:, n, :], v.partition_broadcast(P)).then_inc(lam_loaded, 16)
                sp.dma_start(g_in[:, :], t.subln_g.rearrange("(p a) -> p a", a=1)).then_inc(lam_loaded, 16)
                sp.dma_start(halves[:, :], t.half_map).then_inc(lam_loaded, 16)
                sp.dma_start(q_in[:, :, :], t.qT[:, :, SEQ:SEQ + N_SAMPLE]).then_inc(q_loaded, 16)
                sp.dma_start(t.pages[:, :], t.page_table.rearrange("(a s) n -> a (s n)", a=1))\
                  .then_inc(pages_loaded, 16)
                sp.wait_ge(bias_kept, 1)
                sp.dma_start(t.bias_dram.rearrange("h p n -> p h n"), by_distance[:, :, :]).then_inc(bias_stored, 16)
                sp.wait_ge(bias_stored, 16)
                for b in range(BLOCKS):
                    for u in range(2):
                        row = 2 * DEC_SEQ * b + DEC_SEQ * u
                        sp.dma_start(t.near_dec[row:row + DEC_SEQ, :],
                                     distances(t, min(b, H_DIFF), DEC_SEQ, PAGE + DEC_SEQ)).then_inc(near_loaded, 16)
                sp.wait_ge(near_loaded, 16 * 2 * BLOCKS)
                for head in range(H_DIFF):
                    sp.dma_start(t.near_dram[head], distances(t, head, P, NEAR)).then_inc(bias_stored, 16)
                sp.wait_ge(bias_stored, 16 * (1 + H_DIFF))
                sp.wait_ge(pages_loaded, 16)

            @block.tensor
            def _(pe):
                pe.wait_ge(rb_loaded, 48)
                pe.wait_ge(widened, 1)
                for head in range(H_DIFF + 1):
                    last = pe.matmul(bias_ps[:, head, 0:DIST], rb_wide[:, head, :], buckets[:, :], start=True, stop=True)
                last.then_inc(bias_done, 1)

            @block.vector
            def _(dve):
                dve.memset(rb[0:N_BUCKETS, :], 0.0).then_inc(zeroed, 1)
                dve.memset(t.q_heads[:, :, :, :, :], 0.0).then_inc(zeroed, 1)
                dve.wait_ge(rb_loaded, 48)
                dve.tensor_copy(rb_wide[:, :, :], rb[:, :].unsqueeze(2).broadcast_to([N_BUCKETS + 2, H_DIFF + 1, P]))\
                   .then_inc(widened, 1)
                dve.wait_ge(bias_done, 1)
                dve.tensor_copy(by_distance[:, :, :], bias_ps[:, :, 0:DIST]).then_inc(bias_kept, 1)
                dve.wait_ge(q_loaded, 16)
                dve.wait_ge(zeroed, 2)
                for u in range(2):
                    rows = slice(HEAD * u, HEAD * u + HEAD)
                    for s in range(DEC_BATCH):
                        dve.tensor_copy(t.q_heads[rows, s, :, u, :], q_in[rows, :, DEC_SEQ * s:DEC_SEQ * (s + 1)])
                dve.wait_ge(lam_loaded, 96)
                dve.tensor_tensor(lam_mul[:, 0, :], lam_in[:, 0, :], lam_in[:, 1, :], ALU.mult).then_inc(step, 1)
                dve.tensor_tensor(lam_mul[:, 1, :], lam_in[:, 2, :], lam_in[:, 3, :], ALU.mult).then_inc(step, 1)
                dve.wait_ge(step, 2)
                dve.tensor_reduce(lam_sum[:, :], lam_mul[:, :, :], axis=AX.X, op=ALU.add).then_inc(step, 1)
                dve.wait_ge(exps, 1)
                dve.tensor_tensor(t.neg_lambda[:, :], lam_exp[:, 1:2], lam_exp[:, 0:1], ALU.subtract)\
                   .then_inc(step, 1)
                dve.wait_ge(step, 4)
                dve.tensor_scalar_add(t.neg_lambda[:, :], t.neg_lambda[:, :], -LAMBDA_INIT).then_inc(step, 1)
                dve.wait_ge(step, 5)
                dve.scalar_tensor_tensor(t.row_factor[:, :], halves[:, 1:2], t.neg_lambda[:, 0:1], halves[:, 0:1],
                                         ALU.mult, ALU.add)
                dve.tensor_scalar_mul(t.sub_g[:, :], g_in[:, :], 1.0 - LAMBDA_INIT)

            @block.scalar
            def _(act):
                act.wait_ge(step, 3)
                act.activation(lam_exp[:, :], lam_sum[:, :], ACT.Exp).then_inc(exps, 1)

        clear(nc, sems)


def distances(t, head, rows, cols):
    return bass.AP(t.bias_dram.tensor, head * P * DIST + P - 1, [[DIST - 1, rows], [1, cols]])


DIFF, STICK = 0, 1
TURNS = 4
K_SLOTS = 4
N_WEIGH = 7
SPANS = {DIFF: ((0.0, 0.4), (0.4, 0.55), (0.55, 1.0)), STICK: ((0.0, 0.4), (0.4, 0.55), (0.55, 1.0))}
D_PAGES = N_PAGES + 1
KEYS = PAST_LEN + DEC_SEQ
V_GROUPS = (D_PAGES + 3) // 4
NEW = N_PAGES
S_GROUPS = N_PAGES // 2
S_KEYS = 2 * PAGE + DEC_SEQ
D0 = H_DIFF * 2 * DEC_SEQ


def page_keys(p):
    return PAGE if p < N_PAGES else DEC_SEQ


def group_pages(g):
    return range(4 * g, min(4 * g + 4, D_PAGES))


def score_chunks(kind):
    near = 2 if kind == DIFF else 1
    out = []
    for i in range(PT):
        end, near0 = (i + 1) * P, max(0, (i + 1 - near)) * P
        for u in range(2):
            for k0 in range(0, end, BANK):
                k1 = min(k0 + BANK, end)
                out.append((i, u, k0, k1, min(max(near0, k0), k1)))
    return out


def turned_groups(kind, i):
    blocks = [(u, kb) for u in range(1 if kind == DIFF else 2) for kb in range(i + 1)]
    return [blocks[n:n + 4] for n in range(0, len(blocks), 4)]


def score_group_pages(g):
    return range(2 * g, 2 * g + 2) if g + 1 < S_GROUPS else range(2 * g, D_PAGES)


def attention_plan(kind):
    n_soft = 3 if kind == DIFF else 6
    prompt = [(("score", 0), 2)] + [(("soft", 0, n), 0) for n in range(n_soft)]
    for i in range(PT):
        soft = [(("soft", i + 1, n), 1) for n in range(n_soft)] if i + 1 < PT else []
        if i + 1 < PT:
            prompt.append((("score", i + 1), 2 * (i + 2)))
        n_out = len(turned_groups(kind, i)) + 1
        outs = [(("out", i, n), 4) for n in range(n_out - 1)]
        if i:
            outs.append((("turn_out", i - 1), 1))
        outs.append((("out", i, n_out - 1), i + 1))
        prompt += soft[:1] + outs + soft[1:]
    prompt.append((("turn_out", PT - 1), 1))
    pages = []
    for p in range(D_PAGES):
        pages.append((("page", p), 4))
        if p >= 2 and p % 2 == 0 and p < N_PAGES:
            pages.append((("page_scores", p // 2 - 1), 16))
    pages.append((("page_scores", S_GROUPS - 1), 16))
    weigh = [(("weigh", n), 1) for n in range(N_WEIGH)]
    use = [(("turn", 0), 2)]
    for g in range(1, V_GROUPS):
        use += [(("turn", g), 2), (("apply", 0, g - 1), 16)]
    use += [(("apply", 0, V_GROUPS - 1), 4), (("rows", 0), 0)]
    use += [(("apply", 1, g), 16) for g in range(V_GROUPS)] + [(("rows", 1), 0), (("heads", 0), 4)]
    total = sum(c for _, c in prompt)
    spans = ((pages, *SPANS[kind][0]), (weigh, *SPANS[kind][1]), (use, *SPANS[kind][2]))
    timed = []
    for steps, a, b in spans:
        all_, done = sum(c for _, c in steps), 0
        for step, c in steps:
            timed.append((a + (b - a) * done / all_, step))
            done += c
    out, done, taken = [], 0, 0
    for step, c in prompt:
        while taken < len(timed) and timed[taken][0] <= done / total:
            out.append(timed[taken][1])
            taken += 1
        out.append(step)
        done += c
    return out + [step for _, step in timed[taken:]]


def attention(nc, t, kind):
    with ExitStack() as ctx:
        sems = []

        def sb(name, shape, dt=F32):
            return ctx.enter_context(nc.sbuf_tensor(f"{name}_{kind}", shape, dt))

        def ps(name, shape):
            return ctx.enter_context(nc.psum_tensor(f"{name}_{kind}", shape, F32))

        def sem(name):
            sems.append(ctx.enter_context(nc.semaphore(f"{name}_{kind}")))
            return sems[-1]

        def count(name, per):
            return Count(sem(name), per)

        qT = sb("head_qT_halves", [P, 2, SEQ])
        kT = sb("head_kT", [P, SEQ])
        v = sb("head_v", [P, PT, P])
        near = sb("near_bias", [P, NEAR])
        S = sb("scores", [P, 2, 2, SEQ])
        aux = sb("aux", [P, 2, SEQ])
        wT = sb("weights_T", [P, 16, P])
        stat = sb("stats", [P, 4, 8])
        o_rows = sb("o_rows", [P, 2, P])
        o_sq = sb("o_squares", [P, P])
        o_norm = sb("o_normed", [P, P])
        oT = sb("head_oT", [P, SEQ])
        sc_ps = ps("scores_ps", [P, 2, BANK])
        wT_ps = ps("weights_T_ps", [P, 4, P])
        o_ps = ps("o_ps", [P, BANK])
        k_page = sb("k_pages", [P, K_SLOTS, BLOCKS, P])
        v_page = sb("v_pages", [P, D_PAGES, BLOCKS, P])
        kT_page = sb("k_pages_T", [P, 2, BLOCKS, S_KEYS])
        q_block = sb("q_by_block", [P, BLOCKS * (P + 16)])
        sS = sb("sample_scores", [P, KEYS])
        sW = sb("sample_weights", [P, KEYS])
        o_rows_s = sb("sample_o_rows", [P, BANK])
        sT = sb("sample_weights_T", [P, D_PAGES, P])
        sstat = sb("sample_stats", [P, 4])
        kT_ps = ps("k_page_T_ps", [P, 2, 4, P])
        s_ps = ps("page_scores_ps", [P, BANK])
        sO_ps = ps("sample_o_ps", [P, BANK])

        chunks = score_chunks(kind)
        n_chunks = len(chunks)
        assert n_chunks % 2 == 0
        far_upto = np.cumsum([c[4] > c[2] for c in chunks]).tolist()
        near_upto = np.cumsum([c[3] > c[4] for c in chunks]).tolist()
        n_groups = [len(turned_groups(kind, i)) for i in range(PT)]
        groups_upto = np.cumsum(n_groups).tolist()
        plan = attention_plan(kind)

        qk_loaded, v_loaded, near_loaded = sem("qk_loaded"), sem("v_loaded"), sem("near_loaded")
        sc_done = count("scores_in_psum", n_chunks)
        sc_far = count("far_scores_kept", far_upto[-1])
        sc_near = count("near_scores_kept", near_upto[-1])
        row_max = count("row_max", PT)
        exps = count("exps_done", 2 * PT)
        inv_sum = count("inverse_sums", 2 * PT)
        mixed = count("softmaxes_mixed", PT)
        s_abs = count("abs_done", PT)
        s_expm = count("exp_minus_abs", PT)
        s_ln = count("ln_done", PT)
        s_soft = count("softplus_done", PT)
        s_scan = count("suffix_sums_done", 2 * PT)
        s_sub = count("log_weights_done", PT)
        s_exp = count("stick_weights_done", PT)
        w_turned = count("weights_T_in_psum", groups_upto[-1])
        wT_kept = count("weights_T_kept", groups_upto[-1])
        o_done = count("o_in_psum", PT)
        o_kept = count("o_kept", PT)
        o_squared = count("o_squared", PT)
        sub_step = count("sub_norm_step", PT)
        sub_rstd = count("sub_norm_rstd", PT)
        o_normed = count("o_normed_done", PT)
        oT_done = count("oT_in_psum", PT)
        oT_kept = count("oT_kept", PT)
        oT_stored = sem("oT_stored")
        k_loaded = [sem(f"k_page_loaded{n}") for n in range(K_SLOTS)]
        vp_loaded = [sem(f"v_pages_loaded{g}") for g in range(V_GROUPS)]
        kT_done = count("kT_in_psum", 2 * D_PAGES + V_GROUPS)
        kT_kept = [count("kT_bank0_kept", D_PAGES + (V_GROUPS + 1) // 2), count("kT_bank1_kept", D_PAGES + V_GROUPS // 2)]
        zeroed = sem("zeros_written")
        q_spread = count("q_by_block_done", 1)
        ps_done = count("page_scores_in_psum", S_GROUPS)
        sfar = count("sample_far_kept", S_GROUPS)
        snear = count("sample_near_kept", 1)
        smax = count("sample_max", 1)
        sexp = count("sample_exp", 1)
        sabs = count("sample_abs", 1)
        sexpm = count("sample_exp_minus_abs", 1)
        sln = count("sample_ln", 1)
        ssoft = count("sample_softplus", 1)
        sscan = count("sample_suffix_sums", 1)
        ssub = count("sample_log_weights", 1)
        sstick = count("sample_stick_weights", 1)
        sinv = count("sample_inverse_sums", 2)
        applied = [count("diff_groups_applied", V_GROUPS), count("stick_groups_applied", V_GROUPS)]
        rows_kept = [count("sample_diff_rows_kept", 1), count("sample_stick_rows_kept", 1)]
        heads_done = count("sample_heads_in_psum", 1)
        so_kept = count("sample_o_kept", 1)

        def page_slot(p):
            s = p % K_SLOTS
            return s, p // K_SLOTS, len(range(s, D_PAGES, K_SLOTS))

        kv = t.new_kvd if kind == DIFF else t.new_kvs

        with nc.Block() as block:

            @block.sync
            def _(sp):
                def head_block(b):
                    return t.qT[:, bass.ds(b + TURNS * kind, 1), 0:SEQ], t.kT[:, bass.ds(b + TURNS * kind, 1), 0:SEQ]

                def load_page(it, p, dst, half, signal, free):
                    if p < N_PAGES:
                        page = sp.value_load(t.pages[0:1, bass.ds((it + TURNS * kind) * N_PAGES + p, 1)],
                                             min_val=0, max_val=t.n_pool - 1)
                        src = [c[bass.ds(page, 1), :, half * HALF_W:(half + 1) * HALF_W]
                               .rearrange("a k n -> (a k) n") for c in (t.cache_d, t.cache_s)]
                    else:
                        first = SEQ + (it + TURNS * kind) * DEC_SEQ
                        src = [c[bass.ds(first, DEC_SEQ), half * HALF_W:(half + 1) * HALF_W]
                               for c in (t.new_kvd, t.new_kvs)]
                    n = page_keys(p)
                    sp.wait_ge(*free)
                    for j in range(2):
                        sp.dma_start(dst[0:n, 4 * j:4 * j + 4, :], src[j]).then_inc(signal, 16)

                def load_k(it, p):
                    s, _, _ = page_slot(p)
                    prior = p - K_SLOTS if p >= K_SLOTS else max(range(s, D_PAGES, K_SLOTS)) - D_PAGES
                    item = 2 * prior + 1 if prior >= 0 else 2 * prior + 1 - V_GROUPS
                    load_page(it, p, k_page[:, s, :, :], 0, k_loaded[s], (kT_done.sem, kT_done.after(it, item)))

                def load_v(it, p):
                    load_page(it, p, v_page[:, p, :, :], 1, vp_loaded[p // 4],
                              (applied[1].sem, applied[1].after(it, p // 4 - V_GROUPS)))

                if kind == STICK:
                    sp.dma_start(near[:, :], distances(t, H_DIFF, P, NEAR)).then_inc(near_loaded, 16)
                with sp.Fori(0, TURNS) as it:
                    for p in range(K_SLOTS):
                        load_k(it, p)
                    if kind == DIFF:
                        sp.wait_ge(sc_near.sem, sc_near.after(it, -1))
                        sp.dma_start(near[:, :], t.near_dram[bass.ds(it, 1), :, :].rearrange("a p n -> (a p) n"))\
                          .then_inc(near_loaded, 16)
                    sp.wait_ge(sc_done.sem, sc_done.after(it, -1))
                    q_src, k_src = [a.rearrange("p a n -> p (a n)") for a in head_block(it)]
                    for u in range(2):
                        rows = slice(HEAD * u, HEAD * u + HEAD)
                        sp.dma_start(qT[rows, u, :], q_src[rows, :]).then_inc(qk_loaded, 16)
                    sp.dma_start(kT[:, :], k_src).then_inc(qk_loaded, 16)
                    sp.wait_ge(o_done.sem, o_done.after(it, -1))
                    sp.dma_start(v[:, :, :], kv[0:SEQ, bass.ds(it * P + HALF_W, P)].rearrange("(t p) n -> p t n", p=P))\
                      .then_inc(v_loaded, 16)
                    for p in range(N_PAGES):
                        load_v(it, p)
                        if p + K_SLOTS < D_PAGES:
                            load_k(it, p + K_SLOTS)
                    load_v(it, NEW)

            @block.gpsimd
            def _(pool):
                pool.sem_inc(sub_step.sem, sub_step.per)
                pool.sem_inc(sub_rstd.sem, sub_rstd.per)

                def rstd(it, i):
                    pool.wait_ge(o_squared.sem, o_squared.after(it, i))
                    own_wait(pool, t)
                    pool.tensor_scalar(stat[:, i % 4, 6:7], stat[:, i % 4, 5:6], 1.0 / P, SUBLN_EPS,
                                       ALU.mult, ALU.add).then_inc(sub_step.sem, 1)
                    pool.wait_ge(sub_step.sem, sub_step.after(it, i))
                    pool.tensor_tensor(stat[:, i % 4, 7:8], stat[:, i % 4, 6:7], t.neg_half[:, :], ALU.pow)\
                        .then_inc(sub_rstd.sem, 1)

                if kind == DIFF:
                    with pool.Fori(0, TURNS) as it:
                        for i in range(PT):
                            rstd(it, i)

            @block.tensor
            def _(pe):
                for c in (sc_done, w_turned, o_done, oT_done, kT_done, ps_done, *applied, heads_done):
                    pe.sem_inc(c.sem, c.per)

                def score(it, i):
                    if i == 0:
                        pe.wait_ge(qk_loaded, it * 48 + 48)
                    for g, (ci, u, k0, k1, kn) in enumerate(chunks):
                        if ci != i:
                            continue
                        if g >= 2:
                            pe.wait_ge(sc_far.sem, sc_far.after(it, far_upto[g - 2] - 1))
                            pe.wait_ge(sc_near.sem, sc_near.after(it, near_upto[g - 2] - 1))
                        else:
                            pe.wait_ge(sc_far.sem, sc_far.after(it, -1))
                            pe.wait_ge(sc_near.sem, sc_near.after(it, -1))
                        pe.matmul(sc_ps[:, g % 2, 0:k1 - k0], qT[:, u, i * P:(i + 1) * P], kT[:, k0:k1],
                                  start=True, stop=True).then_inc(sc_done.sem, 1)

                def out(it, i, n):
                    groups = turned_groups(kind, i)
                    first = groups_upto[i] - n_groups[i]
                    if n < len(groups):
                        if n == 0:
                            if kind == DIFF:
                                pe.wait_ge(mixed.sem, mixed.after(it, i))
                            else:
                                pe.wait_ge(s_exp.sem, s_exp.after(it, i))
                        pe.wait_ge(wT_kept.sem, wT_kept.after(it, first + n - 1))
                        for m, (u, kb) in enumerate(groups[n]):
                            src = aux[:, 0, kb * P:(kb + 1) * P] if kind == DIFF else S[:, i % 2, u, kb * P:(kb + 1) * P]
                            last = pe.transpose(wT_ps[:, m, :], src, t.ident[:, :])
                        last.then_inc(w_turned.sem, 1)
                        return
                    pe.wait_ge(wT_kept.sem, wT_kept.after(it, groups_upto[i] - 1))
                    pe.wait_ge(oT_kept.sem, oT_kept.after(it, i - 1))
                    if i == 0:
                        pe.wait_ge(v_loaded, it * 16 + 16)
                    for m, (u, kb) in enumerate([x for g in groups for x in g]):
                        cols = slice(0, P) if kind == DIFF else slice(HEAD * u, HEAD * u + HEAD)
                        last = pe.matmul(o_ps[:, cols], wT[:, m, :], v[:, kb, cols], start=(kb == 0), stop=(kb == i))
                    last.then_inc(o_done.sem, 1)

                def turn_out(it, i):
                    ready = o_normed if kind == DIFF else o_kept
                    pe.wait_ge(ready.sem, ready.after(it, i))
                    pe.wait_ge(oT_kept.sem, oT_kept.after(it, i - 1))
                    pe.transpose(o_ps[:, P:2 * P], o_norm[:, :], t.ident[:, :]).then_inc(oT_done.sem, 1)

                def page(it, p):
                    s, before, loads = page_slot(p)
                    n = page_keys(p)
                    pe.wait_ge(k_loaded[s], it * (32 * loads) + 32 * (before + 1))
                    for half in range(2):
                        pe.wait_ge(kT_kept[half].sem, kT_kept[half].after(it, p - 1))
                        own_wait(pe, t)
                        for b in range(4):
                            last = pe.transpose(kT_ps[:, half, b, 0:n], k_page[0:n, s, 4 * half + b, :],
                                                t.ident[0:n, 0:n])
                        last.then_inc(kT_done.sem, 1)

                def page_scores(it, g):
                    if g == 0:
                        pe.wait_ge(q_spread.sem, q_spread.after(it, 0))
                    for half in range(2):
                        pe.wait_ge(kT_kept[half].sem, kT_kept[half].after(it, score_group_pages(g)[-1]))
                    pe.wait_ge(sfar.sem, sfar.after(it, g - 1))
                    if g == 0:
                        pe.wait_ge(snear.sem, snear.after(it, -1))
                    n = sum(page_keys(p) for p in score_group_pages(g))
                    for b in range(BLOCKS):
                        last = pe.matmul(s_ps[:, 0:n], q_block[:, b * P:(b + 1) * P], kT_page[:, g % 2, b, 0:n],
                                         start=(b == 0), stop=(b == BLOCKS - 1))
                    last.then_inc(ps_done.sem, 1)

                def turn(it, g):
                    if g == 0:
                        pe.wait_ge(sstick.sem, sstick.after(it, 0))
                        pe.wait_ge(sexp.sem, sexp.after(it, 0))
                    pe.wait_ge(kT_kept[g % 2].sem, kT_kept[g % 2].after(it, D_PAGES - 1 + g // 2))
                    for m, p in enumerate(group_pages(g)):
                        n = page_keys(p)
                        last = pe.transpose(kT_ps[0:n, g % 2, m, :], sW[:, p * PAGE:p * PAGE + n], t.ident[:, :])
                    last.then_inc(kT_done.sem, 1)

                def apply(it, kind_half, g):
                    if kind_half == 0:
                        pe.wait_ge(kT_kept[g % 2].sem, kT_kept[g % 2].after(it, D_PAGES + g // 2))
                        pe.wait_ge(vp_loaded[g], (it + 1) * (32 * len(group_pages(g))))
                        if g == 0:
                            pe.wait_ge(so_kept.sem, so_kept.after(it, -1))
                    elif g == 0:
                        pe.wait_ge(rows_kept[0].sem, rows_kept[0].after(it, 0))
                    own_wait(pe, t)
                    for p in group_pages(g):
                        n = page_keys(p)
                        last = pe.matmul(sO_ps[:, :], sT[0:n, p, :], v_page[0:n, p, 4 * kind_half:4 * kind_half + 4, :],
                                         start=(p == 0), stop=(p == NEW))
                    last.then_inc(applied[kind_half].sem, 1)

                def heads(it, _):
                    pe.wait_ge(rows_kept[1].sem, rows_kept[1].after(it, 0))
                    for b in range(4):
                        cols = slice(16 * b, 16 * b + 16)
                        last = pe.matmul(sO_ps[:, 0:P].rearrange("p (u c) -> p u c", u=2)[:, :, cols],
                                         o_rows_s[:, b * P:(b + 1) * P],
                                         t.ident[:, :].rearrange("p (u c) -> p u c", u=2)[:, :, cols],
                                         start=True, stop=True)
                    last.then_inc(heads_done.sem, 1)

                steps = dict(score=score, out=out, turn_out=turn_out, page=page, page_scores=page_scores,
                             turn=turn, apply=apply, heads=heads)
                pe.wait_ge(zeroed, 3)
                with pe.Fori(0, TURNS) as it:
                    for name, *args in plan:
                        if name in steps:
                            steps[name](it, *args)

            @block.vector
            def _(dve):
                for c in (sc_near, row_max, inv_sum, mixed, s_soft, s_scan, s_sub, o_normed, oT_kept, kT_kept[1],
                          q_spread, snear, smax, ssoft, sscan, ssub, sinv, *rows_kept, so_kept):
                    dve.sem_inc(c.sem, c.per)
                if kind == STICK:
                    for c in (wT_kept,):
                        dve.sem_inc(c.sem, c.per)

                def score(it, i):
                    if i == 0:
                        dve.wait_ge(near_loaded, it * 16 + 16 if kind == DIFF else 16)
                    for g, (ci, u, k0, k1, kn) in enumerate(chunks):
                        if ci != i or kn >= k1:
                            continue
                        dve.wait_ge(sc_done.sem, sc_done.after(it, g))
                        if kn > k0:
                            dve.wait_ge(sc_far.sem, sc_far.after(it, far_upto[g] - 1))
                        dve.wait_ge(w_turned.sem, w_turned.after(it, groups_upto[i - 2] - 1 if i >= 2 else
                                                                 groups_upto[PT - 2 + i] - 1 - groups_upto[-1]))
                        col = kn - (i - 1) * P
                        dve.tensor_tensor(S[:, i % 2, u, kn:k1], sc_ps[:, g % 2, kn - k0:k1 - k0],
                                          near[:, col:col + k1 - kn], ALU.add).then_inc(sc_near.sem, 1)

                def soft_diff(it, i, n):
                    end = (i + 1) * P
                    last_chunk = max(g for g, c in enumerate(chunks) if c[0] == i)
                    x = stat[:, i % 4, :]
                    if n == 0:
                        dve.wait_ge(sc_far.sem, sc_far.after(it, far_upto[last_chunk] - 1))
                        dve.wait_ge(sc_near.sem, sc_near.after(it, near_upto[last_chunk] - 1))
                        dve.wait_ge(o_normed.sem, o_normed.after(it, i - 4))
                        dve.tensor_reduce(x[:, 0:2], S[:, i % 2, :, 0:end], axis=AX.X, op=ALU.max, negate=True)\
                           .then_inc(row_max.sem, 1)
                    elif n == 2:
                        dve.wait_ge(exps.sem, exps.after(it, 2 * i + 1))
                        dve.reciprocal(x[:, 4:6], x[:, 2:4]).then_inc(inv_sum.sem, 1)
                        dve.wait_ge(inv_sum.sem, inv_sum.after(it, 2 * i))
                        dve.scalar_tensor_tensor(x[:, 1:2], x[:, 5:6], t.neg_lambda[:, 0:1], x[:, 2:3],
                                                 ALU.mult, ALU.mult).then_inc(inv_sum.sem, 1)
                        dve.wait_ge(inv_sum.sem, inv_sum.after(it, 2 * i + 1))
                        dve.wait_ge(w_turned.sem, w_turned.after(it, groups_upto[i - 1] - 1 if i else -1))
                        dve.scalar_tensor_tensor(aux[:, 0, 0:end], S[:, i % 2, 1, 0:end], x[:, 1:2],
                                                 S[:, i % 2, 0, 0:end], ALU.mult, ALU.add).then_inc(mixed.sem, 1)

                def soft_stick(it, i, n):
                    end = (i + 1) * P
                    if n == 3:
                        dve.wait_ge(s_ln.sem, s_ln.after(it, i))
                        dve.scalar_tensor_tensor(aux[:, :, 0:end], S[:, i % 2, :, 0:end], 0.0, aux[:, :, 0:end],
                                                 ALU.max, ALU.add).then_inc(s_soft.sem, 1)
                    elif n == 4:
                        dve.wait_ge(s_soft.sem, s_soft.after(it, i))
                        for u in range(2):
                            dve.tensor_tensor_scan(aux[:, u, 0:end][:, ::-1], aux[:, u, 0:end][:, ::-1],
                                                   aux[:, u, 0:end][:, ::-1], 0.0, ALU.add, ALU.bypass)\
                               .then_inc(s_scan.sem, 1)
                        dve.wait_ge(s_scan.sem, s_scan.after(it, 2 * i + 1))
                        dve.tensor_tensor(S[:, i % 2, :, 0:end], S[:, i % 2, :, 0:end], aux[:, :, 0:end],
                                          ALU.subtract).then_inc(s_sub.sem, 1)

                def out(it, i, n):
                    groups = turned_groups(kind, i)
                    first = groups_upto[i] - n_groups[i]
                    if kind == STICK and n < len(groups):
                        dve.wait_ge(w_turned.sem, w_turned.after(it, first + n))
                        dve.wait_ge(o_done.sem, o_done.after(it, i - 1))
                        m = len(groups[n])
                        dve.tensor_copy(wT[:, 4 * n:4 * n + m, :], wT_ps[:, 0:m, :]).then_inc(wT_kept.sem, 1)

                def turn_out(it, i):
                    if kind == DIFF:
                        dve.wait_ge(sub_rstd.sem, sub_rstd.after(it, i))
                        dve.wait_ge(oT_done.sem, oT_done.after(it, i - 1))
                        dve.tensor_scalar_mul(o_norm[:, :], o_rows[:, i % 2, :], stat[:, i % 4, 7:8])\
                           .then_inc(o_normed.sem, 1)
                    dve.wait_ge(oT_done.sem, oT_done.after(it, i))
                    if i == 0:
                        dve.wait_ge(oT_stored, it * 16 + 16)
                    if kind == DIFF:
                        dve.tensor_scalar_mul(oT[:, i * P:(i + 1) * P], o_ps[:, P:2 * P], t.sub_g[:, 0:1])\
                           .then_inc(oT_kept.sem, 1)
                    else:
                        dve.tensor_copy(oT[:, i * P:(i + 1) * P], o_ps[:, P:2 * P]).then_inc(oT_kept.sem, 1)

                def page(it, p):
                    n = page_keys(p)
                    g = min(p // 2, S_GROUPS - 1)
                    at = p * PAGE - 2 * g * PAGE
                    if p == 0:
                        dve.wait_ge(ps_done.sem, ps_done.after(it, -1))
                        dve.tensor_copy(q_block[:, :].rearrange("p (b c) -> p b c", b=BLOCKS)[:, :, 0:16],
                                        t.q_heads[:, bass.ds(it + TURNS * kind, 1), :, :, :]
                                        .rearrange("p s b u q -> p (s b) (u q)")).then_inc(q_spread.sem, 1)
                    dve.wait_ge(kT_done.sem, kT_done.after(it, 2 * p + 1))
                    dve.wait_ge(ps_done.sem, ps_done.after(it, g - 2))
                    dve.tensor_copy(kT_page[:, g % 2, 4:8, at:at + n], kT_ps[:, 1, :, 0:n]).then_inc(kT_kept[1].sem, 1)

                def page_scores(it, g):
                    if g == S_GROUPS - 1:
                        dve.wait_ge(ps_done.sem, ps_done.after(it, g))
                        dve.wait_ge(sfar.sem, sfar.after(it, g))
                        n = PAGE + DEC_SEQ
                        dve.tensor_tensor(sS[:, KEYS - n:KEYS], s_ps[:, PAGE:PAGE + n], t.near_dec[:, 0:n], ALU.add)\
                           .then_inc(snear.sem, 1)

                def weigh(it, n):
                    if n == 0:
                        dve.wait_ge(sfar.sem, sfar.after(it, S_GROUPS - 1))
                        dve.wait_ge(snear.sem, snear.after(it, 0))
                        dve.tensor_reduce(sstat[0:D0, 0:1], sS[0:D0, :], axis=AX.X, op=ALU.max, negate=True)\
                           .then_inc(smax.sem, 1)
                    elif n == 3:
                        dve.wait_ge(sln.sem, sln.after(it, 0))
                        dve.scalar_tensor_tensor(sW[D0:P, :], sS[D0:P, :], 0.0, sW[D0:P, :], ALU.max, ALU.add)\
                           .then_inc(ssoft.sem, 1)
                    elif n == 4:
                        dve.wait_ge(ssoft.sem, ssoft.after(it, 0))
                        dve.tensor_tensor_scan(sW[D0:P, ::-1], sW[D0:P, ::-1], sW[D0:P, ::-1], 0.0, ALU.add,
                                               ALU.bypass).then_inc(sscan.sem, 1)
                    elif n == 5:
                        dve.wait_ge(sscan.sem, sscan.after(it, 0))
                        dve.tensor_tensor(sW[D0:P, :], sS[D0:P, :], sW[D0:P, :], ALU.subtract).then_inc(ssub.sem, 1)
                    elif n == 6:
                        dve.wait_ge(sexp.sem, sexp.after(it, 0))
                        dve.reciprocal(sstat[0:D0, 2:3], sstat[0:D0, 1:2]).then_inc(sinv.sem, 1)
                        dve.wait_ge(sinv.sem, sinv.after(it, 0))
                        dve.tensor_tensor(sstat[0:D0, 3:4], sstat[0:D0, 2:3], t.row_factor[0:D0, :], ALU.mult)\
                           .then_inc(sinv.sem, 1)

                def turn(it, g):
                    if g % 2 == 1:
                        m = len(group_pages(g))
                        dve.wait_ge(kT_done.sem, kT_done.after(it, 2 * D_PAGES + g))
                        dve.wait_ge(applied[1].sem, applied[1].after(it, g - V_GROUPS))
                        dve.tensor_copy(sT[:, 4 * g:4 * g + m, :], kT_ps[:, 1, 0:m, :]).then_inc(kT_kept[1].sem, 1)

                def rows(it, kind_half):
                    dve.wait_ge(applied[kind_half].sem, applied[kind_half].after(it, V_GROUPS - 1))
                    dve.wait_ge(heads_done.sem, heads_done.after(it, -1))
                    if kind_half == 0:
                        dve.wait_ge(sinv.sem, sinv.after(it, 1))
                        dve.tensor_scalar_mul(o_rows_s[0:D0, :], sO_ps[0:D0, :], sstat[0:D0, 3:4])\
                           .then_inc(rows_kept[0].sem, 1)
                    else:
                        dve.tensor_copy(o_rows_s[D0:P, :], sO_ps[D0:P, :]).then_inc(rows_kept[1].sem, 1)

                def heads(it, _):
                    dve.wait_ge(heads_done.sem, heads_done.after(it, 0))
                    dve.tensor_copy(t.sample_o[:, bass.ds(it + TURNS * kind, 1), :].rearrange("p a n -> p (a n)"),
                                    sO_ps[:, 0:P]).then_inc(so_kept.sem, 1)

                steps = dict(score=score, soft=soft_diff if kind == DIFF else soft_stick, out=out, turn_out=turn_out,
                             page=page, page_scores=page_scores, weigh=weigh, turn=turn, rows=rows, heads=heads)
                dve.memset(qT[HEAD:P, 0, :], 0.0).then_inc(zeroed, 1)
                dve.memset(qT[0:HEAD, 1, :], 0.0).then_inc(zeroed, 1)
                dve.memset(q_block[:, :], 0.0).then_inc(zeroed, 1)
                dve.wait_ge(zeroed, 3)
                with dve.Fori(0, TURNS) as it:
                    for name, *args in plan:
                        if name in steps:
                            steps[name](it, *args)

            @block.scalar
            def _(act):
                for c in (sc_far, exps, s_abs, s_expm, s_ln, s_exp, o_kept, o_squared, kT_kept[0], sfar, sexp, sabs,
                          sexpm, sln, sstick):
                    act.sem_inc(c.sem, c.per)
                if kind == DIFF:
                    for c in (wT_kept,):
                        act.sem_inc(c.sem, c.per)

                def score(it, i):
                    for g, (ci, u, k0, k1, kn) in enumerate(chunks):
                        if ci != i or kn <= k0:
                            continue
                        act.wait_ge(sc_done.sem, sc_done.after(it, g))
                        act.wait_ge(w_turned.sem, w_turned.after(it, groups_upto[i - 2] - 1 if i >= 2 else
                                                                 groups_upto[PT - 2 + i] - 1 - groups_upto[-1]))
                        act.activation(S[:, i % 2, u, k0:kn], sc_ps[:, g % 2, 0:kn - k0], ACT.Copy)\
                           .then_inc(sc_far.sem, 1)

                def soft_diff(it, i, n):
                    end = (i + 1) * P
                    if n == 1:
                        act.wait_ge(row_max.sem, row_max.after(it, i))
                        for u in range(2):
                            act.activation(S[:, i % 2, u, 0:end], S[:, i % 2, u, 0:end], ACT.Exp,
                                           bias=stat[:, i % 4, u:u + 1],
                                           accum_out=stat[:, i % 4, 2 + u:3 + u]).then_inc(exps.sem, 1)

                def soft_stick(it, i, n):
                    end = (i + 1) * P
                    last_chunk = max(g for g, c in enumerate(chunks) if c[0] == i)
                    if n == 0:
                        act.wait_ge(sc_far.sem, sc_far.after(it, far_upto[last_chunk] - 1))
                        act.wait_ge(sc_near.sem, sc_near.after(it, near_upto[last_chunk] - 1))
                        act.wait_ge(s_sub.sem, s_sub.after(it, i - 1))
                        act.activation(aux[:, :, 0:end], S[:, i % 2, :, 0:end], ACT.Abs).then_inc(s_abs.sem, 1)
                    elif n == 1:
                        act.wait_ge(s_abs.sem, s_abs.after(it, i))
                        act.activation(aux[:, :, 0:end], aux[:, :, 0:end], ACT.Exp, scale=-1.0).then_inc(s_expm.sem, 1)
                    elif n == 2:
                        act.wait_ge(s_expm.sem, s_expm.after(it, i))
                        act.activation(aux[:, :, 0:end], aux[:, :, 0:end], ACT.Ln, bias=1.0).then_inc(s_ln.sem, 1)
                    elif n == 5:
                        act.wait_ge(s_sub.sem, s_sub.after(it, i))
                        act.activation(S[:, i % 2, :, 0:end], S[:, i % 2, :, 0:end], ACT.Exp).then_inc(s_exp.sem, 1)

                def out(it, i, n):
                    groups = turned_groups(kind, i)
                    first = groups_upto[i] - n_groups[i]
                    if n < len(groups):
                        if kind == DIFF:
                            act.wait_ge(w_turned.sem, w_turned.after(it, first + n))
                            act.wait_ge(o_done.sem, o_done.after(it, i - 1))
                            m = len(groups[n])
                            act.activation(wT[:, 4 * n:4 * n + m, :], wT_ps[:, 0:m, :], ACT.Copy)\
                               .then_inc(wT_kept.sem, 1)
                        return
                    act.wait_ge(o_done.sem, o_done.after(it, i))
                    if kind == STICK:
                        act.wait_ge(oT_done.sem, oT_done.after(it, i - 1))
                        act.activation(o_norm[:, :], o_ps[:, 0:P], ACT.Copy).then_inc(o_kept.sem, 1)
                    else:
                        act.wait_ge(o_normed.sem, o_normed.after(it, i - 2))
                        act.activation(o_rows[:, i % 2, :], o_ps[:, 0:P], ACT.Copy, scale=stat[:, i % 4, 4:5])\
                           .then_inc(o_kept.sem, 1)
                        act.wait_ge(o_kept.sem, o_kept.after(it, i))
                        act.wait_ge(o_squared.sem, o_squared.after(it, i - 1))
                        act.activation(o_sq[:, :], o_rows[:, i % 2, :], ACT.Square,
                                       accum_out=stat[:, i % 4, 5:6]).then_inc(o_squared.sem, 1)

                def page(it, p):
                    n = page_keys(p)
                    g = min(p // 2, S_GROUPS - 1)
                    at = p * PAGE - 2 * g * PAGE
                    act.wait_ge(kT_done.sem, kT_done.after(it, 2 * p))
                    act.wait_ge(ps_done.sem, ps_done.after(it, g - 2))
                    act.activation(kT_page[:, g % 2, 0:4, at:at + n], kT_ps[:, 0, :, 0:n], ACT.Copy)\
                       .then_inc(kT_kept[0].sem, 1)

                def page_scores(it, g):
                    n = 2 * PAGE if g + 1 < S_GROUPS else PAGE
                    act.wait_ge(ps_done.sem, ps_done.after(it, g))
                    act.wait_ge(ssub.sem, ssub.after(it, -1))
                    act.wait_ge(sexp.sem, sexp.after(it, -1))
                    act.activation(sS[:, 2 * g * PAGE:2 * g * PAGE + n], s_ps[:, 0:n], ACT.Copy).then_inc(sfar.sem, 1)

                def weigh(it, n):
                    if n == 0:
                        act.wait_ge(sfar.sem, sfar.after(it, S_GROUPS - 1))
                        act.wait_ge(snear.sem, snear.after(it, 0))
                        act.wait_ge(kT_done.sem, kT_done.after(it, -1))
                        act.activation(sW[D0:P, :], sS[D0:P, :], ACT.Abs).then_inc(sabs.sem, 1)
                    elif n == 1:
                        act.wait_ge(sabs.sem, sabs.after(it, 0))
                        act.activation(sW[D0:P, :], sW[D0:P, :], ACT.Exp, scale=-1.0).then_inc(sexpm.sem, 1)
                    elif n == 2:
                        act.wait_ge(sexpm.sem, sexpm.after(it, 0))
                        act.activation(sW[D0:P, :], sW[D0:P, :], ACT.Ln, bias=1.0).then_inc(sln.sem, 1)
                    elif n == 3:
                        act.wait_ge(smax.sem, smax.after(it, 0))
                        act.wait_ge(kT_done.sem, kT_done.after(it, -1))
                        act.wait_ge(rows_kept[0].sem, rows_kept[0].after(it, -1))
                        act.activation(sW[0:D0, :], sS[0:D0, :], ACT.Exp, bias=sstat[0:D0, 0:1],
                                       accum_out=sstat[0:D0, 1:2]).then_inc(sexp.sem, 1)
                    elif n == 6:
                        act.wait_ge(ssub.sem, ssub.after(it, 0))
                        act.activation(sW[D0:P, :], sW[D0:P, :], ACT.Exp).then_inc(sstick.sem, 1)

                def turn(it, g):
                    if g % 2 == 0:
                        m, n = len(group_pages(g)), page_keys(4 * g)
                        act.wait_ge(kT_done.sem, kT_done.after(it, 2 * D_PAGES + g))
                        act.wait_ge(applied[1].sem, applied[1].after(it, g - V_GROUPS))
                        act.activation(sT[0:n, 4 * g:4 * g + m, :], kT_ps[0:n, 0, 0:m, :], ACT.Copy)\
                           .then_inc(kT_kept[0].sem, 1)

                steps = dict(score=score, soft=soft_diff if kind == DIFF else soft_stick, out=out, page=page,
                             page_scores=page_scores, weigh=weigh, turn=turn)
                act.sem_inc(oT_stored, 16)
                with act.Fori(0, TURNS) as it:
                    for name, *args in plan:
                        if name in steps:
                            steps[name](it, *args)
                    act.wait_ge(oT_kept.sem, oT_kept.after(it, PT - 1))
                    act.dma_start(t.oT[:, bass.ds(it + TURNS * kind, 1), 0:SEQ].rearrange("p a n -> p (a n)"), oT[:, :])\
                       .then_inc(oT_stored, 16)
                act.wait_ge(oT_stored, 16 * (TURNS + 1))


        clear(nc, sems)


def sample_heads_out(nc, t):
    with ExitStack() as ctx:
        sems = []

        def sb(name, shape, dt=F32):
            return ctx.enter_context(nc.sbuf_tensor(name, shape, dt))

        def sem(name):
            sems.append(ctx.enter_context(nc.semaphore(name)))
            return sems[-1]

        oT = sb("sample_oT", [P, BLOCKS, P])
        mix = sb("sample_diff", [P, DEC_BATCH, H_DIFF, DEC_SEQ])
        sq = sb("sample_diff_sq", [P, DEC_BATCH * H_DIFF * DEC_SEQ])
        rms = sb("sample_rms", [P, DEC_BATCH * H_DIFF * DEC_SEQ])
        ms_ps = ctx.enter_context(nc.psum_tensor("sample_ms_ps", [P, BANK], F32))
        step, sums, roots, stored = sem("so_step"), sem("so_sums"), sem("so_roots"), sem("so_stored")
        N = DEC_BATCH * H_DIFF * DEC_SEQ
        with nc.Block() as block:

            @block.vector
            def _(dve):
                o = t.sample_o[:, :, :].rearrange("p s (b u q) -> p s b u q", b=BLOCKS, u=2)
                dve.memset(oT[:, :, :], 0.0).then_inc(step, 1)
                for s in range(DEC_BATCH):
                    dve.tensor_tensor(mix[:, s, :, :], o[:, s, 0:H_DIFF, 0, :], o[:, s, 0:H_DIFF, 1, :], ALU.add)\
                       .then_inc(step, 1)
                dve.wait_ge(step, 1 + DEC_BATCH)
                flat = mix[:, :, :, :].rearrange("p s h q -> p (s h q)")
                dve.tensor_tensor(sq[:, :], flat, flat, ALU.mult).then_inc(step, 1)
                for u in range(2):
                    rows = slice(HEAD * u, HEAD * u + HEAD)
                    for b in range(H_DIFF, BLOCKS):
                        dve.tensor_copy(oT[rows, b, 0:N_SAMPLE].rearrange("p (s q) -> p s q", q=DEC_SEQ),
                                        o[rows, :, b, u, :]).then_inc(step, 1)
                dve.wait_ge(sums, 1)
                dve.tensor_scalar(rms[:, :], ms_ps[:, 0:N], 1.0 / P, SUBLN_EPS, ALU.mult, ALU.add).then_inc(step, 1)
                dve.wait_ge(roots, 1)
                dve.reciprocal(rms[:, :], rms[:, :]).then_inc(step, 1)
                done = 1 + DEC_BATCH + 1 + 2 * (BLOCKS - H_DIFF) + 2
                dve.wait_ge(step, done)
                dve.scalar_tensor_tensor(rms[:, :], rms[:, :], t.sub_g[:, 0:1], flat, ALU.mult, ALU.mult)\
                   .then_inc(step, 1)
                dve.wait_ge(step, done + 1)
                for b in range(H_DIFF):
                    dve.tensor_copy(oT[:, b, 0:N_SAMPLE].rearrange("p (s q) -> p s q", q=DEC_SEQ),
                                    rms[:, :].rearrange("p (s h q) -> p h s q", h=H_DIFF, q=DEC_SEQ)[:, b])\
                       .then_inc(step, 1)

            @block.tensor
            def _(pe):
                pe.wait_ge(step, 2 + DEC_BATCH)
                pe.matmul(ms_ps[:, 0:N], t.ones[:, :], sq[:, :], start=True, stop=True).then_inc(sums, 1)

            @block.scalar
            def _(act):
                act.wait_ge(step, 1 + DEC_BATCH + 1 + 2 * (BLOCKS - H_DIFF) + 1)
                act.activation(rms[:, :], rms[:, :], ACT.Sqrt).then_inc(roots, 1)

            @block.sync
            def _(sp):
                sp.wait_ge(step, 1 + DEC_BATCH + 1 + 2 * (BLOCKS - H_DIFF) + 3 + H_DIFF)
                sp.dma_start(t.oT[:, :, SEQ:TILES * P], oT[:, :, :]).then_inc(stored, 16)
                sp.wait_ge(stored, 16)

        clear(nc, sems)


N_LOGITS = N_GROUPS + N_EXPERTS
N_SLOTS = MOE_TILES * P
ALL = TILES * P


def tile_loop(engine, tile):
    with engine.Fori(0, PT // 2) as it:
        for u in range(2):
            tile(it, u)
    tile(PT // 2, 0)


def row_tile(dram, tile):
    return dram[bass.ds(tile * P, P), :]


def mix_out(nc, t):
    with ExitStack() as ctx:
        sems = []

        def sb(name, shape, dt=F32):
            return ctx.enter_context(nc.sbuf_tensor(name, shape, dt))

        def ps(name, shape):
            return ctx.enter_context(nc.psum_tensor(name, shape, F32))

        def sem(name):
            sems.append(ctx.enter_context(nc.semaphore(name)))
            return sems[-1]

        w_out = sb("w_out", [P, BLOCKS, 2, BANK])
        w_route = sb("w_route", [P, KC, N_LOGITS])
        b_route = sb("b_route", [P, N_LOGITS])
        g_row = sb("g_ffn_row", [P, D_MODEL])
        oT = sb("oT_tile", [P, 2, BLOCKS, P])
        x = sb("x_again", [P, 2, D_MODEL])
        x1 = sb("x1_tile", [P, 2, D_MODEL])
        h = sb("h2_tile", [P, 2, D_MODEL])
        hT = sb("h2T_tile", [P, KC, P])
        square = sb("square2", [P, D_MODEL])
        ss = sb("sum_squares2", [P, 2, 3])
        y_ps = ps("mix_out_ps", [P, 2, 2, BANK])
        hT_ps = ps("h2T_ps", [P, 2, BANK])
        lg_ps = ps("logits_ps", [P, BANK])

        w_loaded, r_loaded = sem("w_out_loaded"), sem("routers_loaded")
        x_loaded = [sem(f"x_again_loaded{u}") for u in range(2)]
        o_loaded = [sem(f"oT_loaded{u}") for u in range(2)]
        stored = [sem(f"x1_h2_stored{u}") for u in range(2)]
        y_done = Count(sem("mix_out_in_psum"), 4)
        x1_done = Count(sem("x1_done"), 4)
        squares = Count(sem("squares2_done"), 2)
        rstd_step = Count(sem("rstd2_step"), 2)
        rstd = Count(sem("rstd2_done"), 2)
        h_done = Count(sem("h2_done"), 2)
        hT_done = Count(sem("h2T_in_psum"), 4)
        hT_kept = Count(sem("h2T_kept"), 4)
        lg_done = Count(sem("logits_in_psum"), 2)
        lg_kept = Count(sem("logits_kept"), 2)

        with nc.Block() as block:

            @block.sync
            def _(sp):
                sp.dma_start(w_route[:, :, 0:N_GROUPS], t.w_group.rearrange("(k p) n -> p k n", p=P))\
                  .then_inc(r_loaded, 16)
                sp.dma_start(w_route[:, :, N_GROUPS:N_LOGITS], t.w_erouter.rearrange("(k p) n -> p k n", p=P))\
                  .then_inc(r_loaded, 16)
                sp.dma_start(b_route[:, 0:N_GROUPS], t.b_group.partition_broadcast(P)).then_inc(r_loaded, 16)
                sp.dma_start(b_route[:, N_GROUPS:N_LOGITS], t.b_erouter.partition_broadcast(P)).then_inc(r_loaded, 16)
                sp.dma_start(g_row[:, :], t.g_ffn.partition_broadcast(P)).then_inc(r_loaded, 16)
                for u in range(2):
                    sp.sem_inc(stored[u], 32)

                def load(it, u, tile):
                    sp.dma_start(oT[:, u, :, :], t.oT[:, :, bass.ds(tile * P, P)]).then_inc(o_loaded[u], 16)
                    sp.dma_start(x[:, u, :], row_tile(t.x, tile)).then_inc(x_loaded[u], 16)

                load(0, 0, 0)
                sp.dma_start(w_out[:, :, :, :], t.w_out.rearrange("(k p) (c n) -> p k c n", p=P, n=BANK))\
                  .then_inc(w_loaded, 16)

                def tile(it, u, final=False):
                    if not final:
                        sp.wait_ge(x1_done.sem, x1_done.after(it, 2 * (u - 1) + 1))
                        load(it, 1 - u, it * 2 + u + 1)
                    sp.wait_ge(x1_done.sem, x1_done.after(it, 2 * u + 1))
                    sp.dma_start(row_tile(t.x1, it * 2 + u), x1[:, u, :]).then_inc(stored[u], 16)
                    sp.wait_ge(h_done.sem, h_done.after(it, u))
                    sp.dma_start(row_tile(t.h2, it * 2 + u), h[:, u, :]).then_inc(stored[u], 16)

                with sp.Fori(0, PT // 2) as it:
                    for u in range(2):
                        tile(it, u)
                tile(PT // 2, 0, final=True)
                sp.wait_ge(stored[0], 32 * (2 + PT // 2))
                sp.wait_ge(stored[1], 32 * (1 + PT // 2))

            @block.tensor
            def _(pe):
                for c in (y_done, hT_done, lg_done):
                    pe.sem_inc(c.sem, c.per)

                def out(it, u):
                    pe.wait_ge(o_loaded[u], it * 16 + 16)
                    for c in range(2):
                        pe.wait_ge(x1_done.sem, x1_done.after(it, 2 * (u - 2) + c))
                        for k in range(BLOCKS):
                            last = pe.matmul(y_ps[:, u, c, :], oT[:, u, k, :], w_out[:, k, c, :],
                                             start=(k == 0), stop=(k == BLOCKS - 1))
                        last.then_inc(y_done.sem, 1)

                def route(it, u):
                    pe.wait_ge(h_done.sem, h_done.after(it, u))
                    for half in range(2):
                        pe.wait_ge(hT_kept.sem, hT_kept.after(it, 2 * (u - 1) + half))
                        for k in range(4):
                            last = pe.transpose(hT_ps[:, half, k * P:(k + 1) * P],
                                                h[:, u, (4 * half + k) * P:(4 * half + k + 1) * P], t.ident[:, :])
                        last.then_inc(hT_done.sem, 1)
                    pe.wait_ge(hT_kept.sem, hT_kept.after(it, 2 * u + 1))
                    pe.wait_ge(lg_kept.sem, lg_kept.after(it, u - 1))
                    for k in range(KC):
                        last = pe.matmul(lg_ps[:, 0:N_LOGITS], hT[:, k, :], w_route[:, k, :],
                                         start=(k == 0), stop=(k == KC - 1))
                    last.then_inc(lg_done.sem, 1)

                pe.wait_ge(w_loaded, 16)
                pe.wait_ge(r_loaded, 16 * 5)
                out(0, 0)
                with pe.Fori(0, PT // 2) as it:
                    for u in range(2):
                        out(it + u, 1 - u)
                        route(it, u)
                route(PT // 2, 0)

            @block.vector
            def _(dve):
                for c in (x1_done, h_done, lg_kept):
                    dve.sem_inc(c.sem, c.per)
                dve.wait_ge(r_loaded, 16 * 5)

                def residual(it, u):
                    dve.wait_ge(x_loaded[u], it * 16 + 16)
                    dve.wait_ge(stored[u], it * 32 + 32)
                    dve.wait_ge(h_done.sem, h_done.after(it, u - 2))
                    dve.wait_ge(squares.sem, squares.after(it, u - 2))
                    for c in range(2):
                        dve.wait_ge(y_done.sem, y_done.after(it, 2 * u + c))
                        dve.tensor_tensor(x1[:, u, c * BANK:(c + 1) * BANK], y_ps[:, u, c, :],
                                          x[:, u, c * BANK:(c + 1) * BANK], ALU.add).then_inc(x1_done.sem, 1)

                def tile(it, u, final=False):
                    dve.wait_ge(rstd.sem, rstd.after(it, u))
                    dve.wait_ge(x1_done.sem, x1_done.after(it, 2 * u + 1))
                    dve.wait_ge(hT_done.sem, hT_done.after(it, 2 * (u - 2) + 1))
                    dve.scalar_tensor_tensor(h[:, u, :], x1[:, u, :], ss[:, u, 2:3], g_row[:, :], ALU.mult, ALU.mult)\
                       .then_inc(h_done.sem, 1)
                    if not final:
                        residual(it + u, 1 - u)
                    dve.wait_ge(lg_done.sem, lg_done.after(it, u))
                    dve.tensor_tensor(t.logits[:, bass.ds(it * 2 + u, 1), :].rearrange("p a n -> p (a n)"),
                                      lg_ps[:, 0:N_LOGITS], b_route[:, :], ALU.add).then_inc(lg_kept.sem, 1)

                residual(0, 0)
                with dve.Fori(0, PT // 2) as it:
                    for u in range(2):
                        tile(it, u)
                tile(PT // 2, 0, final=True)

            @block.gpsimd
            def _(pool):
                pool.sem_inc(rstd_step.sem, rstd_step.per)
                pool.sem_inc(rstd.sem, rstd.per)

                def tile(it, u):
                    pool.wait_ge(squares.sem, squares.after(it, u))
                    own_wait(pool, t)
                    pool.tensor_scalar(ss[:, u, 1:2], ss[:, u, 0:1], 1.0 / D_MODEL, NORM_EPS, ALU.mult, ALU.add)\
                        .then_inc(rstd_step.sem, 1)
                    pool.wait_ge(rstd_step.sem, rstd_step.after(it, u))
                    pool.wait_ge(h_done.sem, h_done.after(it, u - 2))
                    pool.tensor_tensor(ss[:, u, 2:3], ss[:, u, 1:2], t.neg_half[:, :], ALU.pow)\
                        .then_inc(rstd.sem, 1)

                tile_loop(pool, tile)

            @block.scalar
            def _(act):
                act.sem_inc(squares.sem, squares.per)
                act.sem_inc(hT_kept.sem, hT_kept.per)

                def square_sum(it, u):
                    act.wait_ge(x1_done.sem, x1_done.after(it, 2 * u + 1))
                    act.wait_ge(squares.sem, squares.after(it, u - 1))
                    act.activation(square[:, :], x1[:, u, :], ACT.Square, accum_out=ss[:, u, 0:1])\
                       .then_inc(squares.sem, 1)

                def tile(it, u, final=False):
                    for half in range(2):
                        act.wait_ge(hT_done.sem, hT_done.after(it, 2 * u + half))
                        act.wait_ge(lg_done.sem, lg_done.after(it, u - 1))
                        act.activation(hT[:, 4 * half:4 * half + 4, :], hT_ps[:, half, :], ACT.Copy)\
                           .then_inc(hT_kept.sem, 1)
                    if not final:
                        square_sum(it + u, 1 - u)

                square_sum(0, 0)
                with act.Fori(0, PT // 2) as it:
                    for u in range(2):
                        tile(it, u)
                tile(PT // 2, 0, final=True)

        clear(nc, sems)


def route(nc, t):
    with ExitStack() as ctx:
        sems = []

        def sb(name, shape, dt=F32):
            return ctx.enter_context(nc.sbuf_tensor(name, shape, dt))

        def sem(name):
            sems.append(ctx.enter_context(nc.semaphore(name)))
            return sems[-1]

        G, J, E = N_GROUPS, PER_GROUP, N_EXPERTS
        rank = sb("first_wins", [P, TILES, G])
        limits = sb("limits", [P, E, TILES])
        tile_no = sb("tile_numbers", [P, MOE_TILES, E])
        spare = sb("spare_slots", [P, TILES])
        before = sb("before", [P, P])
        token = sb("token_ids", [P, TILES])
        column = sb("column_numbers", [P, P])
        part_i = sb("slot_parts_i", [P, 2, TOP_K * TILES], I32)
        part = sb("slot_parts", [P, 2, TOP_K * TILES])
        place = sb("place_hot", [P, 2, P])
        tile_token = sb("token_by_tile", [P, 2, MOE_TILES])
        g_max = sb("g_max", [P, TILES, 1])
        g_exp = sb("g_exp", [P, TILES, G])
        g_hot = sb("g_hot", [P, TILES, G])
        one = sb("one_hot", [P, 2, TILES, J])
        tmp = sb("tmp4", [P, TILES, G])
        top = sb("top", [P, 4, TILES, 1])
        el = sb("group_logits", [P, TILES, J])
        prod = sb("group_products", [P, TILES, J, G])
        hot = sb("expert_hot", [P, 2, TILES, G, J])
        member = sb("member", [P, TILES, E])
        pos = sb("positions", [P, TILES, E])
        total = sb("tile_counts", [P, TILES, E])
        carry = sb("carried", [P, TILES + 1, E])
        filled = sb("filled", [P, E, TILES])
        n_tiles = sb("n_tiles", [P, E])
        ends = sb("tile_ends", [P, E])
        base = sb("slot_bases", [P, E])
        passed = sb("passed", [P, MOE_TILES, E])
        te = sb("tile_expert_f", [P, MOE_TILES])
        slot_f = sb("slot_f", [P, 2, TILES])
        picked = sb("picked", [P, 2, TILES, E])
        zero_y = sb("zero_y", [P, D_MODEL])
        cnt_ps = ctx.enter_context(nc.psum_tensor("counts_ps", [P, 2, BANK], F32))
        loaded, step, gexp, wexp = sem("route_loaded"), sem("route_step"), sem("g_exp_done"), sem("w_exp_done")
        counted, zeroed, spare_stored, placed = sem("counted"), sem("zeroed_y"), sem("spare_rows_stored"), sem("placed")

        with nc.Block() as block:

            @block.vector
            def _(dve):
                done = [0]

                def link(ins):
                    done[0] += 1
                    ins.then_inc(step, 1)
                    dve.wait_ge(step, done[0])

                def wide(ap, shape):
                    return ap.broadcast_to(shape)

                S3 = [P, TILES, G]

                def first_max(values, maximum, out):
                    link(dve.tensor_tensor(tmp[:, :, :], values, wide(maximum, S3), ALU.is_equal))
                    link(dve.tensor_tensor(tmp[:, :, :], tmp[:, :, :], rank[:, :, :], ALU.mult))
                    link(dve.tensor_reduce(top[:, 3, :, :], tmp[:, :, :], axis=AX.X, op=ALU.max))
                    link(dve.tensor_tensor(out, tmp[:, :, :], wide(top[:, 3, :, :], S3), ALU.is_equal))

                gl = t.logits[:, :, 0:G]
                dve.wait_ge(loaded, 16 * 7)
                link(dve.tensor_reduce(g_max[:, :, :], gl, axis=AX.X, op=ALU.max))
                link(dve.tensor_tensor(g_exp[:, :, :], gl, wide(g_max[:, :, :], S3), ALU.subtract))
                t.n_gdiff = done[0]
                first_max(gl, g_max[:, :, :], g_hot[:, :, :])
                for g in range(G):
                    link(dve.tensor_tensor(prod[:, :, :, g], t.logits[:, :, G + J * g:G + J * g + J],
                                           wide(g_hot[:, :, g:g + 1], [P, TILES, J]), ALU.mult))
                link(dve.tensor_reduce(el[:, :, :], prod[:, :, :, :], axis=AX.X, op=ALU.add))
                link(dve.tensor_reduce(top[:, 0, :, :], el[:, :, :], axis=AX.X, op=ALU.max))
                first_max(el[:, :, :], top[:, 0, :, :], one[:, 0, :, :])
                link(dve.scalar_tensor_tensor(el[:, :, :], one[:, 0, :, :], NEG, el[:, :, :], ALU.mult, ALU.add))
                link(dve.tensor_reduce(top[:, 1, :, :], el[:, :, :], axis=AX.X, op=ALU.max))
                first_max(el[:, :, :], top[:, 1, :, :], one[:, 1, :, :])
                link(dve.tensor_tensor(top[:, 2, :, :], top[:, 1, :, :], top[:, 0, :, :], ALU.subtract))
                t.n_wdiff = done[0]
                for k in range(TOP_K):
                    for g in range(G):
                        link(dve.tensor_tensor(hot[:, k, :, g, :], one[:, k, :, :],
                                               wide(g_hot[:, :, g:g + 1], [P, TILES, J]), ALU.mult))
                link(dve.memset(hot[N_SAMPLE:P, :, PT, :, :], 0.0))
                link(dve.tensor_tensor(member[:, :, :], hot[:, 0, :, :, :].rearrange("p t g j -> p t (g j)"),
                                       hot[:, 1, :, :, :].rearrange("p t g j -> p t (g j)"), ALU.add))
                t.n_member = done[0]
                dve.wait_ge(gexp, 1)
                link(dve.tensor_reduce(g_max[:, :, :], g_exp[:, :, :], axis=AX.X, op=ALU.add))
                dve.wait_ge(wexp, 1)
                link(dve.tensor_scalar_add(top[:, 3, :, :], top[:, 2, :, :], 1.0))
                link(dve.tensor_tensor(g_max[:, :, :], g_max[:, :, :], top[:, 3, :, :], ALU.mult))
                link(dve.reciprocal(t.gates[:, 0, :], g_max[:, :, 0]))
                link(dve.tensor_tensor(t.gates[:, 1, :], t.gates[:, 0, :], top[:, 2, :, 0], ALU.mult))
                dve.wait_ge(counted, 1)
                flat = "p t e -> p (t e)"
                link(dve.tensor_copy(pos[:, :, :].rearrange(flat), cnt_ps[:, 0, 0:TILES * E]))
                link(dve.tensor_copy(total[:, :, :].rearrange(flat), cnt_ps[:, 1, 0:TILES * E]))
                link(dve.memset(carry[:, 0, :], 0.0))
                for n in range(TILES):
                    link(dve.tensor_tensor(carry[:, n + 1, :], carry[:, n, :], total[:, n, :], ALU.add))
                link(dve.tensor_tensor(filled[:, :, :],
                                       wide(carry[:, TILES, :].unsqueeze(2), [P, E, TILES]), limits[:, :, :], ALU.is_gt))
                link(dve.tensor_reduce(n_tiles[:, :], filled[:, :, :], axis=AX.X, op=ALU.add))
                link(dve.tensor_tensor_scan(ends[:, :], n_tiles[:, :], n_tiles[:, :], 0.0, ALU.add, ALU.bypass))
                link(dve.tensor_tensor(base[:, :], ends[:, :], n_tiles[:, :], ALU.subtract))
                link(dve.tensor_scalar_mul(base[:, :], base[:, :], float(P)))
                link(dve.tensor_tensor(passed[:, :, :], tile_no[:, :, :],
                                       wide(ends[:, :].unsqueeze(1), [P, MOE_TILES, E]), ALU.is_ge))
                link(dve.tensor_reduce(te[:, :], passed[:, :, :], axis=AX.X, op=ALU.add))
                link(dve.tensor_scalar_min(te[:, :], te[:, :], float(E - 1)))
                link(dve.tensor_copy(t.tile_expert[:, :], te[0:1, :]))
                link(dve.tensor_tensor(pos[:, :, :], pos[:, :, :], carry[:, 0:TILES, :], ALU.add))
                link(dve.tensor_tensor(pos[:, :, :], pos[:, :, :],
                                       wide(base[:, :].unsqueeze(1), [P, TILES, E]), ALU.add))
                for k in range(TOP_K):
                    link(dve.tensor_tensor(picked[:, k, :, :], hot[:, k, :, :, :].rearrange("p t g j -> p t (g j)"),
                                           pos[:, :, :], ALU.mult))
                    link(dve.tensor_reduce(slot_f[:, k, :], picked[:, k, :, :], axis=AX.X, op=ALU.add))
                    link(dve.tensor_tensor(slot_f[:, k, :], slot_f[:, k, :], spare[:, :], ALU.add))
                    link(dve.tensor_copy(t.slots[:, :].rearrange("p (t k) -> p k t", k=2)[:, k], slot_f[:, k, :]))
                link(dve.tensor_scalar(part_i[:, 0, :], t.slots[:, :], P.bit_length() - 1, None, ALU.logical_shift_right))
                link(dve.tensor_scalar(part_i[:, 1, :], t.slots[:, :], P - 1, None, ALU.bitwise_and))
                link(dve.tensor_copy(part[:, :, :], part_i[:, :, :]))
                t.n_first_place = done[0] + 2
                for n in range(TOP_K * TILES):
                    if n >= 2:
                        dve.wait_ge(placed, n - 1)
                    done[0] += 2
                    dve.tensor_scalar(place[:, n % 2, :], column[:, :], part[:, 1, n:n + 1], None, ALU.is_equal)\
                       .then_inc(step, 1)
                    dve.tensor_scalar(tile_token[:, n % 2, :], column[:, 0:MOE_TILES], part[:, 0, n:n + 1],
                                      token[:, n // TOP_K:n // TOP_K + 1], ALU.is_equal, ALU.mult).then_inc(step, 1)
                dve.wait_ge(placed, TOP_K * TILES)
                link(dve.tensor_copy(t.slot_tok[:, :], cnt_ps[:, 0, 0:MOE_TILES]))

            @block.sync
            def _(sp):
                for dst, src in ((rank, t.rank_const), (limits, t.limits_const), (tile_no, t.tile_no_const)):
                    sp.dma_start(dst[:, :, :], src.partition_broadcast(P)).then_inc(loaded, 16)
                sp.dma_start(column[:, :], t.column_const.partition_broadcast(P)).then_inc(loaded, 16)
                for dst, src in ((spare, t.spare_const), (before, t.before_const), (token, t.token_const)):
                    sp.dma_start(dst[:, :], src).then_inc(loaded, 16)
                sp.wait_ge(zeroed, 1)
                sp.dma_start(t.moe_out[N_SLOTS:N_SLOTS + P, :], zero_y[:, :]).then_inc(spare_stored, 16)
                sp.wait_ge(spare_stored, 16)

            @block.tensor
            def _(pe):
                pe.wait_ge(step, t.n_member)
                pe.matmul(cnt_ps[:, 0, 0:TILES * E], before[:, :], member[:, :, :], start=True, stop=True)
                pe.matmul(cnt_ps[:, 1, 0:TILES * E], t.ones[:, :], member[:, :, :], start=True, stop=True)\
                  .then_inc(counted, 1)
                for n in range(TOP_K * TILES):
                    pe.wait_ge(step, t.n_first_place + 2 * n)
                    pe.matmul(cnt_ps[:, 0, 0:MOE_TILES], place[:, n % 2, :], tile_token[:, n % 2, :], start=(n == 0),
                              stop=(n == TOP_K * TILES - 1)).then_inc(placed, 1)

            @block.scalar
            def _(act):
                act.wait_ge(step, t.n_gdiff)
                act.activation(g_exp[:, :, :], g_exp[:, :, :], ACT.Exp).then_inc(gexp, 1)
                act.wait_ge(step, t.n_wdiff)
                act.activation(top[:, 2, :, :], top[:, 2, :, :], ACT.Exp).then_inc(wexp, 1)

            @block.gpsimd
            def _(pool):
                pool.memset(zero_y[:, :], 0.0).then_inc(zeroed, 1)

        clear(nc, sems)


GU = 2 * D_EXPERT


def experts(nc, t):
    with ExitStack() as ctx:
        sems = []

        def sb(name, shape, dt=F32):
            return ctx.enter_context(nc.sbuf_tensor(name, shape, dt))

        def ps(name, shape):
            return ctx.enter_context(nc.psum_tensor(name, shape, F32))

        def sem(name):
            sems.append(ctx.enter_context(nc.semaphore(name)))
            return sems[-1]

        class TileCount:

            def __init__(self, name, per):
                self.sem, self.per = sem(name), per

            def after(self, tile, k):
                return tile * self.per + (2 * self.per + k + 1)

        FK = D_EXPERT // P
        w_gu = sb("w_gate_up", [P, 2, KC, 2, D_EXPERT])
        w_dn = sb("w_down", [P, 2, FK, D_MODEL])
        rows = sb("slot_rows", [P, 2, D_MODEL])
        idx = sb("slot_index", [P, 2], I32)
        xT = sb("slot_rows_T", [P, 2, KC, P])
        gate = sb("silu_gate", [P, 2, D_EXPERT])
        act_rows = sb("expert_act", [P, 2, D_EXPERT])
        aT = sb("expert_act_T", [P, 2, FK, P])
        y = sb("expert_out", [P, 2, D_MODEL])
        gu_ps = ps("gate_up_ps", [P, 2, GU])
        xT_ps = ps("slot_rows_T_ps", [P, 2, BANK])
        aT_ps = ps("act_T_ps", [P, BANK])
        y_ps = ps("expert_out_ps", [P, 2, BANK])

        gu_loaded = [sem(f"w_gate_up_loaded{u}") for u in range(2)]
        dn_loaded = [sem(f"w_down_loaded{u}") for u in range(2)]
        rows_loaded = [sem(f"slot_rows_loaded{u}") for u in range(2)]
        y_stored = [sem(f"expert_out_stored{u}") for u in range(2)]
        idx_done = TileCount("slot_index_done", 1)
        xT_done, xT_kept = TileCount("xT_in_psum", 2), TileCount("xT_kept", 2)
        gu_done, silu = TileCount("gate_up_in_psum", 1), TileCount("silu_done", 1)
        a_done, aT_done, aT_kept = TileCount("act_done", 1), TileCount("aT_in_psum", 1), TileCount("aT_kept", 1)
        y_done = TileCount("y_in_psum", 2)
        y_kept = [TileCount("y_half0_kept", 1), TileCount("y_half1_kept", 1)]

        def tiles(engine, step):
            with engine.Fori(0, MOE_TILES // 2 - 1) as it:
                for u in range(2):
                    step(it * 2 + (1 + u), (1 + u) % 2, it + u)

        LAST = MOE_TILES - 1
        assert LAST % 2 == 1

        with nc.Block() as block:

            @block.sync
            def _(sp):
                def load(tile, u):
                    e = sp.value_load(t.tile_expert[0:1, bass.ds(tile, 1)], min_val=0, max_val=N_EXPERTS - 1)
                    sp.wait_ge(gu_done.sem, gu_done.after(tile, -2))
                    for n, w in enumerate((t.w_gate, t.w_up)):
                        sp.dma_start(w_gu[:, u, :, n, :], w[bass.ds(e, 1), :, :].rearrange("e (k p) n -> p (e k) n", p=P))\
                          .then_inc(gu_loaded[u], 16)
                    sp.wait_ge(y_done.sem, y_done.after(tile, -3))
                    sp.dma_start(w_dn[:, u, :, :], t.w_down[bass.ds(e, 1), :, :].rearrange("e (k p) n -> p (e k) n", p=P))\
                      .then_inc(dn_loaded[u], 16)

                with sp.Fori(0, MOE_TILES // 2) as it:
                    for u in range(2):
                        load(it * 2 + u, u)

            @block.gpsimd
            def _(pool):
                pool.sem_inc(idx_done.sem, 2)
                with pool.Fori(0, MOE_TILES // 2) as it:
                    for u in range(2):
                        tile = it * 2 + u
                        pool.wait_ge(xT_done.sem, xT_done.after(tile, -3))
                        pool.tensor_copy(idx[:, u:u + 1], t.slot_tok[:, bass.ds(tile, 1)]).then_inc(idx_done.sem, 1)
                        pool.wait_ge(idx_done.sem, idx_done.after(tile, 0))
                        own_wait(pool, t)
                        pool.indirect_dma_start(rows[:, u, :], None, t.h2[:, :],
                                                bass.IndirectOffsetOnAxis(ap=idx[:, u:u + 1], axis=0))\
                            .then_inc(rows_loaded[u], 16)

            @block.tensor
            def _(pe):
                for c in (xT_done, gu_done, aT_done, y_done):
                    pe.sem_inc(c.sem, 2 * c.per)

                def turn_rows(tile, u, turn):
                    pe.wait_ge(rows_loaded[u], turn * 16 + 16)
                    for half in range(2):
                        pe.wait_ge(xT_kept.sem, xT_kept.after(tile, half - 2))
                        for k in range(4):
                            last = pe.transpose(xT_ps[:, half, k * P:(k + 1) * P],
                                                rows[:, u, (4 * half + k) * P:(4 * half + k + 1) * P], t.ident[:, :])
                        last.then_inc(xT_done.sem, 1)

                def gate_up(tile, u, turn):
                    pe.wait_ge(xT_kept.sem, xT_kept.after(tile, 1))
                    pe.wait_ge(gu_loaded[u], turn * 32 + 32)
                    pe.wait_ge(a_done.sem, a_done.after(tile, -2))
                    for k in range(KC):
                        last = pe.matmul(gu_ps[:, u, :], xT[:, u, k, :], w_gu[:, u, k, :, :],
                                         start=(k == 0), stop=(k == KC - 1))
                    last.then_inc(gu_done.sem, 1)

                def turn_act(tile, u):
                    pe.wait_ge(a_done.sem, a_done.after(tile, 0))
                    pe.wait_ge(aT_kept.sem, aT_kept.after(tile, -1))
                    for k in range(FK):
                        last = pe.transpose(aT_ps[:, k * P:(k + 1) * P], act_rows[:, u, k * P:(k + 1) * P], t.ident[:, :])
                    last.then_inc(aT_done.sem, 1)

                def down(tile, u, turn):
                    pe.wait_ge(aT_kept.sem, aT_kept.after(tile, 0))
                    pe.wait_ge(dn_loaded[u], turn * 16 + 16)
                    for c in range(2):
                        pe.wait_ge(y_kept[c].sem, y_kept[c].after(tile, -1))
                        for k in range(FK):
                            last = pe.matmul(y_ps[:, c, :], aT[:, u, k, :], w_dn[:, u, k, c * BANK:(c + 1) * BANK],
                                             start=(k == 0), stop=(k == FK - 1))
                        last.then_inc(y_done.sem, 1)

                turn_rows(0, 0, 0)
                gate_up(0, 0, 0)
                turn_rows(1, 1, 0)
                turn_act(0, 0)

                def step(tile, u, turn):
                    gate_up(tile, u, turn)
                    down(tile - 1, 1 - u, turn if u == 1 else turn - 1)
                    turn_rows(tile + 1, 1 - u, turn if u == 0 else turn + 1)
                    turn_act(tile, u)

                tiles(pe, step)
                half = MOE_TILES // 2
                gate_up(LAST, 1, half - 1)
                down(LAST - 1, 0, half - 1)
                turn_act(LAST, 1)
                down(LAST, 1, half - 1)

            @block.vector
            def _(dve):
                for c in (a_done, xT_kept, y_kept[1]):
                    dve.sem_inc(c.sem, 2 * c.per)

                def keep_rows(tile, u):
                    for half in range(2):
                        dve.wait_ge(xT_done.sem, xT_done.after(tile, half))
                        dve.wait_ge(gu_done.sem, gu_done.after(tile, -2))
                        dve.tensor_copy(xT[:, u, 4 * half:4 * half + 4, :], xT_ps[:, half, :]).then_inc(xT_kept.sem, 1)

                def multiply(tile, u):
                    dve.wait_ge(silu.sem, silu.after(tile, 0))
                    dve.wait_ge(aT_done.sem, aT_done.after(tile, -2))
                    dve.tensor_tensor(act_rows[:, u, :], gu_ps[:, u, D_EXPERT:GU], gate[:, u, :], ALU.mult)\
                       .then_inc(a_done.sem, 1)

                def keep_y(tile, u, turn):
                    dve.wait_ge(y_done.sem, y_done.after(tile, 1))
                    dve.wait_ge(y_stored[u], turn * 16 + 16)
                    dve.tensor_copy(y[:, u, BANK:D_MODEL], y_ps[:, 1, :]).then_inc(y_kept[1].sem, 1)

                keep_rows(0, 0)
                multiply(0, 0)
                keep_rows(1, 1)

                def step(tile, u, turn):
                    multiply(tile, u)
                    keep_y(tile - 1, 1 - u, turn if u == 1 else turn - 1)
                    keep_rows(tile + 1, 1 - u)

                tiles(dve, step)
                half = MOE_TILES // 2
                multiply(LAST, 1)
                keep_y(LAST - 1, 0, half - 1)
                keep_y(LAST, 1, half - 1)

            @block.scalar
            def _(act):
                for c in (silu, aT_kept, y_kept[0]):
                    act.sem_inc(c.sem, 2 * c.per)
                for u in range(2):
                    act.sem_inc(y_stored[u], 16)

                def swish(tile, u):
                    act.wait_ge(gu_done.sem, gu_done.after(tile, 0))
                    act.wait_ge(a_done.sem, a_done.after(tile, -2))
                    act.activation(gate[:, u, :], gu_ps[:, u, 0:D_EXPERT], ACT.Silu).then_inc(silu.sem, 1)

                def keep_act(tile, u):
                    act.wait_ge(aT_done.sem, aT_done.after(tile, 0))
                    act.wait_ge(y_done.sem, y_done.after(tile, -3))
                    act.activation(aT[:, u, :, :], aT_ps[:, 0:FK * P], ACT.Copy).then_inc(aT_kept.sem, 1)

                def keep_y(tile, u, turn):
                    act.wait_ge(y_done.sem, y_done.after(tile, 0))
                    act.wait_ge(y_stored[u], turn * 16 + 16)
                    act.activation(y[:, u, 0:BANK], y_ps[:, 0, :], ACT.Copy).then_inc(y_kept[0].sem, 1)

                def store_y(tile, u):
                    act.wait_ge(y_kept[0].sem, y_kept[0].after(tile, 0))
                    act.wait_ge(y_kept[1].sem, y_kept[1].after(tile, 0))
                    act.dma_start(row_tile(t.moe_out, tile), y[:, u, :]).then_inc(y_stored[u], 16)

                swish(0, 0)
                keep_act(0, 0)

                def step(tile, u, turn):
                    swish(tile, u)
                    keep_y(tile - 1, 1 - u, turn if u == 1 else turn - 1)
                    keep_act(tile, u)
                    store_y(tile - 1, 1 - u)

                tiles(act, step)
                half = MOE_TILES // 2
                swish(LAST, 1)
                keep_y(LAST - 1, 0, half - 1)
                keep_act(LAST, 1)
                store_y(LAST - 1, 0)
                keep_y(LAST, 1, half - 1)
                store_y(LAST, 1)
                for u in range(2):
                    act.wait_ge(y_stored[u], 16 * (half + 1))

        clear(nc, sems)


def combine(nc, t):
    with ExitStack() as ctx:
        sems = []

        def sb(name, shape, dt=F32):
            return ctx.enter_context(nc.sbuf_tensor(name, shape, dt))

        def sem(name):
            sems.append(ctx.enter_context(nc.semaphore(name)))
            return sems[-1]

        x = sb("x1_again", [P, 2, D_MODEL])
        rows = sb("expert_rows", [P, 2, TOP_K, D_MODEL])
        idx = sb("slots_now", [P, 2, 2], I32)
        g_row = sb("g_final_row", [P, D_MODEL])
        square = sb("square3", [P, D_MODEL])
        out = sb("out_rows", [P, 2, D_MODEL])
        ss = sb("sum_squares3", [P, 2, 3])
        g_loaded = sem("g_final_loaded")
        x_loaded = [sem(f"x1_loaded{u}") for u in range(2)]
        rows_loaded = [sem(f"expert_rows_loaded{u}") for u in range(2)]
        stored = [sem(f"out_stored{u}") for u in range(2)]
        idx_done = Count(sem("slots_now_done"), 2)
        sums = Count(sem("expert_rows_added"), 4)
        squares = Count(sem("squares3_done"), 2)
        rstd_step = Count(sem("rstd3_step"), 2)
        rstd = Count(sem("rstd3_done"), 2)
        normed = Count(sem("out_done"), 2)

        with nc.Block() as block:

            @block.sync
            def _(sp):
                sp.dma_start(g_row[:, :], t.g_final.partition_broadcast(P)).then_inc(g_loaded, 16)
                for u in range(2):
                    sp.sem_inc(stored[u], 16)
                sp.dma_start(x[:, 0, :], row_tile(t.x1, 0)).then_inc(x_loaded[0], 16)

                def tile(it, u, final=False):
                    if not final:
                        sp.wait_ge(normed.sem, normed.after(it, u - 1))
                        sp.dma_start(x[:, 1 - u, :], row_tile(t.x1, it * 2 + u + 1)).then_inc(x_loaded[1 - u], 16)
                    sp.wait_ge(normed.sem, normed.after(it, u))
                    sp.dma_start(row_tile(t.y, it * 2 + u), out[:, u, :]).then_inc(stored[u], 16)

                with sp.Fori(0, PT // 2) as it:
                    for u in range(2):
                        tile(it, u)
                tile(PT // 2, 0, final=True)
                sp.wait_ge(stored[0], 16 * (2 + PT // 2))
                sp.wait_ge(stored[1], 16 * (1 + PT // 2))

            @block.gpsimd
            def _(pool):
                for c in (idx_done, rstd_step, rstd):
                    pool.sem_inc(c.sem, c.per)

                def gather(it, u):
                    pool.wait_ge(sums.sem, sums.after(it, 2 * (u - 2) + 1))
                    pool.tensor_copy(idx[:, u, :], t.slots[:, bass.ds((it * 2 + u) * 2, 2)]).then_inc(idx_done.sem, 1)
                    pool.wait_ge(idx_done.sem, idx_done.after(it, u))
                    own_wait(pool, t)
                    for k in range(TOP_K):
                        pool.indirect_dma_start(rows[:, u, k, :], None, t.moe_out[:, :],
                                                bass.IndirectOffsetOnAxis(ap=idx[:, u, k:k + 1], axis=0))\
                            .then_inc(rows_loaded[u], 16)

                def tile(it, u, final=False):
                    if not final:
                        gather(it + u, 1 - u)
                    pool.wait_ge(squares.sem, squares.after(it, u))
                    own_wait(pool, t)
                    pool.tensor_scalar(ss[:, u, 1:2], ss[:, u, 0:1], 1.0 / D_MODEL, NORM_EPS, ALU.mult, ALU.add)\
                        .then_inc(rstd_step.sem, 1)
                    pool.wait_ge(rstd_step.sem, rstd_step.after(it, u))
                    pool.wait_ge(normed.sem, normed.after(it, u - 2))
                    pool.tensor_tensor(ss[:, u, 2:3], ss[:, u, 1:2], t.neg_half[:, :], ALU.pow).then_inc(rstd.sem, 1)

                gather(0, 0)
                with pool.Fori(0, PT // 2) as it:
                    for u in range(2):
                        tile(it, u)
                tile(PT // 2, 0, final=True)

            @block.vector
            def _(dve):
                for c in (sums, normed):
                    dve.sem_inc(c.sem, c.per)
                dve.wait_ge(g_loaded, 16)

                def add(it, u):
                    dve.wait_ge(x_loaded[u], it * 16 + 16)
                    dve.wait_ge(rows_loaded[u], it * 32 + 32)
                    for k in range(TOP_K):
                        if k:
                            dve.wait_ge(sums.sem, sums.after(it, 2 * u + k - 1))
                        dve.scalar_tensor_tensor(x[:, u, :], rows[:, u, k, :], t.gates[:, k, bass.ds(it * 2 + u, 1)],
                                                 x[:, u, :], ALU.mult, ALU.add).then_inc(sums.sem, 1)

                def tile(it, u, final=False):
                    if not final:
                        add(it + u, 1 - u)
                    dve.wait_ge(rstd.sem, rstd.after(it, u))
                    dve.wait_ge(stored[u], it * 16 + 16)
                    dve.wait_ge(sums.sem, sums.after(it, 2 * u + 1))
                    dve.scalar_tensor_tensor(out[:, u, :], x[:, u, :], ss[:, u, 2:3], g_row[:, :], ALU.mult, ALU.mult)\
                       .then_inc(normed.sem, 1)

                add(0, 0)
                with dve.Fori(0, PT // 2) as it:
                    for u in range(2):
                        tile(it, u)
                tile(PT // 2, 0, final=True)

            @block.scalar
            def _(act):
                act.sem_inc(squares.sem, squares.per)

                def tile(it, u):
                    act.wait_ge(sums.sem, sums.after(it, 2 * u + 1))
                    act.wait_ge(squares.sem, squares.after(it, u - 1))
                    act.activation(square[:, :], x[:, u, :], ACT.Square, accum_out=ss[:, u, 0:1])\
                       .then_inc(squares.sem, 1)

                tile_loop(act, tile)

        clear(nc, sems)


def buckets_of(n):
    exact = N_BUCKETS // 2
    ratio = np.maximum(n, 1).astype(np.float32) / np.float32(exact)
    large = exact + (np.log(ratio) / np.float32(math.log(MAX_DISTANCE / exact)) * np.float32(N_BUCKETS - exact))\
        .astype(np.int32)
    return np.where(n < exact, n, np.minimum(large, N_BUCKETS - 1))


def host_constants():
    n = 2 * P - 1 - np.arange(DIST)
    table = np.zeros((N_BUCKETS + 2, DIST), np.float32)
    seen = n >= 0
    table[buckets_of(np.maximum(n, 0))[seen], np.arange(DIST)[seen]] += 1
    table[N_BUCKETS - 1, seen] -= 1
    table[N_BUCKETS, n < 0] = NEG
    table[N_BUCKETS + 1, n <= 0] = NEG
    mask_rows = np.zeros((2, H_DIFF + 1), np.float32)
    mask_rows[0, :H_DIFF] = 1
    mask_rows[1, H_DIFF] = 1
    half = np.arange(P) // DEC_SEQ % 2
    half_map = np.stack([1 - half, half], 1).astype(np.float32)
    e = N_EXPERTS
    rank = np.tile(np.arange(N_GROUPS, 0, -1, dtype=np.float32), (TILES, 1))
    limits = np.tile(P * np.arange(TILES, dtype=np.float32), (e, 1))
    tile_no = np.repeat(np.arange(MOE_TILES, dtype=np.float32)[:, None], e, 1)
    spare = np.zeros((P, TILES), np.float32)
    spare[N_SAMPLE:, PT] = N_SLOTS + np.arange(N_SAMPLE, P)
    before = np.triu(np.ones((P, P), np.float32), 1)
    token = (np.arange(TILES)[None] * P + np.arange(P)[:, None]).astype(np.float32)
    more = {"rank_const": rank, "limits_const": limits, "tile_no_const": tile_no, "spare_const": spare,
            "before_const": before, "token_const": token,
            "column_const": np.arange(P, dtype=np.float32)}
    return more | {"bucket_table": table, "mask_rows": mask_rows, "half_map": half_map, "eye": np.eye(P, dtype=np.float32)}


INPUTS = ["x", "cache_d", "cache_s", "page_table", "rel_bias", "g_mix", "w_in", "lambda_q1", "lambda_k1", "lambda_q2",
          "lambda_k2", "subln_g", "w_out", "g_ffn", "w_group", "b_group", "w_erouter", "b_erouter", "w_gate", "w_up",
          "w_down", "g_final", "eye", "bucket_table", "mask_rows", "half_map", "rank_const", "limits_const",
          "tile_no_const", "column_const", "spare_const", "before_const", "token_const"]
OUTPUTS = ["y", "new_kvd", "new_kvs"]


def step_kernel(nc, t):
    def scratch(name, shape, dt=F32):
        return nc.dram_tensor(name, shape, dt).ap()

    t.n_pool = t.cache_d.shape[0]
    t.qT = scratch("scratch_qT", (P, BLOCKS, ALL))
    t.kT = scratch("scratch_kT", (P, BLOCKS, ALL))
    t.oT = scratch("scratch_oT", (P, BLOCKS, ALL))
    t.bias_dram = scratch("scratch_bias", (H_DIFF + 1, P, DIST))
    t.near_dram = scratch("scratch_near", (H_DIFF, P, NEAR))
    t.x1 = scratch("scratch_x1", (ALL, D_MODEL))
    t.h2 = scratch("scratch_h2", (ALL, D_MODEL))
    t.moe_out = scratch("scratch_moe_out", (N_SLOTS + P, D_MODEL))
    with ExitStack() as ctx:
        constants(nc, ctx, t)
        project(nc, t)
        with ExitStack() as att:
            t.sample_o = att.enter_context(nc.sbuf_tensor("sample_o", [P, DEC_BATCH, P], F32))
            tables(nc, att, t)
            attention(nc, t, DIFF)
            attention(nc, t, STICK)
            sample_heads_out(nc, t)
        t.logits = ctx.enter_context(nc.sbuf_tensor("logits", [P, TILES, N_LOGITS], F32))
        t.gates = ctx.enter_context(nc.sbuf_tensor("gates", [P, TOP_K, TILES], F32))
        t.slots = ctx.enter_context(nc.sbuf_tensor("slots", [P, TOP_K * TILES], I32))
        t.slot_tok = ctx.enter_context(nc.sbuf_tensor("slot_tok", [P, MOE_TILES], I32))
        t.tile_expert = ctx.enter_context(nc.sbuf_tensor("tile_expert", [1, MOE_TILES], I32))
        mix_out(nc, t)
        route(nc, t)
        experts(nc, t)
        combine(nc, t)


def kernel(**inputs):
    import concourse.bacc as bacc
    from types import SimpleNamespace
    from concourse.bass_utils import run_bass_kernel_spmd

    a = {k: np.asarray(v) for k, v in inputs.items()}
    n_pool = a["cache_kv_diff"].shape[0]
    host = host_constants()
    host["x"] = np.concatenate([a["x_prompt"].reshape(SEQ, D_MODEL), a["x_sample"].reshape(N_SAMPLE, D_MODEL),
                                np.zeros((ALL - SEQ - N_SAMPLE, D_MODEL), a["x_prompt"].dtype)])
    host["cache_d"] = a["cache_kv_diff"].reshape(n_pool, PAGE, 2 * HALF_W)
    host["cache_s"] = a["cache_kv_sb"].reshape(n_pool, PAGE, 2 * HALF_W)
    host["w_erouter"] = a["w_erouter"][0].reshape(D_MODEL, N_EXPERTS)
    host["b_erouter"] = a["b_erouter"][0].reshape(N_EXPERTS)
    for name in ("w_gate", "w_up"):
        host[name] = a[name][0].reshape(N_EXPERTS, D_MODEL, D_EXPERT)
    host["w_down"] = a["w_down"][0].reshape(N_EXPERTS, D_EXPERT, D_MODEL)
    for name in ("page_table", "rel_bias", "g_final"):
        host[name] = a[name]
    for name in ("g_mix", "w_in", "lambda_q1", "lambda_k1", "lambda_q2", "lambda_k2", "subln_g", "w_out", "g_ffn",
                 "w_group", "b_group"):
        host[name] = a[name][0]

    nc = bacc.Bacc("TRN2", target_bir_lowering=False, num_devices=1)
    arrays, dram = {}, {}
    for name in INPUTS:
        arrays[f"in_{name}"] = np.ascontiguousarray(host[name])
        dram[name] = nc.dram_tensor(f"in_{name}", host[name].shape, mybir.dt.from_np(host[name].dtype),
                                    kind="ExternalInput").ap()
    for name in OUTPUTS:
        dram[name] = nc.dram_tensor(f"out_{name}", (ALL, D_MODEL), F32, kind="ExternalOutput").ap()
    step_kernel(nc, SimpleNamespace(**dram))
    r = run_bass_kernel_spmd(nc, [arrays], core_ids=[0]).results[0]

    def rows(name, *shape):
        out = r[f"out_{name}"]
        return out[0:SEQ].reshape(1, SEQ, *shape), out[SEQ:SEQ + N_SAMPLE].reshape(DEC_BATCH, DEC_SEQ, *shape)

    y_p, y_s = rows("y", D_MODEL)
    kvd_p, kvd_s = rows("new_kvd", 1, 2, H_DIFF, 2 * HEAD)
    kvs_p, kvs_s = rows("new_kvs", 1, 2, H_SB, HEAD)
    return y_p, y_s, kvd_p, kvs_p, kvd_s, kvs_s
```

```python
import math
from contextlib import ExitStack

import numpy as np
import concourse.bass as bass
from concourse import mybir
from concourse.alu_op_type import AluOpType as ALU

ACT = mybir.ActivationFunctionType
AX = mybir.AxisListType
F32 = mybir.dt.float32
I32 = mybir.dt.int32
F32R = mybir.dt.float32r

D_MODEL = 1024
SEQ = 1024
DEC_BATCH, DEC_SEQ = 8, 8
PAST_LEN, PAGE = 2048, 128
N_PAGES = PAST_LEN // PAGE
HEAD = 64
H_DIFF, H_SB = 4, 8
HALF_W = H_DIFF * 2 * HEAD
MIX_W = 2 * HALF_W
N_BUCKETS, MAX_DISTANCE = 32, 128
N_GROUPS, PER_GROUP = 4, 4
N_EXPERTS = N_GROUPS * PER_GROUP
TOP_K = 2
D_EXPERT = 256
NORM_EPS, SUBLN_EPS = 1e-6, 1e-5
LAMBDA_INIT = 0.8 - 0.6 * math.exp(-0.3 * 0)

P = 128
KC = D_MODEL // P
N_SAMPLE = DEC_BATCH * DEC_SEQ
PT = SEQ // P
TILES = PT + 1
BANK = 512
PROJ_G = 3 * MIX_W // BANK
BLOCKS = MIX_W // P
NEAR = 2 * P
DIST = 3 * P
NEG = -1e30
MOE_TILES = (TOP_K * (SEQ + N_SAMPLE) + N_EXPERTS * (P - 1)) // P


class Count:

    def __init__(self, sem, per):
        self.sem, self.per = sem, per

    def after(self, turn, k):
        assert -self.per <= k < self.per
        return turn * self.per + (self.per + k + 1)



def constants(nc, ctx, t):
    t.ident = ctx.enter_context(nc.sbuf_tensor("ident", [P, P], F32))
    t.ones = ctx.enter_context(nc.sbuf_tensor("ones", [P, P], F32))
    t.neg_half = ctx.enter_context(nc.sbuf_tensor("neg_half", [P, 1], F32))
    t.waits_passed = ctx.enter_context(nc.semaphore("waits_passed"))
    t.const_ready = ctx.enter_context(nc.semaphore("const_ready"))
    with nc.Block() as block:

        @block.sync
        def _(sp):
            sp.dma_start(t.ident[:, :], t.eye).then_inc(t.const_ready, 16)

        @block.gpsimd
        def _(pool):
            pool.memset(t.neg_half[:, :], -0.5)
            pool.memset(t.ones[:, :], 1.0)


def own_wait(engine, t):
    engine.sem_inc(t.waits_passed, 1)


def clear(nc, sems):
    with nc.Block() as block:

        @block.gpsimd
        def _(pool):
            for one in sems:
                pool.sem_clear(one)


def project(nc, t):
    with ExitStack() as ctx:
        sems = []

        def sb(name, shape, dt=F32):
            return ctx.enter_context(nc.sbuf_tensor(name, shape, dt))

        def ps(name, shape):
            return ctx.enter_context(nc.psum_tensor(name, shape, F32))

        def sem(name):
            sems.append(ctx.enter_context(nc.semaphore(name)))
            return sems[-1]

        ROLES = 3
        STEPS = ROLES * TILES
        TURNED = 2 * TILES
        assert STEPS % 3 == 0 and TURNED % 3 == 0 and TILES % 3 == 0

        x = sb("x_tiles", [P, TILES, D_MODEL])
        g_T = sb("g_mix_T", [P, KC])
        square = sb("square", [P, D_MODEL])
        ss = sb("sum_squares", [P, 4, TILES])
        hT = sb("x_times_g_T", [P, 2, 4, P])
        hT_hi = sb("h_T_hi", [P, TILES, KC, P], F32R)
        hT_lo = sb("h_T_lo", [P, TILES, KC, P], F32R)
        w_raw = sb("w_in_now", [P, KC, BANK])
        w_hi = sb("w_in_hi", [P, KC, BANK], F32R)
        w_lo = sb("w_in_lo", [P, KC, BANK], F32R)
        proj = sb("proj_rows", [P, 3, BANK])
        qkT = sb("qk_transposed", [P, 3, 4, P])
        xT_ps = ps("xT_ps", [P, 2, BANK])
        pj_ps = ps("proj_ps", [P, 3, BANK])
        tr_ps = ps("qkT_ps", [P, 3, BANK])

        x_loaded = [sem(f"x_loaded{n}") for n in range(TILES)]
        g_loaded = sem("g_mix_loaded")
        w_loaded = [sem(f"w_in_loaded{k}") for k in range(KC)]
        xT_done, hT_done, hi_done, lo_done = sem("xT_in_psum"), sem("hT_done"), sem("hT_hi_done"), sem("hT_lo_done")
        squares, rstd_step, rstd = sem("squares_done"), sem("rstd_step"), sem("rstd_done")
        w_hi_done = Count(sem("w_in_hi_done"), ROLES * KC)
        w_lo_done = Count(sem("w_in_lo_done"), ROLES * KC)
        w_used = Count(sem("w_in_used"), ROLES * (KC - 1))
        pj_done = Count(sem("proj_in_psum"), STEPS)
        pj_kept = Count(sem("proj_kept"), STEPS)
        tr_done = Count(sem("qkT_in_psum"), TURNED)
        tr_kept = Count(sem("qkT_kept"), TURNED)
        rows_stored = [sem(f"rows_stored{u}") for u in range(3)]
        qkT_stored = [sem(f"qkT_stored{u}") for u in range(3)]
        w_view = t.w_in.rearrange("(k p) n -> k p n", p=P)

        def load_w(sp, k, turn, role):
            sp.dma_start(w_raw[:, k, :], w_view[k, :, bass.ds(turn * (ROLES * BANK) + role * BANK, BANK)])\
              .then_inc(w_loaded[k], 16)

        def rows_free(turn, n):
            return turn * (16 * TURNED // 3) + 16 * (1 + len(range(TILES + n % 3, n, 3)))

        with nc.Block() as block:

            @block.sync
            def _(sp):
                for n in range(TILES):
                    sp.dma_start(x[:, n, :], t.x[n * P:(n + 1) * P, :]).then_inc(x_loaded[n], 16)
                    if n < KC:
                        sp.dma_start(w_raw[:, n, :], w_view[n, :, 0:BANK]).then_inc(w_loaded[n], 16)
                for u in range(3):
                    sp.sem_inc(rows_stored[u], 16)
                    sp.sem_inc(qkT_stored[u], 16)

                def next_w(it, role):
                    for k in range(KC):
                        sp.wait_ge(w_lo_done.sem, w_lo_done.after(it, role * KC + k))
                        own_wait(sp, t)
                        load_w(sp, k, it + (role + 1) // ROLES, (role + 1) % ROLES)

                def store(it, role, tile):
                    n = role * TILES + tile
                    if role > 0:
                        sp.wait_ge(pj_kept.sem, pj_kept.after(it, n))
                        own_wait(sp, t)
                        dst = (t.new_kvd, t.new_kvs)[it]
                        sp.dma_start(dst[tile * P:(tile + 1) * P, (role - 1) * HALF_W:role * HALF_W],
                                     proj[:, n % 3, :]).then_inc(rows_stored[n % 3], 16)
                    if role < 2:
                        sp.wait_ge(tr_kept.sem, tr_kept.after(it, n))
                        own_wait(sp, t)
                        dst = (t.qT, t.kT)[role]
                        sp.dma_start(dst[:, it * 4:it * 4 + 4, tile * P:(tile + 1) * P], qkT[:, n % 3, :, :])\
                          .then_inc(qkT_stored[n % 3], 16)

                for it in range(2):
                    for role in range(ROLES):
                        if it * ROLES + role + 1 < 2 * ROLES:
                            next_w(it, role)
                        for tile in range(TILES):
                            store(it, role, tile)
                for u in range(3):
                    sp.wait_ge(rows_stored[u], rows_free(2, 0))
                    sp.wait_ge(qkT_stored[u], 2 * (16 * TURNED // 3) + 16)

            @block.gpsimd
            def _(pool):
                pool.wait_ge(squares, TILES)
                pool.tensor_scalar(ss[:, 1, :], ss[:, 0, :], 1.0 / D_MODEL, NORM_EPS, ALU.mult, ALU.add)\
                    .then_inc(rstd_step, 1)
                for n in range(TILES):
                    if n == 0:
                        pool.wait_ge(rstd_step, 1)
                    pool.tensor_tensor(ss[:, 2, n:n + 1], ss[:, 1, n:n + 1], t.neg_half[:, :], ALU.pow)\
                        .then_inc(rstd_step, 1)
                pool.wait_ge(rstd_step, 1 + TILES)
                pool.tensor_scalar(ss[:, 3, :], ss[:, 2, :], HEAD ** -0.5, 0.0, ALU.mult, ALU.add).then_inc(rstd, 1)

            @block.tensor
            def _(pe):
                for c in (w_used, pj_done, tr_done):
                    pe.sem_inc(c.sem, c.per)
                pe.wait_ge(t.const_ready, 16)
                for n in range(TILES):
                    pe.wait_ge(x_loaded[n], 16)
                    for half in range(2):
                        m = 2 * n + half
                        if m >= 2:
                            pe.wait_ge(hT_done, m - 1)
                        for k in range(4):
                            last = pe.transpose(xT_ps[:, half, k * P:(k + 1) * P],
                                                x[:, n, (4 * half + k) * P:(4 * half + k + 1) * P], t.ident[:, :])
                        last.then_inc(xT_done, 1)

                def turn(it, n):
                    pe.wait_ge(pj_kept.sem, pj_kept.after(it, n))
                    pe.wait_ge(tr_kept.sem, tr_kept.after(it, n - 3))
                    for b in range(4):
                        last = pe.transpose(tr_ps[:, n % 3, b * P:(b + 1) * P], proj[:, n % 3, b * P:(b + 1) * P],
                                            t.ident[:, :])
                    last.then_inc(tr_done.sem, 1)

                def step(it, role, tile):
                    n = role * TILES + tile
                    pe.wait_ge(lo_done, 2 * tile + 2)
                    pe.wait_ge(pj_kept.sem, pj_kept.after(it, n - 3))
                    for k in range(KC):
                        if tile == 0:
                            pe.wait_ge(w_lo_done.sem, w_lo_done.after(it, role * KC + k))
                        for m, (a, b) in enumerate(((hT_hi, w_hi), (hT_lo, w_hi), (hT_hi, w_lo))):
                            last = pe.matmul(pj_ps[:, n % 3, :], a[:, tile, k, :], b[:, k, :],
                                             start=(k == 0 and m == 0), stop=(k == KC - 1 and m == 2))
                        if tile == TILES - 1 and k < KC - 1:
                            last.then_inc(w_used.sem, 1)
                    last.then_inc(pj_done.sem, 1)

                with pe.Fori(0, 2) as it:
                    for role in range(ROLES):
                        for tile in range(TILES):
                            step(it, role, tile)
                            if role < 2 and tile > 0:
                                turn(it, role * TILES + tile - 1)
                        if role < 2:
                            turn(it, role * TILES + TILES - 1)

            @block.vector
            def _(dve):
                for c in (w_lo_done, tr_kept):
                    dve.sem_inc(c.sem, c.per)
                dve.wait_ge(g_loaded, 16)

                def low(n, half):
                    m = 2 * n + half
                    dve.wait_ge(hi_done, m + 1)
                    at = slice(4 * half, 4 * half + 4)
                    dve.tensor_tensor(hT_lo[:, n, at, :], hT[:, half, :, :], hT_hi[:, n, at, :].bitcast(F32),
                                      ALU.subtract).then_inc(lo_done, 1)

                for n in range(TILES):
                    for half in range(2):
                        m = 2 * n + half
                        dve.wait_ge(xT_done, m + 1)
                        if m >= 2:
                            dve.wait_ge(lo_done, m - 1)
                        dve.tensor_tensor(hT[:, half, :, :], xT_ps[:, half, :].rearrange("p (k c) -> p k c", c=P),
                                          g_T[:, 4 * half:4 * half + 4].unsqueeze(2).broadcast_to([P, 4, P]), ALU.mult)\
                           .then_inc(hT_done, 1)
                        if m >= 1:
                            low((m - 1) // 2, (m - 1) % 2)
                low(TILES - 1, 1)

                with dve.Fori(0, 2) as it:
                    for role in range(ROLES):
                        for k in range(KC):
                            dve.wait_ge(w_hi_done.sem, w_hi_done.after(it, role * KC + k))
                            dve.tensor_tensor(w_lo[:, k, :], w_raw[:, k, :], w_hi[:, k, :].bitcast(F32), ALU.subtract)\
                               .then_inc(w_lo_done.sem, 1)
                        if role == 2:
                            continue
                        for tile in range(TILES):
                            n = role * TILES + tile
                            dve.wait_ge(tr_done.sem, tr_done.after(it, n))
                            dve.wait_ge(qkT_stored[n % 3], it * (16 * TURNED // 3) + 16 * (1 + n // 3))
                            dve.tensor_copy(qkT[:, n % 3, :, :], tr_ps[:, n % 3, :]).then_inc(tr_kept.sem, 1)

            @block.scalar
            def _(act):
                for c in (w_hi_done, pj_kept):
                    act.sem_inc(c.sem, c.per)
                with nc.allow_non_contiguous_dma(reason="one small vector"):
                    act.dma_start(g_T[:, :], t.g_mix.rearrange("(k p) -> p k", p=P)).then_inc(g_loaded, 16)
                for n in range(TILES):
                    for half in range(2):
                        m = 2 * n + half
                        act.wait_ge(hT_done, m + 1)
                        act.activation(hT_hi[:, n, 4 * half:4 * half + 4, :], hT[:, half, :, :], ACT.Copy)\
                           .then_inc(hi_done, 1)
                    if n:
                        act.wait_ge(squares, n)
                    act.activation(square[:, :], x[:, n, :], ACT.Square, accum_out=ss[:, 0, n:n + 1])\
                       .then_inc(squares, 1)

                with act.Fori(0, 2) as it:
                    for role in range(ROLES):
                        for k in range(KC):
                            act.wait_ge(w_loaded[k], it * (16 * ROLES) + 16 * (role + 1))
                            if k < KC - 1:
                                act.wait_ge(w_used.sem, w_used.after(it, (role - 1) * (KC - 1) + k))
                            else:
                                act.wait_ge(pj_done.sem, pj_done.after(it, role * TILES - 1))
                            act.activation(w_hi[:, k, :], w_raw[:, k, :], ACT.Copy).then_inc(w_hi_done.sem, 1)
                        if role == 0:
                            act.wait_ge(rstd, 1)
                        for tile in range(TILES):
                            n = role * TILES + tile
                            act.wait_ge(pj_done.sem, pj_done.after(it, n))
                            act.wait_ge(rows_stored[n % 3], rows_free(it, n))
                            if 3 <= n < TURNED + 3:
                                act.wait_ge(tr_done.sem, tr_done.after(it, n - 3))
                            act.activation(proj[:, n % 3, :], pj_ps[:, n % 3, :], ACT.Copy,
                                           scale=ss[:, 3 if role == 0 else 2, tile:tile + 1]).then_inc(pj_kept.sem, 1)

        clear(nc, sems)


def tables(nc, ctx, t):
    def keep(name, shape, dt=F32):
        return ctx.enter_context(nc.sbuf_tensor(name, shape, dt))

    t.q_heads = keep("sample_q_by_head", [P, DEC_BATCH, BLOCKS, 2, DEC_SEQ])
    t.near_dec = keep("near_bias_sample", [P, PAGE + DEC_SEQ])
    t.neg_lambda = keep("neg_lambda", [P, 1])
    t.row_factor = keep("row_factor", [P, 1])
    t.sub_g = keep("sub_g", [P, 1])
    t.pages = keep("page_ids", [1, DEC_BATCH * N_PAGES], I32)
    with ExitStack() as own:
        sems = []

        def sb(name, shape, dt=F32):
            return own.enter_context(nc.sbuf_tensor(name, shape, dt))

        def sem(name):
            sems.append(own.enter_context(nc.semaphore(name)))
            return sems[-1]

        rb = sb("rel_bias_rows", [N_BUCKETS + 2, H_DIFF + 1])
        buckets = sb("buckets", [N_BUCKETS + 2, DIST])
        rb_wide = sb("rel_bias_wide", [N_BUCKETS + 2, H_DIFF + 1, P])
        by_distance = sb("bias_by_distance", [P, H_DIFF + 1, DIST])
        lam_in = sb("lambda_in", [P, 4, HEAD])
        lam_mul = sb("lambda_products", [P, 2, HEAD])
        lam_sum = sb("lambda_sums", [P, 2])
        lam_exp = sb("lambda_exps", [P, 2])
        halves = sb("map_of_halves", [P, 2])
        g_in = sb("subln_in", [P, 1])
        q_in = sb("sample_qT", [P, BLOCKS, N_SAMPLE])
        bias_ps = own.enter_context(nc.psum_tensor("bias_ps", [P, H_DIFF + 1, BANK], F32))
        zeroed, rb_loaded, lam_loaded, q_loaded = sem("zeroed"), sem("rb_loaded"), sem("lam_loaded"), sem("q_loaded")
        bias_done, bias_kept, bias_stored = sem("bias_done"), sem("bias_kept"), sem("bias_stored")
        near_loaded, pages_loaded = sem("near_loaded"), sem("pages_loaded")
        widened = sem("rel_bias_widened")
        step, exps = sem("lambda_step"), sem("lambda_exps_done")

        with nc.Block() as block:

            @block.sync
            def _(sp):
                sp.dma_start(buckets[:, :], t.bucket_table).then_inc(rb_loaded, 16)
                sp.dma_start(rb[N_BUCKETS:N_BUCKETS + 2, :], t.mask_rows).then_inc(rb_loaded, 16)
                sp.wait_ge(zeroed, 1)
                sp.dma_start(rb[0:N_BUCKETS, 0:H_DIFF], t.rel_bias).then_inc(rb_loaded, 16)
                for n, v in enumerate((t.lambda_q1, t.lambda_k1, t.lambda_q2, t.lambda_k2)):
                    sp.dma_start(lam_in[:, n, :], v.partition_broadcast(P)).then_inc(lam_loaded, 16)
                sp.dma_start(g_in[:, :], t.subln_g.rearrange("(p a) -> p a", a=1)).then_inc(lam_loaded, 16)
                sp.dma_start(halves[:, :], t.half_map).then_inc(lam_loaded, 16)
                sp.dma_start(q_in[:, :, :], t.qT[:, :, SEQ:SEQ + N_SAMPLE]).then_inc(q_loaded, 16)
                sp.dma_start(t.pages[:, :], t.page_table.rearrange("(a s) n -> a (s n)", a=1))\
                  .then_inc(pages_loaded, 16)
                sp.wait_ge(bias_kept, 1)
                sp.dma_start(t.bias_dram.rearrange("h p n -> p h n"), by_distance[:, :, :]).then_inc(bias_stored, 16)
                sp.wait_ge(bias_stored, 16)
                for b in range(BLOCKS):
                    for u in range(2):
                        row = 2 * DEC_SEQ * b + DEC_SEQ * u
                        sp.dma_start(t.near_dec[row:row + DEC_SEQ, :],
                                     distances(t, min(b, H_DIFF), DEC_SEQ, PAGE + DEC_SEQ)).then_inc(near_loaded, 16)
                sp.wait_ge(near_loaded, 16 * 2 * BLOCKS)
                for head in range(H_DIFF):
                    sp.dma_start(t.near_dram[head], distances(t, head, P, NEAR)).then_inc(bias_stored, 16)
                sp.wait_ge(bias_stored, 16 * (1 + H_DIFF))
                sp.wait_ge(pages_loaded, 16)

            @block.tensor
            def _(pe):
                pe.wait_ge(rb_loaded, 48)
                pe.wait_ge(widened, 1)
                for head in range(H_DIFF + 1):
                    last = pe.matmul(bias_ps[:, head, 0:DIST], rb_wide[:, head, :], buckets[:, :], start=True, stop=True)
                last.then_inc(bias_done, 1)

            @block.vector
            def _(dve):
                dve.memset(rb[0:N_BUCKETS, :], 0.0).then_inc(zeroed, 1)
                dve.memset(t.q_heads[:, :, :, :, :], 0.0).then_inc(zeroed, 1)
                dve.wait_ge(rb_loaded, 48)
                dve.tensor_copy(rb_wide[:, :, :], rb[:, :].unsqueeze(2).broadcast_to([N_BUCKETS + 2, H_DIFF + 1, P]))\
                   .then_inc(widened, 1)
                dve.wait_ge(bias_done, 1)
                dve.tensor_copy(by_distance[:, :, :], bias_ps[:, :, 0:DIST]).then_inc(bias_kept, 1)
                dve.wait_ge(q_loaded, 16)
                dve.wait_ge(zeroed, 2)
                for u in range(2):
                    rows = slice(HEAD * u, HEAD * u + HEAD)
                    for s in range(DEC_BATCH):
                        dve.tensor_copy(t.q_heads[rows, s, :, u, :], q_in[rows, :, DEC_SEQ * s:DEC_SEQ * (s + 1)])
                dve.wait_ge(lam_loaded, 96)
                dve.tensor_tensor(lam_mul[:, 0, :], lam_in[:, 0, :], lam_in[:, 1, :], ALU.mult).then_inc(step, 1)
                dve.tensor_tensor(lam_mul[:, 1, :], lam_in[:, 2, :], lam_in[:, 3, :], ALU.mult).then_inc(step, 1)
                dve.wait_ge(step, 2)
                dve.tensor_reduce(lam_sum[:, :], lam_mul[:, :, :], axis=AX.X, op=ALU.add).then_inc(step, 1)
                dve.wait_ge(exps, 1)
                dve.tensor_tensor(t.neg_lambda[:, :], lam_exp[:, 1:2], lam_exp[:, 0:1], ALU.subtract)\
                   .then_inc(step, 1)
                dve.wait_ge(step, 4)
                dve.tensor_scalar_add(t.neg_lambda[:, :], t.neg_lambda[:, :], -LAMBDA_INIT).then_inc(step, 1)
                dve.wait_ge(step, 5)
                dve.scalar_tensor_tensor(t.row_factor[:, :], halves[:, 1:2], t.neg_lambda[:, 0:1], halves[:, 0:1],
                                         ALU.mult, ALU.add)
                dve.tensor_scalar_mul(t.sub_g[:, :], g_in[:, :], 1.0 - LAMBDA_INIT)

            @block.scalar
            def _(act):
                act.wait_ge(step, 3)
                act.activation(lam_exp[:, :], lam_sum[:, :], ACT.Exp).then_inc(exps, 1)

        clear(nc, sems)


def distances(t, head, rows, cols):
    return bass.AP(t.bias_dram.tensor, head * P * DIST + P - 1, [[DIST - 1, rows], [1, cols]])


DIFF, STICK = 0, 1
TURNS = 4
K_SLOTS = 4
N_WEIGH = 7
SPANS = {DIFF: ((0.07, 0.4), (0.4, 0.5), (0.55, 1.0)), STICK: ((0.0, 0.295), (0.4, 0.49), (0.55, 1.05))}
WEIGHTS = {DIFF: (1, 1, 1, 2, 1), STICK: (1, 2, 1, 2, 3)}
D_PAGES = N_PAGES + 1
KEYS = PAST_LEN + DEC_SEQ
V_GROUPS = (D_PAGES + 3) // 4
NEW = N_PAGES
S_GROUPS = N_PAGES // 2
S_KEYS = 2 * PAGE + DEC_SEQ
D0 = H_DIFF * 2 * DEC_SEQ


def page_keys(p):
    return PAGE if p < N_PAGES else DEC_SEQ


def group_pages(g):
    return range(4 * g, min(4 * g + 4, D_PAGES))


def score_chunks(kind):
    near = 2 if kind == DIFF else 1
    out = []
    for i in range(PT):
        end, near0 = (i + 1) * P, max(0, (i + 1 - near)) * P
        for u in range(2):
            for k0 in range(0, end, BANK):
                k1 = min(k0 + BANK, end)
                out.append((i, u, k0, k1, min(max(near0, k0), k1)))
    return out


def turned_groups(kind, i):
    blocks = [(u, kb) for u in range(1 if kind == DIFF else 2) for kb in range(i + 1)]
    return [blocks[n:n + 4] for n in range(0, len(blocks), 4)]


def score_group_pages(g):
    return range(2 * g, 2 * g + 2) if g + 1 < S_GROUPS else range(2 * g, D_PAGES)


def attention_plan(kind):
    w_score, w_soft, w_out, w_last, ahead = WEIGHTS[kind]
    n_soft = 3 if kind == DIFF else 6
    chunks = score_chunks(kind)

    def scores(i):
        return [(("score", i, g), w_score) for g, c in enumerate(chunks) if c[0] == i]

    prompt = scores(0) + [(("soft", 0, n), w_soft) for n in range(n_soft)]
    for i in range(PT):
        soft = [(("soft", i + 1, n), w_soft) for n in range(n_soft)] if i + 1 < PT else []
        if i + 1 < PT:
            prompt += scores(i + 1)
        n_out = len(turned_groups(kind, i)) + 1
        outs = [(("out", i, n), w_out) for n in range(n_out - 1)]
        if i:
            outs.append((("turn_out", i - 1), 1))
        outs.append((("out", i, n_out - 1), w_last))
        prompt += soft[:ahead] + outs + soft[ahead:]
    prompt.append((("turn_out", PT - 1), 1))
    pages = []
    for p in range(D_PAGES):
        pages.append((("page", p), 1))
        if p >= 2 and p % 2 == 0 and p < N_PAGES:
            pages += [(("page_scores", p // 2 - 1, part), 2) for part in range(2)]
    pages += [(("page_scores", S_GROUPS - 1, part), 2) for part in range(2)]
    weigh = [(("weigh", n), 1) for n in range(N_WEIGH)]
    use = [(("turn", 0), 1)]
    for g in range(1, V_GROUPS):
        use += [(("turn", g), 1)] + [(("apply", 0, p), 2) for p in group_pages(g - 1)]
    use += [(("apply", 0, p), 2) for p in group_pages(V_GROUPS - 1)] + [(("rows", 0), 0)]
    use += [(("apply", 1, p), 2) for p in range(D_PAGES)] + [(("rows", 1), 0), (("heads", 0), 1)]
    total = sum(w for _, w in prompt)
    timed = []
    for steps, (begin, end) in zip((pages, weigh, use), SPANS[kind]):
        of, done = sum(w for _, w in steps), 0
        for step, w in steps:
            timed.append((begin + (end - begin) * done / of, step))
            done += w
    out, done, taken = [], 0, 0
    for step, w in prompt:
        while taken < len(timed) and timed[taken][0] <= done / total:
            out.append(timed[taken][1])
            taken += 1
        out.append(step)
        done += w
    return out + [step for _, step in timed[taken:]]


def attention(nc, t, kind):
    with ExitStack() as ctx:
        sems = []

        def sb(name, shape, dt=F32):
            return ctx.enter_context(nc.sbuf_tensor(f"{name}_{kind}", shape, dt))

        def ps(name, shape):
            return ctx.enter_context(nc.psum_tensor(f"{name}_{kind}", shape, F32))

        def sem(name):
            sems.append(ctx.enter_context(nc.semaphore(f"{name}_{kind}")))
            return sems[-1]

        def count(name, per):
            return Count(sem(name), per)

        qT = sb("head_qT_halves", [P, 2, SEQ])
        kT = sb("head_kT", [P, SEQ])
        v = sb("head_v", [P, PT, P])
        near = sb("near_bias", [P, NEAR])
        S = sb("scores", [P, 2, 2, SEQ])
        aux = sb("aux", [P, 2, SEQ])
        wT = sb("weights_T", [P, 16, P])
        stat = sb("stats", [P, 4, 8])
        o_rows = sb("o_rows", [P, 2, P])
        o_sq = sb("o_squares", [P, P])
        o_norm = sb("o_normed", [P, P])
        oT = sb("head_oT", [P, SEQ])
        sc_ps = ps("scores_ps", [P, 2, BANK])
        wT_ps = ps("weights_T_ps", [P, 4, P])
        o_ps = ps("o_ps", [P, BANK])
        k_page = sb("k_pages", [P, K_SLOTS, BLOCKS, P])
        v_page = sb("v_pages", [P, D_PAGES, BLOCKS, P])
        kT_page = sb("k_pages_T", [P, 2, BLOCKS, S_KEYS])
        q_block = sb("q_by_block", [P, BLOCKS * (P + 16)])
        sS = sb("sample_scores", [P, KEYS])
        sW = sb("sample_weights", [P, KEYS])
        o_rows_s = sb("sample_o_rows", [P, BANK])
        sT = sb("sample_weights_T", [P, D_PAGES, P])
        sstat = sb("sample_stats", [P, 4])
        kT_ps = ps("k_page_T_ps", [P, 2, 4, P])
        s_ps = ps("page_scores_ps", [P, BANK])
        sO_ps = ps("sample_o_ps", [P, BANK])

        chunks = score_chunks(kind)
        n_chunks = len(chunks)
        assert n_chunks % 2 == 0
        far_upto = np.cumsum([c[4] > c[2] for c in chunks]).tolist()
        near_upto = np.cumsum([c[3] > c[4] for c in chunks]).tolist()
        n_groups = [len(turned_groups(kind, i)) for i in range(PT)]
        groups_upto = np.cumsum(n_groups).tolist()
        plan = attention_plan(kind)

        qk_loaded, v_loaded, near_loaded = sem("qk_loaded"), sem("v_loaded"), sem("near_loaded")
        sc_done = count("scores_in_psum", n_chunks)
        sc_far = count("far_scores_kept", far_upto[-1])
        sc_near = count("near_scores_kept", near_upto[-1])
        row_max = count("row_max", PT)
        exps = count("exps_done", 2 * PT)
        inv_sum = count("inverse_sums", 2 * PT)
        mixed = count("softmaxes_mixed", PT)
        s_abs = count("abs_done", PT)
        s_expm = count("exp_minus_abs", PT)
        s_ln = count("ln_done", PT)
        s_soft = count("softplus_done", PT)
        s_scan = count("suffix_sums_done", 2 * PT)
        s_sub = count("log_weights_done", PT)
        s_exp = count("stick_weights_done", PT)
        w_turned = count("weights_T_in_psum", groups_upto[-1])
        wT_kept = count("weights_T_kept", groups_upto[-1])
        o_done = count("o_in_psum", PT)
        o_kept = count("o_kept", PT)
        o_squared = count("o_squared", PT)
        sub_step = count("sub_norm_step", PT)
        sub_rstd = count("sub_norm_rstd", PT)
        o_normed = count("o_normed_done", PT)
        oT_done = count("oT_in_psum", PT)
        oT_kept = count("oT_kept", PT)
        oT_stored = sem("oT_stored")
        k_loaded = [sem(f"k_page_loaded{n}") for n in range(K_SLOTS)]
        vp_loaded = [sem(f"v_pages_loaded{g}") for g in range(V_GROUPS)]
        kT_done = count("kT_in_psum", 2 * D_PAGES + V_GROUPS)
        kT_kept = [count("kT_bank0_kept", D_PAGES + (V_GROUPS + 1) // 2), count("kT_bank1_kept", D_PAGES + V_GROUPS // 2)]
        zeroed = sem("zeros_written")
        q_spread = count("q_by_block_done", 1)
        ps_done = count("page_scores_in_psum", S_GROUPS)
        sfar = count("sample_far_kept", S_GROUPS)
        snear = count("sample_near_kept", 1)
        smax = count("sample_max", 1)
        sexp = count("sample_exp", 1)
        sabs = count("sample_abs", 1)
        sexpm = count("sample_exp_minus_abs", 1)
        sln = count("sample_ln", 1)
        ssoft = count("sample_softplus", 1)
        sscan = count("sample_suffix_sums", 1)
        ssub = count("sample_log_weights", 1)
        sstick = count("sample_stick_weights", 1)
        sinv = count("sample_inverse_sums", 2)
        applied = [count("diff_groups_applied", V_GROUPS), count("stick_groups_applied", V_GROUPS)]
        rows_kept = [count("sample_diff_rows_kept", 1), count("sample_stick_rows_kept", 1)]
        heads_done = count("sample_heads_in_psum", 1)
        so_kept = count("sample_o_kept", 1)

        def page_slot(p):
            s = p % K_SLOTS
            return s, p // K_SLOTS, len(range(s, D_PAGES, K_SLOTS))

        kv = t.new_kvd if kind == DIFF else t.new_kvs

        with nc.Block() as block:

            @block.sync
            def _(sp):
                def head_block(b):
                    return t.qT[:, bass.ds(b + TURNS * kind, 1), 0:SEQ], t.kT[:, bass.ds(b + TURNS * kind, 1), 0:SEQ]

                def load_page(it, p, dst, half, signal, free):
                    if p < N_PAGES:
                        page = sp.value_load(t.pages[0:1, bass.ds((it + TURNS * kind) * N_PAGES + p, 1)],
                                             min_val=0, max_val=t.n_pool - 1)
                        src = [c[bass.ds(page, 1), :, half * HALF_W:(half + 1) * HALF_W]
                               .rearrange("a k n -> (a k) n") for c in (t.cache_d, t.cache_s)]
                    else:
                        first = SEQ + (it + TURNS * kind) * DEC_SEQ
                        src = [c[bass.ds(first, DEC_SEQ), half * HALF_W:(half + 1) * HALF_W]
                               for c in (t.new_kvd, t.new_kvs)]
                    n = page_keys(p)
                    sp.wait_ge(*free)
                    for j in range(2):
                        sp.dma_start(dst[0:n, 4 * j:4 * j + 4, :], src[j]).then_inc(signal, 16)

                def load_k(it, p):
                    s, _, _ = page_slot(p)
                    prior = p - K_SLOTS if p >= K_SLOTS else max(range(s, D_PAGES, K_SLOTS)) - D_PAGES
                    item = 2 * prior + 1 if prior >= 0 else 2 * prior + 1 - V_GROUPS
                    load_page(it, p, k_page[:, s, :, :], 0, k_loaded[s], (kT_done.sem, kT_done.after(it, item)))

                def load_v(it, p):
                    load_page(it, p, v_page[:, p, :, :], 1, vp_loaded[p // 4],
                              (applied[1].sem, applied[1].after(it, p // 4 - V_GROUPS)))

                if kind == STICK:
                    sp.dma_start(near[:, :], distances(t, H_DIFF, P, NEAR)).then_inc(near_loaded, 16)
                with sp.Fori(0, TURNS) as it:
                    for p in range(K_SLOTS):
                        load_k(it, p)
                    if kind == DIFF:
                        sp.wait_ge(sc_near.sem, sc_near.after(it, -1))
                        sp.dma_start(near[:, :], t.near_dram[bass.ds(it, 1), :, :].rearrange("a p n -> (a p) n"))\
                          .then_inc(near_loaded, 16)
                    sp.wait_ge(sc_done.sem, sc_done.after(it, -1))
                    q_src, k_src = [a.rearrange("p a n -> p (a n)") for a in head_block(it)]
                    for u in range(2):
                        rows = slice(HEAD * u, HEAD * u + HEAD)
                        sp.dma_start(qT[rows, u, :], q_src[rows, :]).then_inc(qk_loaded, 16)
                    sp.dma_start(kT[:, :], k_src).then_inc(qk_loaded, 16)
                    sp.wait_ge(o_done.sem, o_done.after(it, -1))
                    sp.dma_start(v[:, :, :], kv[0:SEQ, bass.ds(it * P + HALF_W, P)].rearrange("(t p) n -> p t n", p=P))\
                      .then_inc(v_loaded, 16)
                    for p in range(N_PAGES):
                        load_v(it, p)
                        if p + K_SLOTS < D_PAGES:
                            load_k(it, p + K_SLOTS)
                    load_v(it, NEW)

            @block.gpsimd
            def _(pool):
                pool.sem_inc(sub_step.sem, sub_step.per)
                pool.sem_inc(sub_rstd.sem, sub_rstd.per)

                def rstd(it, i):
                    pool.wait_ge(o_squared.sem, o_squared.after(it, i))
                    own_wait(pool, t)
                    pool.tensor_scalar(stat[:, i % 4, 6:7], stat[:, i % 4, 5:6], 1.0 / P, SUBLN_EPS,
                                       ALU.mult, ALU.add).then_inc(sub_step.sem, 1)
                    pool.wait_ge(sub_step.sem, sub_step.after(it, i))
                    pool.tensor_tensor(stat[:, i % 4, 7:8], stat[:, i % 4, 6:7], t.neg_half[:, :], ALU.pow)\
                        .then_inc(sub_rstd.sem, 1)

                if kind == DIFF:
                    with pool.Fori(0, TURNS) as it:
                        for i in range(PT):
                            rstd(it, i)

            @block.tensor
            def _(pe):
                for c in (sc_done, w_turned, o_done, oT_done, kT_done, ps_done, *applied, heads_done):
                    pe.sem_inc(c.sem, c.per)

                def score(it, i, chunk):
                    if chunk == 0:
                        pe.wait_ge(qk_loaded, it * 48 + 48)
                    for g, (ci, u, k0, k1, kn) in enumerate(chunks):
                        if g != chunk:
                            continue
                        if g >= 2:
                            pe.wait_ge(sc_far.sem, sc_far.after(it, far_upto[g - 2] - 1))
                            pe.wait_ge(sc_near.sem, sc_near.after(it, near_upto[g - 2] - 1))
                        else:
                            pe.wait_ge(sc_far.sem, sc_far.after(it, -1))
                            pe.wait_ge(sc_near.sem, sc_near.after(it, -1))
                        pe.matmul(sc_ps[:, g % 2, 0:k1 - k0], qT[:, u, i * P:(i + 1) * P], kT[:, k0:k1],
                                  start=True, stop=True).then_inc(sc_done.sem, 1)

                def out(it, i, n):
                    groups = turned_groups(kind, i)
                    first = groups_upto[i] - n_groups[i]
                    if n < len(groups):
                        if n == 0:
                            if kind == DIFF:
                                pe.wait_ge(mixed.sem, mixed.after(it, i))
                            else:
                                pe.wait_ge(s_exp.sem, s_exp.after(it, i))
                        pe.wait_ge(wT_kept.sem, wT_kept.after(it, first + n - 1))
                        for m, (u, kb) in enumerate(groups[n]):
                            src = aux[:, 0, kb * P:(kb + 1) * P] if kind == DIFF else S[:, i % 2, u, kb * P:(kb + 1) * P]
                            last = pe.transpose(wT_ps[:, m, :], src, t.ident[:, :])
                        last.then_inc(w_turned.sem, 1)
                        return
                    pe.wait_ge(wT_kept.sem, wT_kept.after(it, groups_upto[i] - 1))
                    pe.wait_ge(oT_kept.sem, oT_kept.after(it, i - 1))
                    if i == 0:
                        pe.wait_ge(v_loaded, it * 16 + 16)
                    for m, (u, kb) in enumerate([x for g in groups for x in g]):
                        cols = slice(0, P) if kind == DIFF else slice(HEAD * u, HEAD * u + HEAD)
                        last = pe.matmul(o_ps[:, cols], wT[:, m, :], v[:, kb, cols], start=(kb == 0), stop=(kb == i))
                    last.then_inc(o_done.sem, 1)

                def turn_out(it, i):
                    ready = o_normed if kind == DIFF else o_kept
                    pe.wait_ge(ready.sem, ready.after(it, i))
                    pe.wait_ge(oT_kept.sem, oT_kept.after(it, i - 1))
                    pe.transpose(o_ps[:, P:2 * P], o_norm[:, :], t.ident[:, :]).then_inc(oT_done.sem, 1)

                def page(it, p):
                    s, before, loads = page_slot(p)
                    n = page_keys(p)
                    pe.wait_ge(k_loaded[s], it * (32 * loads) + 32 * (before + 1))
                    for half in range(2):
                        pe.wait_ge(kT_kept[half].sem, kT_kept[half].after(it, p - 1))
                        own_wait(pe, t)
                        for b in range(4):
                            last = pe.transpose(kT_ps[:, half, b, 0:n], k_page[0:n, s, 4 * half + b, :],
                                                t.ident[0:n, 0:n])
                        last.then_inc(kT_done.sem, 1)

                def page_scores(it, g, part):
                    if g == 0 and part == 0:
                        pe.wait_ge(q_spread.sem, q_spread.after(it, 0))
                    for half in range(2):
                        pe.wait_ge(kT_kept[half].sem, kT_kept[half].after(it, score_group_pages(g)[-1]))
                    pe.wait_ge(sfar.sem, sfar.after(it, g - 1))
                    if g == 0:
                        pe.wait_ge(snear.sem, snear.after(it, -1))
                    n = sum(page_keys(p) for p in score_group_pages(g))
                    for b in range(4 * part, 4 * part + 4):
                        last = pe.matmul(s_ps[:, 0:n], q_block[:, b * P:(b + 1) * P], kT_page[:, g % 2, b, 0:n],
                                         start=(b == 0), stop=(b == BLOCKS - 1))
                    if part == 1:
                        last.then_inc(ps_done.sem, 1)

                def turn(it, g):
                    if g == 0:
                        pe.wait_ge(sstick.sem, sstick.after(it, 0))
                        pe.wait_ge(sexp.sem, sexp.after(it, 0))
                    pe.wait_ge(kT_kept[g % 2].sem, kT_kept[g % 2].after(it, D_PAGES - 1 + g // 2))
                    for m, p in enumerate(group_pages(g)):
                        n = page_keys(p)
                        last = pe.transpose(kT_ps[0:n, g % 2, m, :], sW[:, p * PAGE:p * PAGE + n], t.ident[:, :])
                    last.then_inc(kT_done.sem, 1)

                def apply(it, kind_half, p):
                    g, n = p // 4, page_keys(p)
                    if kind_half == 0 and p == 4 * g:
                        pe.wait_ge(kT_kept[g % 2].sem, kT_kept[g % 2].after(it, D_PAGES + g // 2))
                        pe.wait_ge(vp_loaded[g], (it + 1) * (32 * len(group_pages(g))))
                        if g == 0:
                            pe.wait_ge(so_kept.sem, so_kept.after(it, -1))
                    elif kind_half == 1 and p == 0:
                        pe.wait_ge(rows_kept[0].sem, rows_kept[0].after(it, 0))
                    own_wait(pe, t)
                    last = pe.matmul(sO_ps[:, :], sT[0:n, p, :], v_page[0:n, p, 4 * kind_half:4 * kind_half + 4, :],
                                     start=(p == 0), stop=(p == NEW))
                    if p == group_pages(g)[-1]:
                        last.then_inc(applied[kind_half].sem, 1)

                def heads(it, _):
                    pe.wait_ge(rows_kept[1].sem, rows_kept[1].after(it, 0))
                    for b in range(4):
                        cols = slice(16 * b, 16 * b + 16)
                        last = pe.matmul(sO_ps[:, 0:P].rearrange("p (u c) -> p u c", u=2)[:, :, cols],
                                         o_rows_s[:, b * P:(b + 1) * P],
                                         t.ident[:, :].rearrange("p (u c) -> p u c", u=2)[:, :, cols],
                                         start=True, stop=True)
                    last.then_inc(heads_done.sem, 1)

                steps = dict(score=score, out=out, turn_out=turn_out, page=page, page_scores=page_scores,
                             turn=turn, apply=apply, heads=heads)
                pe.wait_ge(zeroed, 3)
                with pe.Fori(0, TURNS) as it:
                    for name, *args in plan:
                        if name in steps:
                            steps[name](it, *args)

            @block.vector
            def _(dve):
                for c in (sc_near, row_max, inv_sum, mixed, s_soft, s_scan, s_sub, o_normed, oT_kept, kT_kept[1],
                          q_spread, snear, smax, ssoft, sscan, ssub, sinv, *rows_kept, so_kept):
                    dve.sem_inc(c.sem, c.per)
                if kind == STICK:
                    for c in (wT_kept,):
                        dve.sem_inc(c.sem, c.per)

                def score(it, i, chunk):
                    if chunk == 0:
                        dve.wait_ge(near_loaded, it * 16 + 16 if kind == DIFF else 16)
                    for g, (ci, u, k0, k1, kn) in enumerate(chunks):
                        if g != chunk or kn >= k1:
                            continue
                        dve.wait_ge(sc_done.sem, sc_done.after(it, g))
                        if kn > k0:
                            dve.wait_ge(sc_far.sem, sc_far.after(it, far_upto[g] - 1))
                        dve.wait_ge(w_turned.sem, w_turned.after(it, groups_upto[i - 2] - 1 if i >= 2 else
                                                                 groups_upto[PT - 2 + i] - 1 - groups_upto[-1]))
                        col = kn - (i - 1) * P
                        dve.tensor_tensor(S[:, i % 2, u, kn:k1], sc_ps[:, g % 2, kn - k0:k1 - k0],
                                          near[:, col:col + k1 - kn], ALU.add).then_inc(sc_near.sem, 1)

                def soft_diff(it, i, n):
                    end = (i + 1) * P
                    last_chunk = max(g for g, c in enumerate(chunks) if c[0] == i)
                    x = stat[:, i % 4, :]
                    if n == 0:
                        dve.wait_ge(sc_far.sem, sc_far.after(it, far_upto[last_chunk] - 1))
                        dve.wait_ge(sc_near.sem, sc_near.after(it, near_upto[last_chunk] - 1))
                        dve.wait_ge(o_normed.sem, o_normed.after(it, i - 4))
                        dve.tensor_reduce(x[:, 0:2], S[:, i % 2, :, 0:end], axis=AX.X, op=ALU.max, negate=True)\
                           .then_inc(row_max.sem, 1)
                    elif n == 2:
                        dve.wait_ge(exps.sem, exps.after(it, 2 * i + 1))
                        dve.reciprocal(x[:, 4:6], x[:, 2:4]).then_inc(inv_sum.sem, 1)
                        dve.wait_ge(inv_sum.sem, inv_sum.after(it, 2 * i))
                        dve.scalar_tensor_tensor(x[:, 1:2], x[:, 5:6], t.neg_lambda[:, 0:1], x[:, 2:3],
                                                 ALU.mult, ALU.mult).then_inc(inv_sum.sem, 1)
                        dve.wait_ge(inv_sum.sem, inv_sum.after(it, 2 * i + 1))
                        dve.wait_ge(w_turned.sem, w_turned.after(it, groups_upto[i - 1] - 1 if i else -1))
                        dve.scalar_tensor_tensor(aux[:, 0, 0:end], S[:, i % 2, 1, 0:end], x[:, 1:2],
                                                 S[:, i % 2, 0, 0:end], ALU.mult, ALU.add).then_inc(mixed.sem, 1)

                def soft_stick(it, i, n):
                    end = (i + 1) * P
                    if n == 3:
                        dve.wait_ge(s_ln.sem, s_ln.after(it, i))
                        dve.scalar_tensor_tensor(aux[:, :, 0:end], S[:, i % 2, :, 0:end], 0.0, aux[:, :, 0:end],
                                                 ALU.max, ALU.add).then_inc(s_soft.sem, 1)
                    elif n == 4:
                        dve.wait_ge(s_soft.sem, s_soft.after(it, i))
                        for u in range(2):
                            dve.tensor_tensor_scan(aux[:, u, 0:end][:, ::-1], aux[:, u, 0:end][:, ::-1],
                                                   aux[:, u, 0:end][:, ::-1], 0.0, ALU.add, ALU.bypass)\
                               .then_inc(s_scan.sem, 1)
                        dve.wait_ge(s_scan.sem, s_scan.after(it, 2 * i + 1))
                        dve.tensor_tensor(S[:, i % 2, :, 0:end], S[:, i % 2, :, 0:end], aux[:, :, 0:end],
                                          ALU.subtract).then_inc(s_sub.sem, 1)

                def out(it, i, n):
                    groups = turned_groups(kind, i)
                    first = groups_upto[i] - n_groups[i]
                    if kind == STICK and n < len(groups):
                        dve.wait_ge(w_turned.sem, w_turned.after(it, first + n))
                        dve.wait_ge(o_done.sem, o_done.after(it, i - 1))
                        m = len(groups[n])
                        dve.tensor_copy(wT[:, 4 * n:4 * n + m, :], wT_ps[:, 0:m, :]).then_inc(wT_kept.sem, 1)

                def turn_out(it, i):
                    if kind == DIFF:
                        dve.wait_ge(sub_rstd.sem, sub_rstd.after(it, i))
                        dve.wait_ge(oT_done.sem, oT_done.after(it, i - 1))
                        dve.tensor_scalar_mul(o_norm[:, :], o_rows[:, i % 2, :], stat[:, i % 4, 7:8])\
                           .then_inc(o_normed.sem, 1)
                    dve.wait_ge(oT_done.sem, oT_done.after(it, i))
                    if i == 0:
                        dve.wait_ge(oT_stored, it * 16 + 16)
                    if kind == DIFF:
                        dve.tensor_scalar_mul(oT[:, i * P:(i + 1) * P], o_ps[:, P:2 * P], t.sub_g[:, 0:1])\
                           .then_inc(oT_kept.sem, 1)
                    else:
                        dve.tensor_copy(oT[:, i * P:(i + 1) * P], o_ps[:, P:2 * P]).then_inc(oT_kept.sem, 1)

                def page(it, p):
                    n = page_keys(p)
                    g = min(p // 2, S_GROUPS - 1)
                    at = p * PAGE - 2 * g * PAGE
                    if p == 0:
                        dve.wait_ge(ps_done.sem, ps_done.after(it, -1))
                        dve.tensor_copy(q_block[:, :].rearrange("p (b c) -> p b c", b=BLOCKS)[:, :, 0:16],
                                        t.q_heads[:, bass.ds(it + TURNS * kind, 1), :, :, :]
                                        .rearrange("p s b u q -> p (s b) (u q)")).then_inc(q_spread.sem, 1)
                    dve.wait_ge(kT_done.sem, kT_done.after(it, 2 * p + 1))
                    dve.wait_ge(ps_done.sem, ps_done.after(it, g - 2))
                    dve.tensor_copy(kT_page[:, g % 2, 4:8, at:at + n], kT_ps[:, 1, :, 0:n]).then_inc(kT_kept[1].sem, 1)

                def page_scores(it, g, part):
                    if part == 1 and g == S_GROUPS - 1:
                        dve.wait_ge(ps_done.sem, ps_done.after(it, g))
                        dve.wait_ge(sfar.sem, sfar.after(it, g))
                        n = PAGE + DEC_SEQ
                        dve.tensor_tensor(sS[:, KEYS - n:KEYS], s_ps[:, PAGE:PAGE + n], t.near_dec[:, 0:n], ALU.add)\
                           .then_inc(snear.sem, 1)

                def weigh(it, n):
                    if n == 0:
                        dve.wait_ge(sfar.sem, sfar.after(it, S_GROUPS - 1))
                        dve.wait_ge(snear.sem, snear.after(it, 0))
                        dve.tensor_reduce(sstat[0:D0, 0:1], sS[0:D0, :], axis=AX.X, op=ALU.max, negate=True)\
                           .then_inc(smax.sem, 1)
                    elif n == 3:
                        dve.wait_ge(sln.sem, sln.after(it, 0))
                        dve.scalar_tensor_tensor(sW[D0:P, :], sS[D0:P, :], 0.0, sW[D0:P, :], ALU.max, ALU.add)\
                           .then_inc(ssoft.sem, 1)
                    elif n == 4:
                        dve.wait_ge(ssoft.sem, ssoft.after(it, 0))
                        dve.tensor_tensor_scan(sW[D0:P, ::-1], sW[D0:P, ::-1], sW[D0:P, ::-1], 0.0, ALU.add,
                                               ALU.bypass).then_inc(sscan.sem, 1)
                    elif n == 5:
                        dve.wait_ge(sscan.sem, sscan.after(it, 0))
                        dve.tensor_tensor(sW[D0:P, :], sS[D0:P, :], sW[D0:P, :], ALU.subtract).then_inc(ssub.sem, 1)
                    elif n == 6:
                        dve.wait_ge(sexp.sem, sexp.after(it, 0))
                        dve.reciprocal(sstat[0:D0, 2:3], sstat[0:D0, 1:2]).then_inc(sinv.sem, 1)
                        dve.wait_ge(sinv.sem, sinv.after(it, 0))
                        dve.tensor_tensor(sstat[0:D0, 3:4], sstat[0:D0, 2:3], t.row_factor[0:D0, :], ALU.mult)\
                           .then_inc(sinv.sem, 1)

                def turn(it, g):
                    if g % 2 == 1:
                        m = len(group_pages(g))
                        dve.wait_ge(kT_done.sem, kT_done.after(it, 2 * D_PAGES + g))
                        dve.wait_ge(applied[1].sem, applied[1].after(it, g - V_GROUPS))
                        dve.tensor_copy(sT[:, 4 * g:4 * g + m, :], kT_ps[:, 1, 0:m, :]).then_inc(kT_kept[1].sem, 1)

                def rows(it, kind_half):
                    dve.wait_ge(applied[kind_half].sem, applied[kind_half].after(it, V_GROUPS - 1))
                    dve.wait_ge(heads_done.sem, heads_done.after(it, -1))
                    if kind_half == 0:
                        dve.wait_ge(sinv.sem, sinv.after(it, 1))
                        dve.tensor_scalar_mul(o_rows_s[0:D0, :], sO_ps[0:D0, :], sstat[0:D0, 3:4])\
                           .then_inc(rows_kept[0].sem, 1)
                    else:
                        dve.tensor_copy(o_rows_s[D0:P, :], sO_ps[D0:P, :]).then_inc(rows_kept[1].sem, 1)

                def heads(it, _):
                    dve.wait_ge(heads_done.sem, heads_done.after(it, 0))
                    dve.tensor_copy(t.sample_o[:, bass.ds(it + TURNS * kind, 1), :].rearrange("p a n -> p (a n)"),
                                    sO_ps[:, 0:P]).then_inc(so_kept.sem, 1)

                steps = dict(score=score, soft=soft_diff if kind == DIFF else soft_stick, out=out, turn_out=turn_out,
                             page=page, page_scores=page_scores, weigh=weigh, turn=turn, rows=rows, heads=heads)
                dve.memset(qT[HEAD:P, 0, :], 0.0).then_inc(zeroed, 1)
                dve.memset(qT[0:HEAD, 1, :], 0.0).then_inc(zeroed, 1)
                dve.memset(q_block[:, :], 0.0).then_inc(zeroed, 1)
                dve.wait_ge(zeroed, 3)
                with dve.Fori(0, TURNS) as it:
                    for name, *args in plan:
                        if name in steps:
                            steps[name](it, *args)

            @block.scalar
            def _(act):
                for c in (sc_far, exps, s_abs, s_expm, s_ln, s_exp, o_kept, o_squared, kT_kept[0], sfar, sexp, sabs,
                          sexpm, sln, sstick):
                    act.sem_inc(c.sem, c.per)
                if kind == DIFF:
                    for c in (wT_kept,):
                        act.sem_inc(c.sem, c.per)

                def score(it, i, chunk):
                    for g, (ci, u, k0, k1, kn) in enumerate(chunks):
                        if g != chunk or kn <= k0:
                            continue
                        act.wait_ge(sc_done.sem, sc_done.after(it, g))
                        act.wait_ge(w_turned.sem, w_turned.after(it, groups_upto[i - 2] - 1 if i >= 2 else
                                                                 groups_upto[PT - 2 + i] - 1 - groups_upto[-1]))
                        act.activation(S[:, i % 2, u, k0:kn], sc_ps[:, g % 2, 0:kn - k0], ACT.Copy)\
                           .then_inc(sc_far.sem, 1)

                def soft_diff(it, i, n):
                    end = (i + 1) * P
                    if n == 1:
                        act.wait_ge(row_max.sem, row_max.after(it, i))
                        for u in range(2):
                            act.activation(S[:, i % 2, u, 0:end], S[:, i % 2, u, 0:end], ACT.Exp,
                                           bias=stat[:, i % 4, u:u + 1],
                                           accum_out=stat[:, i % 4, 2 + u:3 + u]).then_inc(exps.sem, 1)

                def soft_stick(it, i, n):
                    end = (i + 1) * P
                    last_chunk = max(g for g, c in enumerate(chunks) if c[0] == i)
                    if n == 0:
                        act.wait_ge(sc_far.sem, sc_far.after(it, far_upto[last_chunk] - 1))
                        act.wait_ge(sc_near.sem, sc_near.after(it, near_upto[last_chunk] - 1))
                        act.wait_ge(s_sub.sem, s_sub.after(it, i - 1))
                        act.activation(aux[:, :, 0:end], S[:, i % 2, :, 0:end], ACT.Abs).then_inc(s_abs.sem, 1)
                    elif n == 1:
                        act.wait_ge(s_abs.sem, s_abs.after(it, i))
                        act.activation(aux[:, :, 0:end], aux[:, :, 0:end], ACT.Exp, scale=-1.0).then_inc(s_expm.sem, 1)
                    elif n == 2:
                        act.wait_ge(s_expm.sem, s_expm.after(it, i))
                        act.activation(aux[:, :, 0:end], aux[:, :, 0:end], ACT.Ln, bias=1.0).then_inc(s_ln.sem, 1)
                    elif n == 5:
                        act.wait_ge(s_sub.sem, s_sub.after(it, i))
                        act.activation(S[:, i % 2, :, 0:end], S[:, i % 2, :, 0:end], ACT.Exp).then_inc(s_exp.sem, 1)

                def out(it, i, n):
                    groups = turned_groups(kind, i)
                    first = groups_upto[i] - n_groups[i]
                    if n < len(groups):
                        if kind == DIFF:
                            act.wait_ge(w_turned.sem, w_turned.after(it, first + n))
                            act.wait_ge(o_done.sem, o_done.after(it, i - 1))
                            m = len(groups[n])
                            act.activation(wT[:, 4 * n:4 * n + m, :], wT_ps[:, 0:m, :], ACT.Copy)\
                               .then_inc(wT_kept.sem, 1)
                        return
                    act.wait_ge(o_done.sem, o_done.after(it, i))
                    if kind == STICK:
                        act.wait_ge(oT_done.sem, oT_done.after(it, i - 1))
                        act.activation(o_norm[:, :], o_ps[:, 0:P], ACT.Copy).then_inc(o_kept.sem, 1)
                    else:
                        act.wait_ge(o_normed.sem, o_normed.after(it, i - 2))
                        act.activation(o_rows[:, i % 2, :], o_ps[:, 0:P], ACT.Copy, scale=stat[:, i % 4, 4:5])\
                           .then_inc(o_kept.sem, 1)
                        act.wait_ge(o_kept.sem, o_kept.after(it, i))
                        act.wait_ge(o_squared.sem, o_squared.after(it, i - 1))
                        act.activation(o_sq[:, :], o_rows[:, i % 2, :], ACT.Square,
                                       accum_out=stat[:, i % 4, 5:6]).then_inc(o_squared.sem, 1)

                def page(it, p):
                    n = page_keys(p)
                    g = min(p // 2, S_GROUPS - 1)
                    at = p * PAGE - 2 * g * PAGE
                    act.wait_ge(kT_done.sem, kT_done.after(it, 2 * p))
                    act.wait_ge(ps_done.sem, ps_done.after(it, g - 2))
                    act.activation(kT_page[:, g % 2, 0:4, at:at + n], kT_ps[:, 0, :, 0:n], ACT.Copy)\
                       .then_inc(kT_kept[0].sem, 1)

                def page_scores(it, g, part):
                    if part == 0:
                        return
                    n = 2 * PAGE if g + 1 < S_GROUPS else PAGE
                    act.wait_ge(ps_done.sem, ps_done.after(it, g))
                    act.wait_ge(ssub.sem, ssub.after(it, -1))
                    act.wait_ge(sexp.sem, sexp.after(it, -1))
                    act.activation(sS[:, 2 * g * PAGE:2 * g * PAGE + n], s_ps[:, 0:n], ACT.Copy).then_inc(sfar.sem, 1)

                def weigh(it, n):
                    if n == 0:
                        act.wait_ge(sfar.sem, sfar.after(it, S_GROUPS - 1))
                        act.wait_ge(snear.sem, snear.after(it, 0))
                        act.wait_ge(kT_done.sem, kT_done.after(it, -1))
                        act.activation(sW[D0:P, :], sS[D0:P, :], ACT.Abs).then_inc(sabs.sem, 1)
                    elif n == 1:
                        act.wait_ge(sabs.sem, sabs.after(it, 0))
                        act.activation(sW[D0:P, :], sW[D0:P, :], ACT.Exp, scale=-1.0).then_inc(sexpm.sem, 1)
                    elif n == 2:
                        act.wait_ge(sexpm.sem, sexpm.after(it, 0))
                        act.activation(sW[D0:P, :], sW[D0:P, :], ACT.Ln, bias=1.0).then_inc(sln.sem, 1)
                    elif n == 3:
                        act.wait_ge(smax.sem, smax.after(it, 0))
                        act.wait_ge(kT_done.sem, kT_done.after(it, -1))
                        act.wait_ge(rows_kept[0].sem, rows_kept[0].after(it, -1))
                        act.activation(sW[0:D0, :], sS[0:D0, :], ACT.Exp, bias=sstat[0:D0, 0:1],
                                       accum_out=sstat[0:D0, 1:2]).then_inc(sexp.sem, 1)
                    elif n == 6:
                        act.wait_ge(ssub.sem, ssub.after(it, 0))
                        act.activation(sW[D0:P, :], sW[D0:P, :], ACT.Exp).then_inc(sstick.sem, 1)

                def turn(it, g):
                    if g % 2 == 0:
                        m, n = len(group_pages(g)), page_keys(4 * g)
                        act.wait_ge(kT_done.sem, kT_done.after(it, 2 * D_PAGES + g))
                        act.wait_ge(applied[1].sem, applied[1].after(it, g - V_GROUPS))
                        act.activation(sT[0:n, 4 * g:4 * g + m, :], kT_ps[0:n, 0, 0:m, :], ACT.Copy)\
                           .then_inc(kT_kept[0].sem, 1)

                steps = dict(score=score, soft=soft_diff if kind == DIFF else soft_stick, out=out, page=page,
                             page_scores=page_scores, weigh=weigh, turn=turn)
                act.sem_inc(oT_stored, 16)
                with act.Fori(0, TURNS) as it:
                    for name, *args in plan:
                        if name in steps:
                            steps[name](it, *args)
                    act.wait_ge(oT_kept.sem, oT_kept.after(it, PT - 1))
                    act.dma_start(t.oT[:, bass.ds(it + TURNS * kind, 1), 0:SEQ].rearrange("p a n -> p (a n)"), oT[:, :])\
                       .then_inc(oT_stored, 16)
                act.wait_ge(oT_stored, 16 * (TURNS + 1))


        clear(nc, sems)


def sample_heads_out(nc, t):
    with ExitStack() as ctx:
        sems = []

        def sb(name, shape, dt=F32):
            return ctx.enter_context(nc.sbuf_tensor(name, shape, dt))

        def sem(name):
            sems.append(ctx.enter_context(nc.semaphore(name)))
            return sems[-1]

        oT = sb("sample_oT", [P, BLOCKS, P])
        mix = sb("sample_diff", [P, DEC_BATCH, H_DIFF, DEC_SEQ])
        sq = sb("sample_diff_sq", [P, DEC_BATCH * H_DIFF * DEC_SEQ])
        rms = sb("sample_rms", [P, DEC_BATCH * H_DIFF * DEC_SEQ])
        ms_ps = ctx.enter_context(nc.psum_tensor("sample_ms_ps", [P, BANK], F32))
        step, sums, roots, stored = sem("so_step"), sem("so_sums"), sem("so_roots"), sem("so_stored")
        N = DEC_BATCH * H_DIFF * DEC_SEQ
        with nc.Block() as block:

            @block.vector
            def _(dve):
                o = t.sample_o[:, :, :].rearrange("p s (b u q) -> p s b u q", b=BLOCKS, u=2)
                dve.memset(oT[:, :, :], 0.0).then_inc(step, 1)
                for s in range(DEC_BATCH):
                    dve.tensor_tensor(mix[:, s, :, :], o[:, s, 0:H_DIFF, 0, :], o[:, s, 0:H_DIFF, 1, :], ALU.add)\
                       .then_inc(step, 1)
                dve.wait_ge(step, 1 + DEC_BATCH)
                flat = mix[:, :, :, :].rearrange("p s h q -> p (s h q)")
                dve.tensor_tensor(sq[:, :], flat, flat, ALU.mult).then_inc(step, 1)
                for u in range(2):
                    rows = slice(HEAD * u, HEAD * u + HEAD)
                    for b in range(H_DIFF, BLOCKS):
                        dve.tensor_copy(oT[rows, b, 0:N_SAMPLE].rearrange("p (s q) -> p s q", q=DEC_SEQ),
                                        o[rows, :, b, u, :]).then_inc(step, 1)
                dve.wait_ge(sums, 1)
                dve.tensor_scalar(rms[:, :], ms_ps[:, 0:N], 1.0 / P, SUBLN_EPS, ALU.mult, ALU.add).then_inc(step, 1)
                dve.wait_ge(roots, 1)
                dve.reciprocal(rms[:, :], rms[:, :]).then_inc(step, 1)
                done = 1 + DEC_BATCH + 1 + 2 * (BLOCKS - H_DIFF) + 2
                dve.wait_ge(step, done)
                dve.scalar_tensor_tensor(rms[:, :], rms[:, :], t.sub_g[:, 0:1], flat, ALU.mult, ALU.mult)\
                   .then_inc(step, 1)
                dve.wait_ge(step, done + 1)
                for b in range(H_DIFF):
                    dve.tensor_copy(oT[:, b, 0:N_SAMPLE].rearrange("p (s q) -> p s q", q=DEC_SEQ),
                                    rms[:, :].rearrange("p (s h q) -> p h s q", h=H_DIFF, q=DEC_SEQ)[:, b])\
                       .then_inc(step, 1)

            @block.tensor
            def _(pe):
                pe.wait_ge(step, 2 + DEC_BATCH)
                pe.matmul(ms_ps[:, 0:N], t.ones[:, :], sq[:, :], start=True, stop=True).then_inc(sums, 1)

            @block.scalar
            def _(act):
                act.wait_ge(step, 1 + DEC_BATCH + 1 + 2 * (BLOCKS - H_DIFF) + 1)
                act.activation(rms[:, :], rms[:, :], ACT.Sqrt).then_inc(roots, 1)

            @block.sync
            def _(sp):
                sp.wait_ge(step, 1 + DEC_BATCH + 1 + 2 * (BLOCKS - H_DIFF) + 3 + H_DIFF)
                sp.dma_start(t.oT[:, :, SEQ:TILES * P], oT[:, :, :]).then_inc(stored, 16)
                sp.wait_ge(stored, 16)

        clear(nc, sems)


N_LOGITS = N_GROUPS + N_EXPERTS
N_SLOTS = MOE_TILES * P
ALL = TILES * P


def tile_loop(engine, tile):
    with engine.Fori(0, PT // 2) as it:
        for u in range(2):
            tile(it, u)
    tile(PT // 2, 0)


def row_tile(dram, tile):
    return dram[bass.ds(tile * P, P), :]


def mix_out(nc, t):
    with ExitStack() as ctx:
        sems = []

        def sb(name, shape, dt=F32):
            return ctx.enter_context(nc.sbuf_tensor(name, shape, dt))

        def ps(name, shape):
            return ctx.enter_context(nc.psum_tensor(name, shape, F32))

        def sem(name):
            sems.append(ctx.enter_context(nc.semaphore(name)))
            return sems[-1]

        w_out = sb("w_out", [P, BLOCKS, 2, BANK])
        w_route = sb("w_route", [P, KC, N_LOGITS])
        b_route = sb("b_route", [P, N_LOGITS])
        g_row = sb("g_ffn_row", [P, D_MODEL])
        oT = sb("oT_tile", [P, 2, BLOCKS, P])
        x = sb("x_again", [P, 2, D_MODEL])
        x1 = sb("x1_tile", [P, 2, D_MODEL])
        h = sb("h2_tile", [P, 2, D_MODEL])
        hT = sb("h2T_tile", [P, KC, P])
        square = sb("square2", [P, D_MODEL])
        ss = sb("sum_squares2", [P, 2, 3])
        y_ps = ps("mix_out_ps", [P, 2, 2, BANK])
        hT_ps = ps("h2T_ps", [P, 2, BANK])
        lg_ps = ps("logits_ps", [P, BANK])

        w_loaded, r_loaded = sem("w_out_loaded"), sem("routers_loaded")
        x_loaded = [sem(f"x_again_loaded{u}") for u in range(2)]
        o_loaded = [sem(f"oT_loaded{u}") for u in range(2)]
        stored = [sem(f"x1_h2_stored{u}") for u in range(2)]
        y_done = Count(sem("mix_out_in_psum"), 4)
        x1_done = Count(sem("x1_done"), 4)
        squares = Count(sem("squares2_done"), 2)
        rstd_step = Count(sem("rstd2_step"), 2)
        rstd = Count(sem("rstd2_done"), 2)
        h_done = Count(sem("h2_done"), 2)
        hT_done = Count(sem("h2T_in_psum"), 4)
        hT_kept = Count(sem("h2T_kept"), 4)
        lg_done = Count(sem("logits_in_psum"), 2)
        lg_kept = Count(sem("logits_kept"), 2)

        with nc.Block() as block:

            @block.sync
            def _(sp):
                sp.dma_start(w_route[:, :, 0:N_GROUPS], t.w_group.rearrange("(k p) n -> p k n", p=P))\
                  .then_inc(r_loaded, 16)
                sp.dma_start(w_route[:, :, N_GROUPS:N_LOGITS], t.w_erouter.rearrange("(k p) n -> p k n", p=P))\
                  .then_inc(r_loaded, 16)
                sp.dma_start(b_route[:, 0:N_GROUPS], t.b_group.partition_broadcast(P)).then_inc(r_loaded, 16)
                sp.dma_start(b_route[:, N_GROUPS:N_LOGITS], t.b_erouter.partition_broadcast(P)).then_inc(r_loaded, 16)
                sp.dma_start(g_row[:, :], t.g_ffn.partition_broadcast(P)).then_inc(r_loaded, 16)
                for u in range(2):
                    sp.sem_inc(stored[u], 32)

                def load(it, u, tile):
                    sp.dma_start(oT[:, u, :, :], t.oT[:, :, bass.ds(tile * P, P)]).then_inc(o_loaded[u], 16)
                    sp.dma_start(x[:, u, :], row_tile(t.x, tile)).then_inc(x_loaded[u], 16)

                load(0, 0, 0)
                sp.dma_start(w_out[:, :, :, :], t.w_out.rearrange("(k p) (c n) -> p k c n", p=P, n=BANK))\
                  .then_inc(w_loaded, 16)

                def tile(it, u, final=False):
                    if not final:
                        sp.wait_ge(x1_done.sem, x1_done.after(it, 2 * (u - 1) + 1))
                        load(it, 1 - u, it * 2 + u + 1)
                    sp.wait_ge(x1_done.sem, x1_done.after(it, 2 * u + 1))
                    sp.dma_start(row_tile(t.x1, it * 2 + u), x1[:, u, :]).then_inc(stored[u], 16)
                    sp.wait_ge(h_done.sem, h_done.after(it, u))
                    sp.dma_start(row_tile(t.h2, it * 2 + u), h[:, u, :]).then_inc(stored[u], 16)

                with sp.Fori(0, PT // 2) as it:
                    for u in range(2):
                        tile(it, u)
                tile(PT // 2, 0, final=True)
                sp.wait_ge(stored[0], 32 * (2 + PT // 2))
                sp.wait_ge(stored[1], 32 * (1 + PT // 2))

            @block.tensor
            def _(pe):
                for c in (y_done, hT_done, lg_done):
                    pe.sem_inc(c.sem, c.per)

                def out(it, u):
                    pe.wait_ge(o_loaded[u], it * 16 + 16)
                    for c in range(2):
                        pe.wait_ge(x1_done.sem, x1_done.after(it, 2 * (u - 2) + c))
                        for k in range(BLOCKS):
                            last = pe.matmul(y_ps[:, u, c, :], oT[:, u, k, :], w_out[:, k, c, :],
                                             start=(k == 0), stop=(k == BLOCKS - 1))
                        last.then_inc(y_done.sem, 1)

                def route(it, u):
                    pe.wait_ge(h_done.sem, h_done.after(it, u))
                    for half in range(2):
                        pe.wait_ge(hT_kept.sem, hT_kept.after(it, 2 * (u - 1) + half))
                        for k in range(4):
                            last = pe.transpose(hT_ps[:, half, k * P:(k + 1) * P],
                                                h[:, u, (4 * half + k) * P:(4 * half + k + 1) * P], t.ident[:, :])
                        last.then_inc(hT_done.sem, 1)
                    pe.wait_ge(hT_kept.sem, hT_kept.after(it, 2 * u + 1))
                    pe.wait_ge(lg_kept.sem, lg_kept.after(it, u - 1))
                    for k in range(KC):
                        last = pe.matmul(lg_ps[:, 0:N_LOGITS], hT[:, k, :], w_route[:, k, :],
                                         start=(k == 0), stop=(k == KC - 1))
                    last.then_inc(lg_done.sem, 1)

                pe.wait_ge(w_loaded, 16)
                pe.wait_ge(r_loaded, 16 * 5)
                out(0, 0)
                with pe.Fori(0, PT // 2) as it:
                    for u in range(2):
                        out(it + u, 1 - u)
                        route(it, u)
                route(PT // 2, 0)

            @block.vector
            def _(dve):
                for c in (x1_done, h_done, lg_kept):
                    dve.sem_inc(c.sem, c.per)
                dve.wait_ge(r_loaded, 16 * 5)

                def residual(it, u):
                    dve.wait_ge(x_loaded[u], it * 16 + 16)
                    dve.wait_ge(stored[u], it * 32 + 32)
                    dve.wait_ge(h_done.sem, h_done.after(it, u - 2))
                    dve.wait_ge(squares.sem, squares.after(it, u - 2))
                    for c in range(2):
                        dve.wait_ge(y_done.sem, y_done.after(it, 2 * u + c))
                        dve.tensor_tensor(x1[:, u, c * BANK:(c + 1) * BANK], y_ps[:, u, c, :],
                                          x[:, u, c * BANK:(c + 1) * BANK], ALU.add).then_inc(x1_done.sem, 1)

                def tile(it, u, final=False):
                    dve.wait_ge(rstd.sem, rstd.after(it, u))
                    dve.wait_ge(x1_done.sem, x1_done.after(it, 2 * u + 1))
                    dve.wait_ge(hT_done.sem, hT_done.after(it, 2 * (u - 2) + 1))
                    dve.scalar_tensor_tensor(h[:, u, :], x1[:, u, :], ss[:, u, 2:3], g_row[:, :], ALU.mult, ALU.mult)\
                       .then_inc(h_done.sem, 1)
                    if not final:
                        residual(it + u, 1 - u)
                    dve.wait_ge(lg_done.sem, lg_done.after(it, u))
                    dve.tensor_tensor(t.logits[:, bass.ds(it * 2 + u, 1), :].rearrange("p a n -> p (a n)"),
                                      lg_ps[:, 0:N_LOGITS], b_route[:, :], ALU.add).then_inc(lg_kept.sem, 1)

                residual(0, 0)
                with dve.Fori(0, PT // 2) as it:
                    for u in range(2):
                        tile(it, u)
                tile(PT // 2, 0, final=True)

            @block.gpsimd
            def _(pool):
                pool.sem_inc(rstd_step.sem, rstd_step.per)
                pool.sem_inc(rstd.sem, rstd.per)

                def tile(it, u):
                    pool.wait_ge(squares.sem, squares.after(it, u))
                    own_wait(pool, t)
                    pool.tensor_scalar(ss[:, u, 1:2], ss[:, u, 0:1], 1.0 / D_MODEL, NORM_EPS, ALU.mult, ALU.add)\
                        .then_inc(rstd_step.sem, 1)
                    pool.wait_ge(rstd_step.sem, rstd_step.after(it, u))
                    pool.wait_ge(h_done.sem, h_done.after(it, u - 2))
                    pool.tensor_tensor(ss[:, u, 2:3], ss[:, u, 1:2], t.neg_half[:, :], ALU.pow)\
                        .then_inc(rstd.sem, 1)

                tile_loop(pool, tile)

            @block.scalar
            def _(act):
                act.sem_inc(squares.sem, squares.per)
                act.sem_inc(hT_kept.sem, hT_kept.per)

                def square_sum(it, u):
                    act.wait_ge(x1_done.sem, x1_done.after(it, 2 * u + 1))
                    act.wait_ge(squares.sem, squares.after(it, u - 1))
                    act.activation(square[:, :], x1[:, u, :], ACT.Square, accum_out=ss[:, u, 0:1])\
                       .then_inc(squares.sem, 1)

                def tile(it, u, final=False):
                    for half in range(2):
                        act.wait_ge(hT_done.sem, hT_done.after(it, 2 * u + half))
                        act.wait_ge(lg_done.sem, lg_done.after(it, u - 1))
                        act.activation(hT[:, 4 * half:4 * half + 4, :], hT_ps[:, half, :], ACT.Copy)\
                           .then_inc(hT_kept.sem, 1)
                    if not final:
                        square_sum(it + u, 1 - u)

                square_sum(0, 0)
                with act.Fori(0, PT // 2) as it:
                    for u in range(2):
                        tile(it, u)
                tile(PT // 2, 0, final=True)

        clear(nc, sems)


def route(nc, t):
    with ExitStack() as ctx:
        sems = []

        def sb(name, shape, dt=F32):
            return ctx.enter_context(nc.sbuf_tensor(name, shape, dt))

        def sem(name):
            sems.append(ctx.enter_context(nc.semaphore(name)))
            return sems[-1]

        G, J, E = N_GROUPS, PER_GROUP, N_EXPERTS
        rank = sb("first_wins", [P, TILES, G])
        limits = sb("limits", [P, E, TILES])
        tile_no = sb("tile_numbers", [P, MOE_TILES, E])
        spare = sb("spare_slots", [P, TILES])
        before = sb("before", [P, P])
        token = sb("token_ids", [P, TILES])
        column = sb("column_numbers", [P, P])
        part_i = sb("slot_parts_i", [P, 2, TOP_K * TILES], I32)
        part = sb("slot_parts", [P, 2, TOP_K * TILES])
        place = sb("place_hot", [P, 2, P])
        tile_token = sb("token_by_tile", [P, 2, MOE_TILES])
        g_max = sb("g_max", [P, TILES, 1])
        g_exp = sb("g_exp", [P, TILES, G])
        g_hot = sb("g_hot", [P, TILES, G])
        one = sb("one_hot", [P, 2, TILES, J])
        tmp = sb("tmp4", [P, TILES, G])
        top = sb("top", [P, 4, TILES, 1])
        el = sb("group_logits", [P, TILES, J])
        prod = sb("group_products", [P, TILES, J, G])
        hot = sb("expert_hot", [P, 2, TILES, G, J])
        member = sb("member", [P, TILES, E])
        pos = sb("positions", [P, TILES, E])
        total = sb("tile_counts", [P, TILES, E])
        carry = sb("carried", [P, TILES + 1, E])
        filled = sb("filled", [P, E, TILES])
        n_tiles = sb("n_tiles", [P, E])
        ends = sb("tile_ends", [P, E])
        base = sb("slot_bases", [P, E])
        passed = sb("passed", [P, MOE_TILES, E])
        te = sb("tile_expert_f", [P, MOE_TILES])
        slot_f = sb("slot_f", [P, 2, TILES])
        picked = sb("picked", [P, 2, TILES, E])
        zero_y = sb("zero_y", [P, D_MODEL])
        cnt_ps = ctx.enter_context(nc.psum_tensor("counts_ps", [P, 2, BANK], F32))
        loaded, step, gexp, wexp = sem("route_loaded"), sem("route_step"), sem("g_exp_done"), sem("w_exp_done")
        counted, zeroed, spare_stored, placed = sem("counted"), sem("zeroed_y"), sem("spare_rows_stored"), sem("placed")

        with nc.Block() as block:

            @block.vector
            def _(dve):
                done = [0]

                def link(ins):
                    done[0] += 1
                    ins.then_inc(step, 1)
                    dve.wait_ge(step, done[0])

                def wide(ap, shape):
                    return ap.broadcast_to(shape)

                S3 = [P, TILES, G]

                def first_max(values, maximum, out):
                    link(dve.tensor_tensor(tmp[:, :, :], values, wide(maximum, S3), ALU.is_equal))
                    link(dve.tensor_tensor(tmp[:, :, :], tmp[:, :, :], rank[:, :, :], ALU.mult))
                    link(dve.tensor_reduce(top[:, 3, :, :], tmp[:, :, :], axis=AX.X, op=ALU.max))
                    link(dve.tensor_tensor(out, tmp[:, :, :], wide(top[:, 3, :, :], S3), ALU.is_equal))

                gl = t.logits[:, :, 0:G]
                dve.wait_ge(loaded, 16 * 7)
                link(dve.tensor_reduce(g_max[:, :, :], gl, axis=AX.X, op=ALU.max))
                link(dve.tensor_tensor(g_exp[:, :, :], gl, wide(g_max[:, :, :], S3), ALU.subtract))
                t.n_gdiff = done[0]
                first_max(gl, g_max[:, :, :], g_hot[:, :, :])
                for g in range(G):
                    link(dve.tensor_tensor(prod[:, :, :, g], t.logits[:, :, G + J * g:G + J * g + J],
                                           wide(g_hot[:, :, g:g + 1], [P, TILES, J]), ALU.mult))
                link(dve.tensor_reduce(el[:, :, :], prod[:, :, :, :], axis=AX.X, op=ALU.add))
                link(dve.tensor_reduce(top[:, 0, :, :], el[:, :, :], axis=AX.X, op=ALU.max))
                first_max(el[:, :, :], top[:, 0, :, :], one[:, 0, :, :])
                link(dve.scalar_tensor_tensor(el[:, :, :], one[:, 0, :, :], NEG, el[:, :, :], ALU.mult, ALU.add))
                link(dve.tensor_reduce(top[:, 1, :, :], el[:, :, :], axis=AX.X, op=ALU.max))
                first_max(el[:, :, :], top[:, 1, :, :], one[:, 1, :, :])
                link(dve.tensor_tensor(top[:, 2, :, :], top[:, 1, :, :], top[:, 0, :, :], ALU.subtract))
                t.n_wdiff = done[0]
                for k in range(TOP_K):
                    for g in range(G):
                        link(dve.tensor_tensor(hot[:, k, :, g, :], one[:, k, :, :],
                                               wide(g_hot[:, :, g:g + 1], [P, TILES, J]), ALU.mult))
                link(dve.memset(hot[N_SAMPLE:P, :, PT, :, :], 0.0))
                link(dve.tensor_tensor(member[:, :, :], hot[:, 0, :, :, :].rearrange("p t g j -> p t (g j)"),
                                       hot[:, 1, :, :, :].rearrange("p t g j -> p t (g j)"), ALU.add))
                t.n_member = done[0]
                dve.wait_ge(gexp, 1)
                link(dve.tensor_reduce(g_max[:, :, :], g_exp[:, :, :], axis=AX.X, op=ALU.add))
                dve.wait_ge(wexp, 1)
                link(dve.tensor_scalar_add(top[:, 3, :, :], top[:, 2, :, :], 1.0))
                link(dve.tensor_tensor(g_max[:, :, :], g_max[:, :, :], top[:, 3, :, :], ALU.mult))
                link(dve.reciprocal(t.gates[:, 0, :], g_max[:, :, 0]))
                link(dve.tensor_tensor(t.gates[:, 1, :], t.gates[:, 0, :], top[:, 2, :, 0], ALU.mult))
                dve.wait_ge(counted, 1)
                flat = "p t e -> p (t e)"
                link(dve.tensor_copy(pos[:, :, :].rearrange(flat), cnt_ps[:, 0, 0:TILES * E]))
                link(dve.tensor_copy(total[:, :, :].rearrange(flat), cnt_ps[:, 1, 0:TILES * E]))
                link(dve.memset(carry[:, 0, :], 0.0))
                for n in range(TILES):
                    link(dve.tensor_tensor(carry[:, n + 1, :], carry[:, n, :], total[:, n, :], ALU.add))
                link(dve.tensor_tensor(filled[:, :, :],
                                       wide(carry[:, TILES, :].unsqueeze(2), [P, E, TILES]), limits[:, :, :], ALU.is_gt))
                link(dve.tensor_reduce(n_tiles[:, :], filled[:, :, :], axis=AX.X, op=ALU.add))
                link(dve.tensor_tensor_scan(ends[:, :], n_tiles[:, :], n_tiles[:, :], 0.0, ALU.add, ALU.bypass))
                link(dve.tensor_tensor(base[:, :], ends[:, :], n_tiles[:, :], ALU.subtract))
                link(dve.tensor_scalar_mul(base[:, :], base[:, :], float(P)))
                link(dve.tensor_tensor(passed[:, :, :], tile_no[:, :, :],
                                       wide(ends[:, :].unsqueeze(1), [P, MOE_TILES, E]), ALU.is_ge))
                link(dve.tensor_reduce(te[:, :], passed[:, :, :], axis=AX.X, op=ALU.add))
                link(dve.tensor_scalar_min(te[:, :], te[:, :], float(E - 1)))
                link(dve.tensor_copy(t.tile_expert[:, :], te[0:1, :]))
                link(dve.tensor_tensor(pos[:, :, :], pos[:, :, :], carry[:, 0:TILES, :], ALU.add))
                link(dve.tensor_tensor(pos[:, :, :], pos[:, :, :],
                                       wide(base[:, :].unsqueeze(1), [P, TILES, E]), ALU.add))
                for k in range(TOP_K):
                    link(dve.tensor_tensor(picked[:, k, :, :], hot[:, k, :, :, :].rearrange("p t g j -> p t (g j)"),
                                           pos[:, :, :], ALU.mult))
                    link(dve.tensor_reduce(slot_f[:, k, :], picked[:, k, :, :], axis=AX.X, op=ALU.add))
                    link(dve.tensor_tensor(slot_f[:, k, :], slot_f[:, k, :], spare[:, :], ALU.add))
                    link(dve.tensor_copy(t.slots[:, :].rearrange("p (t k) -> p k t", k=2)[:, k], slot_f[:, k, :]))
                link(dve.tensor_scalar(part_i[:, 0, :], t.slots[:, :], P.bit_length() - 1, None, ALU.logical_shift_right))
                link(dve.tensor_scalar(part_i[:, 1, :], t.slots[:, :], P - 1, None, ALU.bitwise_and))
                link(dve.tensor_copy(part[:, :, :], part_i[:, :, :]))
                t.n_first_place = done[0] + 2
                for n in range(TOP_K * TILES):
                    if n >= 2:
                        dve.wait_ge(placed, n - 1)
                    done[0] += 2
                    dve.tensor_scalar(place[:, n % 2, :], column[:, :], part[:, 1, n:n + 1], None, ALU.is_equal)\
                       .then_inc(step, 1)
                    dve.tensor_scalar(tile_token[:, n % 2, :], column[:, 0:MOE_TILES], part[:, 0, n:n + 1],
                                      token[:, n // TOP_K:n // TOP_K + 1], ALU.is_equal, ALU.mult).then_inc(step, 1)
                dve.wait_ge(placed, TOP_K * TILES)
                link(dve.tensor_copy(t.slot_tok[:, :], cnt_ps[:, 0, 0:MOE_TILES]))

            @block.sync
            def _(sp):
                for dst, src in ((rank, t.rank_const), (limits, t.limits_const), (tile_no, t.tile_no_const)):
                    sp.dma_start(dst[:, :, :], src.partition_broadcast(P)).then_inc(loaded, 16)
                sp.dma_start(column[:, :], t.column_const.partition_broadcast(P)).then_inc(loaded, 16)
                for dst, src in ((spare, t.spare_const), (before, t.before_const), (token, t.token_const)):
                    sp.dma_start(dst[:, :], src).then_inc(loaded, 16)
                sp.wait_ge(zeroed, 1)
                sp.dma_start(t.moe_out[N_SLOTS:N_SLOTS + P, :], zero_y[:, :]).then_inc(spare_stored, 16)
                sp.wait_ge(spare_stored, 16)

            @block.tensor
            def _(pe):
                pe.wait_ge(step, t.n_member)
                pe.matmul(cnt_ps[:, 0, 0:TILES * E], before[:, :], member[:, :, :], start=True, stop=True)
                pe.matmul(cnt_ps[:, 1, 0:TILES * E], t.ones[:, :], member[:, :, :], start=True, stop=True)\
                  .then_inc(counted, 1)
                for n in range(TOP_K * TILES):
                    pe.wait_ge(step, t.n_first_place + 2 * n)
                    pe.matmul(cnt_ps[:, 0, 0:MOE_TILES], place[:, n % 2, :], tile_token[:, n % 2, :], start=(n == 0),
                              stop=(n == TOP_K * TILES - 1)).then_inc(placed, 1)

            @block.scalar
            def _(act):
                act.wait_ge(step, t.n_gdiff)
                act.activation(g_exp[:, :, :], g_exp[:, :, :], ACT.Exp).then_inc(gexp, 1)
                act.wait_ge(step, t.n_wdiff)
                act.activation(top[:, 2, :, :], top[:, 2, :, :], ACT.Exp).then_inc(wexp, 1)

            @block.gpsimd
            def _(pool):
                pool.memset(zero_y[:, :], 0.0).then_inc(zeroed, 1)

        clear(nc, sems)


GU = 2 * D_EXPERT


def experts(nc, t):
    with ExitStack() as ctx:
        sems = []

        def sb(name, shape, dt=F32):
            return ctx.enter_context(nc.sbuf_tensor(name, shape, dt))

        def ps(name, shape):
            return ctx.enter_context(nc.psum_tensor(name, shape, F32))

        def sem(name):
            sems.append(ctx.enter_context(nc.semaphore(name)))
            return sems[-1]

        class TileCount:

            def __init__(self, name, per):
                self.sem, self.per = sem(name), per

            def after(self, tile, k):
                return tile * self.per + (2 * self.per + k + 1)

        FK = D_EXPERT // P
        w_gu = sb("w_gate_up", [P, 2, KC, 2, D_EXPERT])
        w_dn = sb("w_down", [P, 2, FK, D_MODEL])
        rows = sb("slot_rows", [P, 2, D_MODEL])
        idx = sb("slot_index", [P, 2], I32)
        xT = sb("slot_rows_T", [P, 2, KC, P])
        gate = sb("silu_gate", [P, 2, D_EXPERT])
        act_rows = sb("expert_act", [P, 2, D_EXPERT])
        aT = sb("expert_act_T", [P, 2, FK, P])
        y = sb("expert_out", [P, 2, D_MODEL])
        gu_ps = ps("gate_up_ps", [P, 2, GU])
        xT_ps = ps("slot_rows_T_ps", [P, 2, BANK])
        aT_ps = ps("act_T_ps", [P, BANK])
        y_ps = ps("expert_out_ps", [P, 2, BANK])

        gu_loaded = [sem(f"w_gate_up_loaded{u}") for u in range(2)]
        dn_loaded = [sem(f"w_down_loaded{u}") for u in range(2)]
        rows_loaded = [sem(f"slot_rows_loaded{u}") for u in range(2)]
        y_stored = [sem(f"expert_out_stored{u}") for u in range(2)]
        idx_done = TileCount("slot_index_done", 1)
        xT_done, xT_kept = TileCount("xT_in_psum", 2), TileCount("xT_kept", 2)
        gu_done, silu = TileCount("gate_up_in_psum", 1), TileCount("silu_done", 1)
        a_done, aT_done, aT_kept = TileCount("act_done", 1), TileCount("aT_in_psum", 1), TileCount("aT_kept", 1)
        y_done = TileCount("y_in_psum", 2)
        y_kept = [TileCount("y_half0_kept", 1), TileCount("y_half1_kept", 1)]

        def tiles(engine, step):
            with engine.Fori(0, MOE_TILES // 2 - 1) as it:
                for u in range(2):
                    step(it * 2 + (1 + u), (1 + u) % 2, it + u)

        LAST = MOE_TILES - 1
        assert LAST % 2 == 1

        with nc.Block() as block:

            @block.sync
            def _(sp):
                def load(tile, u):
                    e = sp.value_load(t.tile_expert[0:1, bass.ds(tile, 1)], min_val=0, max_val=N_EXPERTS - 1)
                    sp.wait_ge(gu_done.sem, gu_done.after(tile, -2))
                    for n, w in enumerate((t.w_gate, t.w_up)):
                        sp.dma_start(w_gu[:, u, :, n, :], w[bass.ds(e, 1), :, :].rearrange("e (k p) n -> p (e k) n", p=P))\
                          .then_inc(gu_loaded[u], 16)
                    sp.wait_ge(y_done.sem, y_done.after(tile, -3))
                    sp.dma_start(w_dn[:, u, :, :], t.w_down[bass.ds(e, 1), :, :].rearrange("e (k p) n -> p (e k) n", p=P))\
                      .then_inc(dn_loaded[u], 16)

                with sp.Fori(0, MOE_TILES // 2) as it:
                    for u in range(2):
                        load(it * 2 + u, u)

            @block.gpsimd
            def _(pool):
                pool.sem_inc(idx_done.sem, 2)
                with pool.Fori(0, MOE_TILES // 2) as it:
                    for u in range(2):
                        tile = it * 2 + u
                        pool.wait_ge(xT_done.sem, xT_done.after(tile, -3))
                        pool.tensor_copy(idx[:, u:u + 1], t.slot_tok[:, bass.ds(tile, 1)]).then_inc(idx_done.sem, 1)
                        pool.wait_ge(idx_done.sem, idx_done.after(tile, 0))
                        own_wait(pool, t)
                        pool.indirect_dma_start(rows[:, u, :], None, t.h2[:, :],
                                                bass.IndirectOffsetOnAxis(ap=idx[:, u:u + 1], axis=0))\
                            .then_inc(rows_loaded[u], 16)

            @block.tensor
            def _(pe):
                for c in (xT_done, gu_done, aT_done, y_done):
                    pe.sem_inc(c.sem, 2 * c.per)

                def turn_rows(tile, u, turn):
                    pe.wait_ge(rows_loaded[u], turn * 16 + 16)
                    for half in range(2):
                        pe.wait_ge(xT_kept.sem, xT_kept.after(tile, half - 2))
                        for k in range(4):
                            last = pe.transpose(xT_ps[:, half, k * P:(k + 1) * P],
                                                rows[:, u, (4 * half + k) * P:(4 * half + k + 1) * P], t.ident[:, :])
                        last.then_inc(xT_done.sem, 1)

                def gate_up(tile, u, turn):
                    pe.wait_ge(xT_kept.sem, xT_kept.after(tile, 1))
                    pe.wait_ge(gu_loaded[u], turn * 32 + 32)
                    pe.wait_ge(a_done.sem, a_done.after(tile, -2))
                    for k in range(KC):
                        last = pe.matmul(gu_ps[:, u, :], xT[:, u, k, :], w_gu[:, u, k, :, :],
                                         start=(k == 0), stop=(k == KC - 1))
                    last.then_inc(gu_done.sem, 1)

                def turn_act(tile, u):
                    pe.wait_ge(a_done.sem, a_done.after(tile, 0))
                    pe.wait_ge(aT_kept.sem, aT_kept.after(tile, -1))
                    for k in range(FK):
                        last = pe.transpose(aT_ps[:, k * P:(k + 1) * P], act_rows[:, u, k * P:(k + 1) * P], t.ident[:, :])
                    last.then_inc(aT_done.sem, 1)

                def down(tile, u, turn):
                    pe.wait_ge(aT_kept.sem, aT_kept.after(tile, 0))
                    pe.wait_ge(dn_loaded[u], turn * 16 + 16)
                    for c in range(2):
                        pe.wait_ge(y_kept[c].sem, y_kept[c].after(tile, -1))
                        for k in range(FK):
                            last = pe.matmul(y_ps[:, c, :], aT[:, u, k, :], w_dn[:, u, k, c * BANK:(c + 1) * BANK],
                                             start=(k == 0), stop=(k == FK - 1))
                        last.then_inc(y_done.sem, 1)

                turn_rows(0, 0, 0)
                gate_up(0, 0, 0)
                turn_rows(1, 1, 0)
                turn_act(0, 0)

                def step(tile, u, turn):
                    gate_up(tile, u, turn)
                    down(tile - 1, 1 - u, turn if u == 1 else turn - 1)
                    turn_rows(tile + 1, 1 - u, turn if u == 0 else turn + 1)
                    turn_act(tile, u)

                tiles(pe, step)
                half = MOE_TILES // 2
                gate_up(LAST, 1, half - 1)
                down(LAST - 1, 0, half - 1)
                turn_act(LAST, 1)
                down(LAST, 1, half - 1)

            @block.vector
            def _(dve):
                for c in (a_done, xT_kept, y_kept[1]):
                    dve.sem_inc(c.sem, 2 * c.per)

                def keep_rows(tile, u):
                    for half in range(2):
                        dve.wait_ge(xT_done.sem, xT_done.after(tile, half))
                        dve.wait_ge(gu_done.sem, gu_done.after(tile, -2))
                        dve.tensor_copy(xT[:, u, 4 * half:4 * half + 4, :], xT_ps[:, half, :]).then_inc(xT_kept.sem, 1)

                def multiply(tile, u):
                    dve.wait_ge(silu.sem, silu.after(tile, 0))
                    dve.wait_ge(aT_done.sem, aT_done.after(tile, -2))
                    dve.tensor_tensor(act_rows[:, u, :], gu_ps[:, u, D_EXPERT:GU], gate[:, u, :], ALU.mult)\
                       .then_inc(a_done.sem, 1)

                def keep_y(tile, u, turn):
                    dve.wait_ge(y_done.sem, y_done.after(tile, 1))
                    dve.wait_ge(y_stored[u], turn * 16 + 16)
                    dve.tensor_copy(y[:, u, BANK:D_MODEL], y_ps[:, 1, :]).then_inc(y_kept[1].sem, 1)

                keep_rows(0, 0)
                multiply(0, 0)
                keep_rows(1, 1)

                def step(tile, u, turn):
                    multiply(tile, u)
                    keep_y(tile - 1, 1 - u, turn if u == 1 else turn - 1)
                    keep_rows(tile + 1, 1 - u)

                tiles(dve, step)
                half = MOE_TILES // 2
                multiply(LAST, 1)
                keep_y(LAST - 1, 0, half - 1)
                keep_y(LAST, 1, half - 1)

            @block.scalar
            def _(act):
                for c in (silu, aT_kept, y_kept[0]):
                    act.sem_inc(c.sem, 2 * c.per)
                for u in range(2):
                    act.sem_inc(y_stored[u], 16)

                def swish(tile, u):
                    act.wait_ge(gu_done.sem, gu_done.after(tile, 0))
                    act.wait_ge(a_done.sem, a_done.after(tile, -2))
                    act.activation(gate[:, u, :], gu_ps[:, u, 0:D_EXPERT], ACT.Silu).then_inc(silu.sem, 1)

                def keep_act(tile, u):
                    act.wait_ge(aT_done.sem, aT_done.after(tile, 0))
                    act.wait_ge(y_done.sem, y_done.after(tile, -3))
                    act.activation(aT[:, u, :, :], aT_ps[:, 0:FK * P], ACT.Copy).then_inc(aT_kept.sem, 1)

                def keep_y(tile, u, turn):
                    act.wait_ge(y_done.sem, y_done.after(tile, 0))
                    act.wait_ge(y_stored[u], turn * 16 + 16)
                    act.activation(y[:, u, 0:BANK], y_ps[:, 0, :], ACT.Copy).then_inc(y_kept[0].sem, 1)

                def store_y(tile, u):
                    act.wait_ge(y_kept[0].sem, y_kept[0].after(tile, 0))
                    act.wait_ge(y_kept[1].sem, y_kept[1].after(tile, 0))
                    act.dma_start(row_tile(t.moe_out, tile), y[:, u, :]).then_inc(y_stored[u], 16)

                swish(0, 0)
                keep_act(0, 0)

                def step(tile, u, turn):
                    swish(tile, u)
                    keep_y(tile - 1, 1 - u, turn if u == 1 else turn - 1)
                    keep_act(tile, u)
                    store_y(tile - 1, 1 - u)

                tiles(act, step)
                half = MOE_TILES // 2
                swish(LAST, 1)
                keep_y(LAST - 1, 0, half - 1)
                keep_act(LAST, 1)
                store_y(LAST - 1, 0)
                keep_y(LAST, 1, half - 1)
                store_y(LAST, 1)
                for u in range(2):
                    act.wait_ge(y_stored[u], 16 * (half + 1))

        clear(nc, sems)


def combine(nc, t):
    with ExitStack() as ctx:
        sems = []

        def sb(name, shape, dt=F32):
            return ctx.enter_context(nc.sbuf_tensor(name, shape, dt))

        def sem(name):
            sems.append(ctx.enter_context(nc.semaphore(name)))
            return sems[-1]

        x = sb("x1_again", [P, 2, D_MODEL])
        rows = sb("expert_rows", [P, 2, TOP_K, D_MODEL])
        idx = sb("slots_now", [P, 2, 2], I32)
        g_row = sb("g_final_row", [P, D_MODEL])
        square = sb("square3", [P, D_MODEL])
        out = sb("out_rows", [P, 2, D_MODEL])
        ss = sb("sum_squares3", [P, 2, 3])
        g_loaded = sem("g_final_loaded")
        x_loaded = [sem(f"x1_loaded{u}") for u in range(2)]
        rows_loaded = [sem(f"expert_rows_loaded{u}") for u in range(2)]
        stored = [sem(f"out_stored{u}") for u in range(2)]
        idx_done = Count(sem("slots_now_done"), 2)
        sums = Count(sem("expert_rows_added"), 4)
        squares = Count(sem("squares3_done"), 2)
        rstd_step = Count(sem("rstd3_step"), 2)
        rstd = Count(sem("rstd3_done"), 2)
        normed = Count(sem("out_done"), 2)

        with nc.Block() as block:

            @block.sync
            def _(sp):
                sp.dma_start(g_row[:, :], t.g_final.partition_broadcast(P)).then_inc(g_loaded, 16)
                for u in range(2):
                    sp.sem_inc(stored[u], 16)
                sp.dma_start(x[:, 0, :], row_tile(t.x1, 0)).then_inc(x_loaded[0], 16)

                def tile(it, u, final=False):
                    if not final:
                        sp.wait_ge(normed.sem, normed.after(it, u - 1))
                        sp.dma_start(x[:, 1 - u, :], row_tile(t.x1, it * 2 + u + 1)).then_inc(x_loaded[1 - u], 16)
                    sp.wait_ge(normed.sem, normed.after(it, u))
                    sp.dma_start(row_tile(t.y, it * 2 + u), out[:, u, :]).then_inc(stored[u], 16)

                with sp.Fori(0, PT // 2) as it:
                    for u in range(2):
                        tile(it, u)
                tile(PT // 2, 0, final=True)
                sp.wait_ge(stored[0], 16 * (2 + PT // 2))
                sp.wait_ge(stored[1], 16 * (1 + PT // 2))

            @block.gpsimd
            def _(pool):
                for c in (idx_done, rstd_step, rstd):
                    pool.sem_inc(c.sem, c.per)

                def gather(it, u):
                    pool.wait_ge(sums.sem, sums.after(it, 2 * (u - 2) + 1))
                    pool.tensor_copy(idx[:, u, :], t.slots[:, bass.ds((it * 2 + u) * 2, 2)]).then_inc(idx_done.sem, 1)
                    pool.wait_ge(idx_done.sem, idx_done.after(it, u))
                    own_wait(pool, t)
                    for k in range(TOP_K):
                        pool.indirect_dma_start(rows[:, u, k, :], None, t.moe_out[:, :],
                                                bass.IndirectOffsetOnAxis(ap=idx[:, u, k:k + 1], axis=0))\
                            .then_inc(rows_loaded[u], 16)

                def tile(it, u, final=False):
                    if not final:
                        gather(it + u, 1 - u)
                    pool.wait_ge(squares.sem, squares.after(it, u))
                    own_wait(pool, t)
                    pool.tensor_scalar(ss[:, u, 1:2], ss[:, u, 0:1], 1.0 / D_MODEL, NORM_EPS, ALU.mult, ALU.add)\
                        .then_inc(rstd_step.sem, 1)
                    pool.wait_ge(rstd_step.sem, rstd_step.after(it, u))
                    pool.wait_ge(normed.sem, normed.after(it, u - 2))
                    pool.tensor_tensor(ss[:, u, 2:3], ss[:, u, 1:2], t.neg_half[:, :], ALU.pow).then_inc(rstd.sem, 1)

                gather(0, 0)
                with pool.Fori(0, PT // 2) as it:
                    for u in range(2):
                        tile(it, u)
                tile(PT // 2, 0, final=True)

            @block.vector
            def _(dve):
                for c in (sums, normed):
                    dve.sem_inc(c.sem, c.per)
                dve.wait_ge(g_loaded, 16)

                def add(it, u):
                    dve.wait_ge(x_loaded[u], it * 16 + 16)
                    dve.wait_ge(rows_loaded[u], it * 32 + 32)
                    for k in range(TOP_K):
                        if k:
                            dve.wait_ge(sums.sem, sums.after(it, 2 * u + k - 1))
                        dve.scalar_tensor_tensor(x[:, u, :], rows[:, u, k, :], t.gates[:, k, bass.ds(it * 2 + u, 1)],
                                                 x[:, u, :], ALU.mult, ALU.add).then_inc(sums.sem, 1)

                def tile(it, u, final=False):
                    if not final:
                        add(it + u, 1 - u)
                    dve.wait_ge(rstd.sem, rstd.after(it, u))
                    dve.wait_ge(stored[u], it * 16 + 16)
                    dve.wait_ge(sums.sem, sums.after(it, 2 * u + 1))
                    dve.scalar_tensor_tensor(out[:, u, :], x[:, u, :], ss[:, u, 2:3], g_row[:, :], ALU.mult, ALU.mult)\
                       .then_inc(normed.sem, 1)

                add(0, 0)
                with dve.Fori(0, PT // 2) as it:
                    for u in range(2):
                        tile(it, u)
                tile(PT // 2, 0, final=True)

            @block.scalar
            def _(act):
                act.sem_inc(squares.sem, squares.per)

                def tile(it, u):
                    act.wait_ge(sums.sem, sums.after(it, 2 * u + 1))
                    act.wait_ge(squares.sem, squares.after(it, u - 1))
                    act.activation(square[:, :], x[:, u, :], ACT.Square, accum_out=ss[:, u, 0:1])\
                       .then_inc(squares.sem, 1)

                tile_loop(act, tile)

        clear(nc, sems)


def buckets_of(n):
    exact = N_BUCKETS // 2
    ratio = np.maximum(n, 1).astype(np.float32) / np.float32(exact)
    large = exact + (np.log(ratio) / np.float32(math.log(MAX_DISTANCE / exact)) * np.float32(N_BUCKETS - exact))\
        .astype(np.int32)
    return np.where(n < exact, n, np.minimum(large, N_BUCKETS - 1))


def host_constants():
    n = 2 * P - 1 - np.arange(DIST)
    table = np.zeros((N_BUCKETS + 2, DIST), np.float32)
    seen = n >= 0
    table[buckets_of(np.maximum(n, 0))[seen], np.arange(DIST)[seen]] += 1
    table[N_BUCKETS - 1, seen] -= 1
    table[N_BUCKETS, n < 0] = NEG
    table[N_BUCKETS + 1, n <= 0] = NEG
    mask_rows = np.zeros((2, H_DIFF + 1), np.float32)
    mask_rows[0, :H_DIFF] = 1
    mask_rows[1, H_DIFF] = 1
    half = np.arange(P) // DEC_SEQ % 2
    half_map = np.stack([1 - half, half], 1).astype(np.float32)
    e = N_EXPERTS
    rank = np.tile(np.arange(N_GROUPS, 0, -1, dtype=np.float32), (TILES, 1))
    limits = np.tile(P * np.arange(TILES, dtype=np.float32), (e, 1))
    tile_no = np.repeat(np.arange(MOE_TILES, dtype=np.float32)[:, None], e, 1)
    spare = np.zeros((P, TILES), np.float32)
    spare[N_SAMPLE:, PT] = N_SLOTS + np.arange(N_SAMPLE, P)
    before = np.triu(np.ones((P, P), np.float32), 1)
    token = (np.arange(TILES)[None] * P + np.arange(P)[:, None]).astype(np.float32)
    more = {"rank_const": rank, "limits_const": limits, "tile_no_const": tile_no, "spare_const": spare,
            "before_const": before, "token_const": token,
            "column_const": np.arange(P, dtype=np.float32)}
    return more | {"bucket_table": table, "mask_rows": mask_rows, "half_map": half_map, "eye": np.eye(P, dtype=np.float32)}


INPUTS = ["x", "cache_d", "cache_s", "page_table", "rel_bias", "g_mix", "w_in", "lambda_q1", "lambda_k1", "lambda_q2",
          "lambda_k2", "subln_g", "w_out", "g_ffn", "w_group", "b_group", "w_erouter", "b_erouter", "w_gate", "w_up",
          "w_down", "g_final", "eye", "bucket_table", "mask_rows", "half_map", "rank_const", "limits_const",
          "tile_no_const", "column_const", "spare_const", "before_const", "token_const"]
OUTPUTS = ["y", "new_kvd", "new_kvs"]


def step_kernel(nc, t):
    def scratch(name, shape, dt=F32):
        return nc.dram_tensor(name, shape, dt).ap()

    t.n_pool = t.cache_d.shape[0]
    t.qT = scratch("scratch_qT", (P, BLOCKS, ALL))
    t.kT = scratch("scratch_kT", (P, BLOCKS, ALL))
    t.oT = scratch("scratch_oT", (P, BLOCKS, ALL))
    t.bias_dram = scratch("scratch_bias", (H_DIFF + 1, P, DIST))
    t.near_dram = scratch("scratch_near", (H_DIFF, P, NEAR))
    t.x1 = scratch("scratch_x1", (ALL, D_MODEL))
    t.h2 = scratch("scratch_h2", (ALL, D_MODEL))
    t.moe_out = scratch("scratch_moe_out", (N_SLOTS + P, D_MODEL))
    with ExitStack() as ctx:
        constants(nc, ctx, t)
        project(nc, t)
        with ExitStack() as att:
            t.sample_o = att.enter_context(nc.sbuf_tensor("sample_o", [P, DEC_BATCH, P], F32))
            tables(nc, att, t)
            attention(nc, t, DIFF)
            attention(nc, t, STICK)
            sample_heads_out(nc, t)
        t.logits = ctx.enter_context(nc.sbuf_tensor("logits", [P, TILES, N_LOGITS], F32))
        t.gates = ctx.enter_context(nc.sbuf_tensor("gates", [P, TOP_K, TILES], F32))
        t.slots = ctx.enter_context(nc.sbuf_tensor("slots", [P, TOP_K * TILES], I32))
        t.slot_tok = ctx.enter_context(nc.sbuf_tensor("slot_tok", [P, MOE_TILES], I32))
        t.tile_expert = ctx.enter_context(nc.sbuf_tensor("tile_expert", [1, MOE_TILES], I32))
        mix_out(nc, t)
        route(nc, t)
        experts(nc, t)
        combine(nc, t)


def kernel(**inputs):
    import concourse.bacc as bacc
    from types import SimpleNamespace
    from concourse.bass_utils import run_bass_kernel_spmd

    a = {k: np.asarray(v) for k, v in inputs.items()}
    n_pool = a["cache_kv_diff"].shape[0]
    host = host_constants()
    host["x"] = np.concatenate([a["x_prompt"].reshape(SEQ, D_MODEL), a["x_sample"].reshape(N_SAMPLE, D_MODEL),
                                np.zeros((ALL - SEQ - N_SAMPLE, D_MODEL), a["x_prompt"].dtype)])
    host["cache_d"] = a["cache_kv_diff"].reshape(n_pool, PAGE, 2 * HALF_W)
    host["cache_s"] = a["cache_kv_sb"].reshape(n_pool, PAGE, 2 * HALF_W)
    host["w_erouter"] = a["w_erouter"][0].reshape(D_MODEL, N_EXPERTS)
    host["b_erouter"] = a["b_erouter"][0].reshape(N_EXPERTS)
    for name in ("w_gate", "w_up"):
        host[name] = a[name][0].reshape(N_EXPERTS, D_MODEL, D_EXPERT)
    host["w_down"] = a["w_down"][0].reshape(N_EXPERTS, D_EXPERT, D_MODEL)
    for name in ("page_table", "rel_bias", "g_final"):
        host[name] = a[name]
    for name in ("g_mix", "w_in", "lambda_q1", "lambda_k1", "lambda_q2", "lambda_k2", "subln_g", "w_out", "g_ffn",
                 "w_group", "b_group"):
        host[name] = a[name][0]

    nc = bacc.Bacc("TRN2", target_bir_lowering=False, num_devices=1)
    arrays, dram = {}, {}
    for name in INPUTS:
        arrays[f"in_{name}"] = np.ascontiguousarray(host[name])
        dram[name] = nc.dram_tensor(f"in_{name}", host[name].shape, mybir.dt.from_np(host[name].dtype),
                                    kind="ExternalInput").ap()
    for name in OUTPUTS:
        dram[name] = nc.dram_tensor(f"out_{name}", (ALL, D_MODEL), F32, kind="ExternalOutput").ap()
    step_kernel(nc, SimpleNamespace(**dram))
    r = run_bass_kernel_spmd(nc, [arrays], core_ids=[0]).results[0]

    def rows(name, *shape):
        out = r[f"out_{name}"]
        return out[0:SEQ].reshape(1, SEQ, *shape), out[SEQ:SEQ + N_SAMPLE].reshape(DEC_BATCH, DEC_SEQ, *shape)

    y_p, y_s = rows("y", D_MODEL)
    kvd_p, kvd_s = rows("new_kvd", 1, 2, H_DIFF, 2 * HEAD)
    kvs_p, kvs_s = rows("new_kvs", 1, 2, H_SB, HEAD)
    return y_p, y_s, kvd_p, kvs_p, kvd_s, kvs_s
```

```python
import math
from contextlib import ExitStack

import numpy as np
import concourse.bass as bass
from concourse import mybir
from concourse.alu_op_type import AluOpType as ALU

ACT = mybir.ActivationFunctionType
AX = mybir.AxisListType
F32 = mybir.dt.float32
I32 = mybir.dt.int32
F32R = mybir.dt.float32r

D_MODEL = 1024
SEQ = 1024
DEC_BATCH, DEC_SEQ = 8, 8
PAST_LEN, PAGE = 2048, 128
N_PAGES = PAST_LEN // PAGE
HEAD = 64
H_DIFF, H_SB = 4, 8
HALF_W = H_DIFF * 2 * HEAD
MIX_W = 2 * HALF_W
N_BUCKETS, MAX_DISTANCE = 32, 128
N_GROUPS, PER_GROUP = 4, 4
N_EXPERTS = N_GROUPS * PER_GROUP
TOP_K = 2
D_EXPERT = 256
NORM_EPS, SUBLN_EPS = 1e-6, 1e-5
LAMBDA_INIT = 0.8 - 0.6 * math.exp(-0.3 * 0)

P = 128
KC = D_MODEL // P
N_SAMPLE = DEC_BATCH * DEC_SEQ
PT = SEQ // P
TILES = PT + 1
BANK = 512
PROJ_G = 3 * MIX_W // BANK
BLOCKS = MIX_W // P
NEAR = 2 * P
DIST = 3 * P
NEG = -1e30
MOE_TILES = (TOP_K * (SEQ + N_SAMPLE) + N_EXPERTS * (P - 1)) // P


class Count:

    def __init__(self, sem, per):
        self.sem, self.per = sem, per

    def after(self, turn, k):
        assert -self.per <= k < self.per
        return turn * self.per + (self.per + k + 1)



def constants(nc, ctx, t):
    t.ident = ctx.enter_context(nc.sbuf_tensor("ident", [P, P], F32))
    t.ones = ctx.enter_context(nc.sbuf_tensor("ones", [P, P], F32))
    t.neg_half = ctx.enter_context(nc.sbuf_tensor("neg_half", [P, 1], F32))
    t.waits_passed = ctx.enter_context(nc.semaphore("waits_passed"))
    t.const_ready = ctx.enter_context(nc.semaphore("const_ready"))
    with nc.Block() as block:

        @block.sync
        def _(sp):
            sp.dma_start(t.ident[:, :], t.eye).then_inc(t.const_ready, 16)

        @block.gpsimd
        def _(pool):
            pool.memset(t.neg_half[:, :], -0.5)
            pool.memset(t.ones[:, :], 1.0)


def own_wait(engine, t):
    engine.sem_inc(t.waits_passed, 1)


def clear(nc, sems):
    with nc.Block() as block:

        @block.gpsimd
        def _(pool):
            for one in sems:
                pool.sem_clear(one)


def project(nc, t):
    with ExitStack() as ctx:
        sems = []

        def sb(name, shape, dt=F32):
            return ctx.enter_context(nc.sbuf_tensor(name, shape, dt))

        def ps(name, shape):
            return ctx.enter_context(nc.psum_tensor(name, shape, F32))

        def sem(name):
            sems.append(ctx.enter_context(nc.semaphore(name)))
            return sems[-1]

        ROLES = 3
        STEPS = ROLES * TILES
        TURNED = 2 * TILES
        assert STEPS % 3 == 0 and TURNED % 3 == 0 and TILES % 3 == 0

        x = sb("x_tiles", [P, TILES, D_MODEL])
        g_T = sb("g_mix_T", [P, KC])
        square = sb("square", [P, D_MODEL])
        ss = sb("sum_squares", [P, 4, TILES])
        hT = sb("x_times_g_T", [P, 2, 4, P])
        hT_hi = sb("h_T_hi", [P, TILES, KC, P], F32R)
        hT_lo = sb("h_T_lo", [P, TILES, KC, P], F32R)
        w_raw = sb("w_in_now", [P, KC, BANK])
        w_hi = sb("w_in_hi", [P, KC, BANK], F32R)
        w_lo = sb("w_in_lo", [P, KC, BANK], F32R)
        proj = sb("proj_rows", [P, 3, BANK])
        qkT = sb("qk_transposed", [P, 3, 4, P])
        xT_ps = ps("xT_ps", [P, 2, BANK])
        pj_ps = ps("proj_ps", [P, 3, BANK])
        tr_ps = ps("qkT_ps", [P, 3, BANK])

        x_loaded = [sem(f"x_loaded{n}") for n in range(TILES)]
        g_loaded = sem("g_mix_loaded")
        w_loaded = [sem(f"w_in_loaded{k}") for k in range(KC)]
        xT_done, hT_done, hi_done, lo_done = sem("xT_in_psum"), sem("hT_done"), sem("hT_hi_done"), sem("hT_lo_done")
        squares, rstd_step, rstd = sem("squares_done"), sem("rstd_step"), sem("rstd_done")
        w_hi_done = Count(sem("w_in_hi_done"), ROLES * KC)
        w_lo_done = Count(sem("w_in_lo_done"), ROLES * KC)
        w_used = Count(sem("w_in_used"), ROLES * (KC - 1))
        pj_done = Count(sem("proj_in_psum"), STEPS)
        pj_kept = Count(sem("proj_kept"), STEPS)
        tr_done = Count(sem("qkT_in_psum"), TURNED)
        tr_kept = Count(sem("qkT_kept"), TURNED)
        rows_stored = [sem(f"rows_stored{u}") for u in range(3)]
        qkT_stored = [sem(f"qkT_stored{u}") for u in range(3)]
        w_view = t.w_in.rearrange("(k p) n -> k p n", p=P)
        tables = Tables(nc, ctx, sems, t, [pj_ps[:, n, :] for n in range(3)] + [tr_ps[:, n, :] for n in range(2)])

        def load_w(sp, k, turn, role):
            sp.dma_start(w_raw[:, k, :], w_view[k, :, bass.ds(turn * (ROLES * BANK) + role * BANK, BANK)])\
              .then_inc(w_loaded[k], 16)

        def rows_free(turn, n):
            return turn * (16 * TURNED // 3) + 16 * (1 + len(range(TILES + n % 3, n, 3)))

        with nc.Block() as block:

            @block.sync
            def _(sp):
                for n in range(TILES):
                    sp.dma_start(x[:, n, :], t.x[n * P:(n + 1) * P, :]).then_inc(x_loaded[n], 16)
                    if n < KC:
                        sp.dma_start(w_raw[:, n, :], w_view[n, :, 0:BANK]).then_inc(w_loaded[n], 16)
                tables.loads(sp)
                tables.spread(sp)
                for u in range(3):
                    sp.sem_inc(rows_stored[u], 16)
                    sp.sem_inc(qkT_stored[u], 16)

                def next_w(it, role):
                    for k in range(KC):
                        sp.wait_ge(w_lo_done.sem, w_lo_done.after(it, role * KC + k))
                        own_wait(sp, t)
                        load_w(sp, k, it + (role + 1) // ROLES, (role + 1) % ROLES)

                def store(it, role, tile):
                    n = role * TILES + tile
                    if role > 0:
                        sp.wait_ge(pj_kept.sem, pj_kept.after(it, n))
                        own_wait(sp, t)
                        dst = (t.new_kvd, t.new_kvs)[it]
                        sp.dma_start(dst[tile * P:(tile + 1) * P, (role - 1) * HALF_W:role * HALF_W],
                                     proj[:, n % 3, :]).then_inc(rows_stored[n % 3], 16)
                    if role < 2:
                        sp.wait_ge(tr_kept.sem, tr_kept.after(it, n))
                        own_wait(sp, t)
                        dst = (t.qT, t.kT)[role]
                        sp.dma_start(dst[:, it * 4:it * 4 + 4, tile * P:(tile + 1) * P], qkT[:, n % 3, :, :])\
                          .then_inc(qkT_stored[n % 3], 16)

                for it in range(2):
                    for role in range(ROLES):
                        if it * ROLES + role + 1 < 2 * ROLES:
                            next_w(it, role)
                        for tile in range(TILES):
                            store(it, role, tile)
                tables.loads_done(sp)
                for u in range(3):
                    sp.wait_ge(rows_stored[u], rows_free(2, 0))
                    sp.wait_ge(qkT_stored[u], 2 * (16 * TURNED // 3) + 16)

            @block.gpsimd
            def _(pool):
                pool.wait_ge(squares, TILES)
                pool.tensor_scalar(ss[:, 1, :], ss[:, 0, :], 1.0 / D_MODEL, NORM_EPS, ALU.mult, ALU.add)\
                    .then_inc(rstd_step, 1)
                for n in range(TILES):
                    if n == 0:
                        pool.wait_ge(rstd_step, 1)
                    pool.tensor_tensor(ss[:, 2, n:n + 1], ss[:, 1, n:n + 1], t.neg_half[:, :], ALU.pow)\
                        .then_inc(rstd_step, 1)
                pool.wait_ge(rstd_step, 1 + TILES)
                pool.tensor_scalar(ss[:, 3, :], ss[:, 2, :], HEAD ** -0.5, 0.0, ALU.mult, ALU.add).then_inc(rstd, 1)

            @block.tensor
            def _(pe):
                for c in (w_used, pj_done, tr_done):
                    pe.sem_inc(c.sem, c.per)
                pe.wait_ge(t.const_ready, 16)
                for n in range(TILES):
                    pe.wait_ge(x_loaded[n], 16)
                    for half in range(2):
                        m = 2 * n + half
                        if m >= 2:
                            pe.wait_ge(hT_done, m - 1)
                        for k in range(4):
                            last = pe.transpose(xT_ps[:, half, k * P:(k + 1) * P],
                                                x[:, n, (4 * half + k) * P:(4 * half + k + 1) * P], t.ident[:, :])
                        last.then_inc(xT_done, 1)
                tables.bias(pe)
                pe.wait_ge(tables.bias_kept, H_DIFF + 1)

                def turn(it, n):
                    pe.wait_ge(pj_kept.sem, pj_kept.after(it, n))
                    pe.wait_ge(tr_kept.sem, tr_kept.after(it, n - 3))
                    for b in range(4):
                        last = pe.transpose(tr_ps[:, n % 3, b * P:(b + 1) * P], proj[:, n % 3, b * P:(b + 1) * P],
                                            t.ident[:, :])
                    last.then_inc(tr_done.sem, 1)

                def step(it, role, tile):
                    n = role * TILES + tile
                    pe.wait_ge(lo_done, 2 * tile + 2)
                    pe.wait_ge(pj_kept.sem, pj_kept.after(it, n - 3))
                    for k in range(KC):
                        if tile == 0:
                            pe.wait_ge(w_lo_done.sem, w_lo_done.after(it, role * KC + k))
                        for m, (a, b) in enumerate(((hT_hi, w_hi), (hT_lo, w_hi), (hT_hi, w_lo))):
                            last = pe.matmul(pj_ps[:, n % 3, :], a[:, tile, k, :], b[:, k, :],
                                             start=(k == 0 and m == 0), stop=(k == KC - 1 and m == 2))
                        if tile == TILES - 1 and k < KC - 1:
                            last.then_inc(w_used.sem, 1)
                    last.then_inc(pj_done.sem, 1)

                with pe.Fori(0, 2) as it:
                    for role in range(ROLES):
                        for tile in range(TILES):
                            step(it, role, tile)
                            if role < 2 and tile > 0:
                                turn(it, role * TILES + tile - 1)
                        if role < 2:
                            turn(it, role * TILES + TILES - 1)

            @block.vector
            def _(dve):
                for c in (w_lo_done, tr_kept):
                    dve.sem_inc(c.sem, c.per)
                tables.zeros(dve)
                dve.wait_ge(g_loaded, 16)

                def low(n, half):
                    m = 2 * n + half
                    dve.wait_ge(hi_done, m + 1)
                    at = slice(4 * half, 4 * half + 4)
                    dve.tensor_tensor(hT_lo[:, n, at, :], hT[:, half, :, :], hT_hi[:, n, at, :].bitcast(F32),
                                      ALU.subtract).then_inc(lo_done, 1)

                for n in range(TILES):
                    for half in range(2):
                        m = 2 * n + half
                        dve.wait_ge(xT_done, m + 1)
                        if m >= 2:
                            dve.wait_ge(lo_done, m - 1)
                        dve.tensor_tensor(hT[:, half, :, :], xT_ps[:, half, :].rearrange("p (k c) -> p k c", c=P),
                                          g_T[:, 4 * half:4 * half + 4].unsqueeze(2).broadcast_to([P, 4, P]), ALU.mult)\
                           .then_inc(hT_done, 1)
                        if m >= 1:
                            low((m - 1) // 2, (m - 1) % 2)
                    if n == TILES - 3:
                        tables.widen(dve)
                low(TILES - 1, 1)
                tables.rest(dve)

                with dve.Fori(0, 2) as it:
                    for role in range(ROLES):
                        for k in range(KC):
                            dve.wait_ge(w_hi_done.sem, w_hi_done.after(it, role * KC + k))
                            dve.tensor_tensor(w_lo[:, k, :], w_raw[:, k, :], w_hi[:, k, :].bitcast(F32), ALU.subtract)\
                               .then_inc(w_lo_done.sem, 1)
                        if role == 2:
                            continue
                        for tile in range(TILES):
                            n = role * TILES + tile
                            dve.wait_ge(tr_done.sem, tr_done.after(it, n))
                            dve.wait_ge(qkT_stored[n % 3], it * (16 * TURNED // 3) + 16 * (1 + n // 3))
                            dve.tensor_copy(qkT[:, n % 3, :, :], tr_ps[:, n % 3, :]).then_inc(tr_kept.sem, 1)

            @block.scalar
            def _(act):
                for c in (w_hi_done, pj_kept):
                    act.sem_inc(c.sem, c.per)
                with nc.allow_non_contiguous_dma(reason="one small vector"):
                    act.dma_start(g_T[:, :], t.g_mix.rearrange("(k p) -> p k", p=P)).then_inc(g_loaded, 16)
                for n in range(TILES):
                    for half in range(2):
                        m = 2 * n + half
                        act.wait_ge(hT_done, m + 1)
                        act.activation(hT_hi[:, n, 4 * half:4 * half + 4, :], hT[:, half, :, :], ACT.Copy)\
                           .then_inc(hi_done, 1)
                    if n:
                        act.wait_ge(squares, n)
                    act.activation(square[:, :], x[:, n, :], ACT.Square, accum_out=ss[:, 0, n:n + 1])\
                       .then_inc(squares, 1)
                tables.exps_of_sums(act)

                with act.Fori(0, 2) as it:
                    for role in range(ROLES):
                        for k in range(KC):
                            act.wait_ge(w_loaded[k], it * (16 * ROLES) + 16 * (role + 1))
                            if k < KC - 1:
                                act.wait_ge(w_used.sem, w_used.after(it, (role - 1) * (KC - 1) + k))
                            else:
                                act.wait_ge(pj_done.sem, pj_done.after(it, role * TILES - 1))
                            act.activation(w_hi[:, k, :], w_raw[:, k, :], ACT.Copy).then_inc(w_hi_done.sem, 1)
                        if role == 0:
                            act.wait_ge(rstd, 1)
                        for tile in range(TILES):
                            n = role * TILES + tile
                            act.wait_ge(pj_done.sem, pj_done.after(it, n))
                            act.wait_ge(rows_stored[n % 3], rows_free(it, n))
                            if 3 <= n < TURNED + 3:
                                act.wait_ge(tr_done.sem, tr_done.after(it, n - 3))
                            act.activation(proj[:, n % 3, :], pj_ps[:, n % 3, :], ACT.Copy,
                                           scale=ss[:, 3 if role == 0 else 2, tile:tile + 1]).then_inc(pj_kept.sem, 1)

        clear(nc, sems)


def table_places(nc, ctx, t):
    def keep(name, shape, dt=F32):
        return ctx.enter_context(nc.sbuf_tensor(name, shape, dt))

    t.q_heads = keep("sample_q_by_head", [P, DEC_BATCH, BLOCKS, 2, DEC_SEQ])
    t.near_dec = keep("near_bias_sample", [P, PAGE + DEC_SEQ])
    t.neg_lambda = keep("neg_lambda", [P, 1])
    t.row_factor = keep("row_factor", [P, 1])
    t.sub_g = keep("sub_g", [P, 1])
    t.pages = keep("page_ids", [1, DEC_BATCH * N_PAGES], I32)


class Tables:

    def __init__(self, nc, ctx, sems, t, banks):
        def sb(name, shape, dt=F32):
            return ctx.enter_context(nc.sbuf_tensor(name, shape, dt))

        def sem(name):
            sems.append(ctx.enter_context(nc.semaphore(name)))
            return sems[-1]

        self.t, self.banks = t, banks
        self.rb = sb("rel_bias_rows", [N_BUCKETS + 2, H_DIFF + 1])
        self.buckets = sb("buckets", [N_BUCKETS + 2, DIST])
        self.rb_wide = sb("rel_bias_wide", [N_BUCKETS + 2, H_DIFF + 1, P])
        self.by_distance = sb("bias_by_distance", [P, H_DIFF + 1, DIST])
        self.lam_in = sb("lambda_in", [P, 4, HEAD])
        self.lam_mul = sb("lambda_products", [P, 2, HEAD])
        self.lam_sum = sb("lambda_sums", [P, 2])
        self.lam_exp = sb("lambda_exps", [P, 2])
        self.halves = sb("map_of_halves", [P, 2])
        self.g_in = sb("subln_in", [P, 1])
        self.zeroed, self.rb_loaded, self.lam_loaded = sem("rb_zeroed"), sem("rb_loaded"), sem("lam_loaded")
        self.bias_done, self.bias_kept, self.bias_stored = sem("bias_done"), sem("bias_kept"), sem("bias_stored")
        self.near_loaded, self.pages_loaded = sem("near_loaded"), sem("pages_loaded")
        self.widened = sem("rel_bias_widened")
        self.step, self.exps = sem("lambda_step"), sem("lambda_exps_done")

    def loads(self, sp):
        t = self.t
        sp.dma_start(self.buckets[:, :], t.bucket_table).then_inc(self.rb_loaded, 16)
        sp.dma_start(self.rb[N_BUCKETS:N_BUCKETS + 2, :], t.mask_rows).then_inc(self.rb_loaded, 16)
        sp.wait_ge(self.zeroed, 1)
        sp.dma_start(self.rb[0:N_BUCKETS, 0:H_DIFF], t.rel_bias).then_inc(self.rb_loaded, 16)
        for n, v in enumerate((t.lambda_q1, t.lambda_k1, t.lambda_q2, t.lambda_k2)):
            sp.dma_start(self.lam_in[:, n, :], v.partition_broadcast(P)).then_inc(self.lam_loaded, 16)
        sp.dma_start(self.g_in[:, :], t.subln_g.rearrange("(p a) -> p a", a=1)).then_inc(self.lam_loaded, 16)
        sp.dma_start(self.halves[:, :], t.half_map).then_inc(self.lam_loaded, 16)
        sp.dma_start(t.pages[:, :], t.page_table.rearrange("(a s) n -> a (s n)", a=1)).then_inc(self.pages_loaded, 16)

    def spread(self, sp):
        t = self.t
        sp.wait_ge(self.bias_kept, H_DIFF + 1)
        sp.dma_start(t.bias_dram.rearrange("h p n -> p h n"), self.by_distance[:, :, :]).then_inc(self.bias_stored, 16)
        sp.wait_ge(self.bias_stored, 16)
        for b in range(BLOCKS):
            for u in range(2):
                row = 2 * DEC_SEQ * b + DEC_SEQ * u
                sp.dma_start(t.near_dec[row:row + DEC_SEQ, :],
                             distances(t, min(b, H_DIFF), DEC_SEQ, PAGE + DEC_SEQ)).then_inc(self.near_loaded, 16)
        for head in range(H_DIFF):
            sp.dma_start(t.near_dram[head], distances(t, head, P, NEAR)).then_inc(self.bias_stored, 16)

    def loads_done(self, sp):
        sp.wait_ge(self.near_loaded, 16 * 2 * BLOCKS)
        sp.wait_ge(self.bias_stored, 16 * (1 + H_DIFF))
        sp.wait_ge(self.pages_loaded, 16)

    def bias(self, pe):
        pe.wait_ge(self.rb_loaded, 48)
        pe.wait_ge(self.widened, 1)
        for head in range(H_DIFF + 1):
            pe.matmul(self.banks[head][:, 0:DIST], self.rb_wide[:, head, :], self.buckets[:, :], start=True, stop=True)\
              .then_inc(self.bias_done, 1)

    def zeros(self, dve):
        dve.memset(self.rb[0:N_BUCKETS, :], 0.0).then_inc(self.zeroed, 1)
        dve.memset(self.t.q_heads[:, :, :, :, :], 0.0).then_inc(self.zeroed, 1)

    def widen(self, dve):
        dve.wait_ge(self.rb_loaded, 48)
        dve.tensor_copy(self.rb_wide[:, :, :], self.rb[:, :].unsqueeze(2).broadcast_to([N_BUCKETS + 2, H_DIFF + 1, P]))\
           .then_inc(self.widened, 1)
        dve.wait_ge(self.lam_loaded, 96)
        for n in range(2):
            dve.tensor_tensor(self.lam_mul[:, n, :], self.lam_in[:, 2 * n, :], self.lam_in[:, 2 * n + 1, :], ALU.mult)\
               .then_inc(self.step, 1)
        dve.wait_ge(self.step, 2)
        dve.tensor_reduce(self.lam_sum[:, :], self.lam_mul[:, :, :], axis=AX.X, op=ALU.add).then_inc(self.step, 1)

    def rest(self, dve):
        t, step = self.t, self.step
        for head in range(H_DIFF + 1):
            dve.wait_ge(self.bias_done, head + 1)
            dve.tensor_copy(self.by_distance[:, head, :], self.banks[head][:, 0:DIST]).then_inc(self.bias_kept, 1)
        dve.wait_ge(self.exps, 1)
        dve.tensor_tensor(t.neg_lambda[:, :], self.lam_exp[:, 1:2], self.lam_exp[:, 0:1], ALU.subtract).then_inc(step, 1)
        dve.wait_ge(step, 4)
        dve.tensor_scalar_add(t.neg_lambda[:, :], t.neg_lambda[:, :], -LAMBDA_INIT).then_inc(step, 1)
        dve.wait_ge(step, 5)
        dve.scalar_tensor_tensor(t.row_factor[:, :], self.halves[:, 1:2], t.neg_lambda[:, 0:1], self.halves[:, 0:1],
                                 ALU.mult, ALU.add)
        dve.tensor_scalar_mul(t.sub_g[:, :], self.g_in[:, :], 1.0 - LAMBDA_INIT)

    def exps_of_sums(self, act):
        act.wait_ge(self.step, 3)
        act.activation(self.lam_exp[:, :], self.lam_sum[:, :], ACT.Exp).then_inc(self.exps, 1)


def distances(t, head, rows, cols):
    return bass.AP(t.bias_dram.tensor, head * P * DIST + P - 1, [[DIST - 1, rows], [1, cols]])


DIFF, STICK = 0, 1
TURNS = 4
K_SLOTS = 4
N_WEIGH = 7
SPANS = {DIFF: ((0.065, 0.4), (0.4, 0.5), (0.52, 0.99)), STICK: ((0.0, 0.33), (0.395, 0.475), (0.55, 1.05))}
WEIGHTS = {DIFF: (1, 1, 1, 2, 1), STICK: (1, 2, 1, 6, 3)}
D_PAGES = N_PAGES + 1
KEYS = PAST_LEN + DEC_SEQ
V_GROUPS = (D_PAGES + 3) // 4
NEW = N_PAGES
S_GROUPS = N_PAGES // 2
S_KEYS = 2 * PAGE + DEC_SEQ
D0 = H_DIFF * 2 * DEC_SEQ


def page_keys(p):
    return PAGE if p < N_PAGES else DEC_SEQ


def group_pages(g):
    return range(4 * g, min(4 * g + 4, D_PAGES))


def score_chunks(kind):
    near = 2 if kind == DIFF else 1
    out = []
    for i in range(PT):
        end, near0 = (i + 1) * P, max(0, (i + 1 - near)) * P
        for u in range(2):
            for k0 in range(0, end, BANK):
                k1 = min(k0 + BANK, end)
                out.append((i, u, k0, k1, min(max(near0, k0), k1)))
    return out


def turned_groups(kind, i):
    blocks = [(u, kb) for u in range(1 if kind == DIFF else 2) for kb in range(i + 1)]
    return [blocks[n:n + 4] for n in range(0, len(blocks), 4)]


def score_group_pages(g):
    return range(2 * g, 2 * g + 2) if g + 1 < S_GROUPS else range(2 * g, D_PAGES)


def attention_plan(kind):
    w_score, w_soft, w_out, w_last, ahead = WEIGHTS[kind]
    n_soft = 3 if kind == DIFF else 6
    chunks = score_chunks(kind)

    def scores(i):
        return [(("score", i, g), w_score) for g, c in enumerate(chunks) if c[0] == i]

    prompt = scores(0) + [(("soft", 0, n), w_soft) for n in range(n_soft)]
    for i in range(PT):
        soft = [(("soft", i + 1, n), w_soft) for n in range(n_soft)] if i + 1 < PT else []
        if i + 1 < PT:
            prompt += scores(i + 1)
        n_out = len(turned_groups(kind, i)) + 1
        outs = [(("out", i, n), w_out) for n in range(n_out - 1)]
        if i:
            outs.append((("turn_out", i - 1), 1))
        outs.append((("out", i, n_out - 1), w_last))
        prompt += soft[:ahead] + outs + soft[ahead:]
    prompt.append((("turn_out", PT - 1), 1))
    pages = []
    for p in range(D_PAGES):
        pages.append((("page", p), 1))
        if p >= 2 and p % 2 == 0 and p < N_PAGES:
            pages += [(("page_scores", p // 2 - 1, part), 2) for part in range(2)]
    pages += [(("page_scores", S_GROUPS - 1, part), 2) for part in range(2)]
    weigh = [(("weigh", n), 1) for n in range(N_WEIGH)]
    use = [(("turn", 0), 1)]
    for g in range(1, V_GROUPS):
        use += [(("turn", g), 1)] + [(("apply", 0, p), 2) for p in group_pages(g - 1)]
    use += [(("apply", 0, p), 2) for p in group_pages(V_GROUPS - 1)] + [(("rows", 0), 0)]
    use += [(("apply", 1, p), 2) for p in range(D_PAGES)] + [(("rows", 1), 0), (("heads", 0), 1)]
    total = sum(w for _, w in prompt)
    timed = []
    for steps, (begin, end) in zip((pages, weigh, use), SPANS[kind]):
        of, done = sum(w for _, w in steps), 0
        for step, w in steps:
            timed.append((begin + (end - begin) * done / of, step))
            done += w
    out, done, taken = [], 0, 0
    for step, w in prompt:
        while taken < len(timed) and timed[taken][0] <= done / total:
            out.append(timed[taken][1])
            taken += 1
        out.append(step)
        done += w
    return out + [step for _, step in timed[taken:]]


def attention(nc, t, kind):
    with ExitStack() as ctx:
        sems = []

        def sb(name, shape, dt=F32):
            return ctx.enter_context(nc.sbuf_tensor(f"{name}_{kind}", shape, dt))

        def ps(name, shape):
            return ctx.enter_context(nc.psum_tensor(f"{name}_{kind}", shape, F32))

        def sem(name):
            sems.append(ctx.enter_context(nc.semaphore(f"{name}_{kind}")))
            return sems[-1]

        def count(name, per):
            return Count(sem(name), per)

        qT = sb("head_qT_halves", [P, 2, SEQ])
        kT = sb("head_kT", [P, SEQ])
        v = sb("head_v", [P, PT, P])
        near = sb("near_bias", [P, NEAR])
        S = sb("scores", [P, 2, 2, SEQ])
        aux = sb("aux", [P, 2, SEQ])
        wT = sb("weights_T", [P, 16, P])
        stat = sb("stats", [P, 4, 8])
        o_rows = sb("o_rows", [P, 2, P])
        o_sq = sb("o_squares", [P, P])
        o_norm = sb("o_normed", [P, P])
        oT = sb("head_oT", [P, SEQ])
        sc_ps = ps("scores_ps", [P, 2, BANK])
        wT_ps = ps("weights_T_ps", [P, 4, P])
        o_ps = ps("o_ps", [P, BANK])
        k_page = sb("k_pages", [P, K_SLOTS, BLOCKS, P])
        v_page = sb("v_pages", [P, D_PAGES, BLOCKS, P])
        kT_page = sb("k_pages_T", [P, 2, BLOCKS, S_KEYS])
        q_block = sb("q_by_block", [P, BLOCKS * (P + 16)])
        sS = sb("sample_scores", [P, KEYS])
        sW = sb("sample_weights", [P, KEYS])
        o_rows_s = sb("sample_o_rows", [P, BANK])
        sT = sb("sample_weights_T", [P, D_PAGES, P])
        sstat = sb("sample_stats", [P, 4])
        kT_ps = ps("k_page_T_ps", [P, 2, 4, P])
        s_ps = ps("page_scores_ps", [P, BANK])
        sO_ps = ps("sample_o_ps", [P, BANK])

        chunks = score_chunks(kind)
        n_chunks = len(chunks)
        assert n_chunks % 2 == 0
        far_upto = np.cumsum([c[4] > c[2] for c in chunks]).tolist()
        near_upto = np.cumsum([c[3] > c[4] for c in chunks]).tolist()
        n_groups = [len(turned_groups(kind, i)) for i in range(PT)]
        groups_upto = np.cumsum(n_groups).tolist()
        plan = attention_plan(kind)

        qk_loaded, v_loaded, near_loaded = sem("qk_loaded"), sem("v_loaded"), sem("near_loaded")
        sc_done = count("scores_in_psum", n_chunks)
        sc_far = count("far_scores_kept", far_upto[-1])
        sc_near = count("near_scores_kept", near_upto[-1])
        row_max = count("row_max", PT)
        exps = count("exps_done", 2 * PT)
        inv_sum = count("inverse_sums", 2 * PT)
        mixed = count("softmaxes_mixed", PT)
        s_abs = count("abs_done", PT)
        s_expm = count("exp_minus_abs", PT)
        s_ln = count("ln_done", PT)
        s_soft = count("softplus_done", PT)
        s_scan = count("suffix_sums_done", 2 * PT)
        s_sub = count("log_weights_done", PT)
        s_exp = count("stick_weights_done", PT)
        w_turned = count("weights_T_in_psum", groups_upto[-1])
        wT_kept = count("weights_T_kept", groups_upto[-1])
        o_done = count("o_in_psum", PT)
        o_kept = count("o_kept", PT)
        o_squared = count("o_squared", PT)
        sub_step = count("sub_norm_step", PT)
        sub_rstd = count("sub_norm_rstd", PT)
        o_normed = count("o_normed_done", PT)
        oT_done = count("oT_in_psum", PT)
        oT_kept = count("oT_kept", PT)
        oT_stored = sem("oT_stored")
        k_loaded = [sem(f"k_page_loaded{n}") for n in range(K_SLOTS)]
        vp_loaded = [sem(f"v_pages_loaded{g}") for g in range(V_GROUPS)]
        kT_done = count("kT_in_psum", 2 * D_PAGES + V_GROUPS)
        kT_kept = [count("kT_bank0_kept", D_PAGES + (V_GROUPS + 1) // 2), count("kT_bank1_kept", D_PAGES + V_GROUPS // 2)]
        q_in = sb("sample_qT", [P, BLOCKS, N_SAMPLE if kind == DIFF else 1])
        q_in_loaded = sem("sample_qT_loaded")
        zeroed = sem("zeros_written")
        q_spread = count("q_by_block_done", 1)
        ps_done = count("page_scores_in_psum", S_GROUPS)
        sfar = count("sample_far_kept", S_GROUPS)
        snear = count("sample_near_kept", 1)
        smax = count("sample_max", 1)
        sexp = count("sample_exp", 1)
        sabs = count("sample_abs", 1)
        sexpm = count("sample_exp_minus_abs", 1)
        sln = count("sample_ln", 1)
        ssoft = count("sample_softplus", 1)
        sscan = count("sample_suffix_sums", 1)
        ssub = count("sample_log_weights", 1)
        sstick = count("sample_stick_weights", 1)
        sinv = count("sample_inverse_sums", 2)
        applied = [count("diff_groups_applied", V_GROUPS), count("stick_groups_applied", V_GROUPS)]
        rows_kept = [count("sample_diff_rows_kept", 1), count("sample_stick_rows_kept", 1)]
        heads_done = count("sample_heads_in_psum", 1)
        so_kept = count("sample_o_kept", 1)

        def page_slot(p):
            s = p % K_SLOTS
            return s, p // K_SLOTS, len(range(s, D_PAGES, K_SLOTS))

        kv = t.new_kvd if kind == DIFF else t.new_kvs

        with nc.Block() as block:

            @block.sync
            def _(sp):
                def head_block(b):
                    return t.qT[:, bass.ds(b + TURNS * kind, 1), 0:SEQ], t.kT[:, bass.ds(b + TURNS * kind, 1), 0:SEQ]

                def load_page(it, p, dst, half, signal, free):
                    if p < N_PAGES:
                        page = sp.value_load(t.pages[0:1, bass.ds((it + TURNS * kind) * N_PAGES + p, 1)],
                                             min_val=0, max_val=t.n_pool - 1)
                        src = [c[bass.ds(page, 1), :, half * HALF_W:(half + 1) * HALF_W]
                               .rearrange("a k n -> (a k) n") for c in (t.cache_d, t.cache_s)]
                    else:
                        first = SEQ + (it + TURNS * kind) * DEC_SEQ
                        src = [c[bass.ds(first, DEC_SEQ), half * HALF_W:(half + 1) * HALF_W]
                               for c in (t.new_kvd, t.new_kvs)]
                    n = page_keys(p)
                    sp.wait_ge(*free)
                    for j in range(2):
                        sp.dma_start(dst[0:n, 4 * j:4 * j + 4, :], src[j]).then_inc(signal, 16)

                def load_k(it, p):
                    s, _, _ = page_slot(p)
                    prior = p - K_SLOTS if p >= K_SLOTS else max(range(s, D_PAGES, K_SLOTS)) - D_PAGES
                    item = 2 * prior + 1 if prior >= 0 else 2 * prior + 1 - V_GROUPS
                    load_page(it, p, k_page[:, s, :, :], 0, k_loaded[s], (kT_done.sem, kT_done.after(it, item)))

                def load_v(it, p):
                    load_page(it, p, v_page[:, p, :, :], 1, vp_loaded[p // 4],
                              (applied[1].sem, applied[1].after(it, p // 4 - V_GROUPS)))

                if kind == DIFF:
                    sp.dma_start(q_in[:, :, :], t.qT[:, :, SEQ:SEQ + N_SAMPLE]).then_inc(q_in_loaded, 16)
                if kind == STICK:
                    sp.dma_start(near[:, :], distances(t, H_DIFF, P, NEAR)).then_inc(near_loaded, 16)
                with sp.Fori(0, TURNS) as it:
                    for p in range(K_SLOTS):
                        load_k(it, p)
                    if kind == DIFF:
                        sp.wait_ge(sc_near.sem, sc_near.after(it, -1))
                        sp.dma_start(near[:, :], t.near_dram[bass.ds(it, 1), :, :].rearrange("a p n -> (a p) n"))\
                          .then_inc(near_loaded, 16)
                    sp.wait_ge(sc_done.sem, sc_done.after(it, -1))
                    q_src, k_src = [a.rearrange("p a n -> p (a n)") for a in head_block(it)]
                    for u in range(2):
                        rows = slice(HEAD * u, HEAD * u + HEAD)
                        sp.dma_start(qT[rows, u, :], q_src[rows, :]).then_inc(qk_loaded, 16)
                    sp.dma_start(kT[:, :], k_src).then_inc(qk_loaded, 16)
                    sp.wait_ge(o_done.sem, o_done.after(it, -1))
                    sp.dma_start(v[:, :, :], kv[0:SEQ, bass.ds(it * P + HALF_W, P)].rearrange("(t p) n -> p t n", p=P))\
                      .then_inc(v_loaded, 16)
                    for p in range(N_PAGES):
                        load_v(it, p)
                        if p + K_SLOTS < D_PAGES:
                            load_k(it, p + K_SLOTS)
                    load_v(it, NEW)

            @block.gpsimd
            def _(pool):
                pool.sem_inc(sub_step.sem, sub_step.per)
                pool.sem_inc(sub_rstd.sem, sub_rstd.per)

                def rstd(it, i):
                    pool.wait_ge(o_squared.sem, o_squared.after(it, i))
                    own_wait(pool, t)
                    pool.tensor_scalar(stat[:, i % 4, 6:7], stat[:, i % 4, 5:6], 1.0 / P, SUBLN_EPS,
                                       ALU.mult, ALU.add).then_inc(sub_step.sem, 1)
                    pool.wait_ge(sub_step.sem, sub_step.after(it, i))
                    pool.tensor_tensor(stat[:, i % 4, 7:8], stat[:, i % 4, 6:7], t.neg_half[:, :], ALU.pow)\
                        .then_inc(sub_rstd.sem, 1)

                if kind == DIFF:
                    with pool.Fori(0, TURNS) as it:
                        for i in range(PT):
                            rstd(it, i)

            @block.tensor
            def _(pe):
                for c in (sc_done, w_turned, o_done, oT_done, kT_done, ps_done, *applied, heads_done):
                    pe.sem_inc(c.sem, c.per)

                def score(it, i, chunk):
                    if chunk == 0:
                        pe.wait_ge(qk_loaded, it * 48 + 48)
                    for g, (ci, u, k0, k1, kn) in enumerate(chunks):
                        if g != chunk:
                            continue
                        if g >= 2:
                            pe.wait_ge(sc_far.sem, sc_far.after(it, far_upto[g - 2] - 1))
                            pe.wait_ge(sc_near.sem, sc_near.after(it, near_upto[g - 2] - 1))
                        else:
                            pe.wait_ge(sc_far.sem, sc_far.after(it, -1))
                            pe.wait_ge(sc_near.sem, sc_near.after(it, -1))
                        pe.matmul(sc_ps[:, g % 2, 0:k1 - k0], qT[:, u, i * P:(i + 1) * P], kT[:, k0:k1],
                                  start=True, stop=True).then_inc(sc_done.sem, 1)

                def out(it, i, n):
                    groups = turned_groups(kind, i)
                    first = groups_upto[i] - n_groups[i]
                    if n < len(groups):
                        if n == 0:
                            if kind == DIFF:
                                pe.wait_ge(mixed.sem, mixed.after(it, i))
                            else:
                                pe.wait_ge(s_exp.sem, s_exp.after(it, i))
                        pe.wait_ge(wT_kept.sem, wT_kept.after(it, first + n - 1))
                        for m, (u, kb) in enumerate(groups[n]):
                            src = aux[:, 0, kb * P:(kb + 1) * P] if kind == DIFF else S[:, i % 2, u, kb * P:(kb + 1) * P]
                            last = pe.transpose(wT_ps[:, m, :], src, t.ident[:, :])
                        last.then_inc(w_turned.sem, 1)
                        return
                    pe.wait_ge(wT_kept.sem, wT_kept.after(it, groups_upto[i] - 1))
                    pe.wait_ge(oT_kept.sem, oT_kept.after(it, i - 1))
                    if i == 0:
                        pe.wait_ge(v_loaded, it * 16 + 16)
                    for m, (u, kb) in enumerate([x for g in groups for x in g]):
                        cols = slice(0, P) if kind == DIFF else slice(HEAD * u, HEAD * u + HEAD)
                        last = pe.matmul(o_ps[:, cols], wT[:, m, :], v[:, kb, cols], start=(kb == 0), stop=(kb == i))
                    last.then_inc(o_done.sem, 1)

                def turn_out(it, i):
                    ready = o_normed if kind == DIFF else o_kept
                    pe.wait_ge(ready.sem, ready.after(it, i))
                    pe.wait_ge(oT_kept.sem, oT_kept.after(it, i - 1))
                    pe.transpose(o_ps[:, P:2 * P], o_norm[:, :], t.ident[:, :]).then_inc(oT_done.sem, 1)

                def page(it, p):
                    s, before, loads = page_slot(p)
                    n = page_keys(p)
                    pe.wait_ge(k_loaded[s], it * (32 * loads) + 32 * (before + 1))
                    for half in range(2):
                        pe.wait_ge(kT_kept[half].sem, kT_kept[half].after(it, p - 1))
                        own_wait(pe, t)
                        for b in range(4):
                            last = pe.transpose(kT_ps[:, half, b, 0:n], k_page[0:n, s, 4 * half + b, :],
                                                t.ident[0:n, 0:n])
                        last.then_inc(kT_done.sem, 1)

                def page_scores(it, g, part):
                    if g == 0 and part == 0:
                        pe.wait_ge(q_spread.sem, q_spread.after(it, 0))
                    for half in range(2):
                        pe.wait_ge(kT_kept[half].sem, kT_kept[half].after(it, score_group_pages(g)[-1]))
                    pe.wait_ge(sfar.sem, sfar.after(it, g - 1))
                    if g == 0:
                        pe.wait_ge(snear.sem, snear.after(it, -1))
                    n = sum(page_keys(p) for p in score_group_pages(g))
                    for b in range(4 * part, 4 * part + 4):
                        last = pe.matmul(s_ps[:, 0:n], q_block[:, b * P:(b + 1) * P], kT_page[:, g % 2, b, 0:n],
                                         start=(b == 0), stop=(b == BLOCKS - 1))
                    if part == 1:
                        last.then_inc(ps_done.sem, 1)

                def turn(it, g):
                    if g == 0:
                        pe.wait_ge(sstick.sem, sstick.after(it, 0))
                        pe.wait_ge(sexp.sem, sexp.after(it, 0))
                    pe.wait_ge(kT_kept[g % 2].sem, kT_kept[g % 2].after(it, D_PAGES - 1 + g // 2))
                    for m, p in enumerate(group_pages(g)):
                        n = page_keys(p)
                        last = pe.transpose(kT_ps[0:n, g % 2, m, :], sW[:, p * PAGE:p * PAGE + n], t.ident[:, :])
                    last.then_inc(kT_done.sem, 1)

                def apply(it, kind_half, p):
                    g, n = p // 4, page_keys(p)
                    if kind_half == 0 and p == 4 * g:
                        pe.wait_ge(kT_kept[g % 2].sem, kT_kept[g % 2].after(it, D_PAGES + g // 2))
                        pe.wait_ge(vp_loaded[g], (it + 1) * (32 * len(group_pages(g))))
                        if g == 0:
                            pe.wait_ge(so_kept.sem, so_kept.after(it, -1))
                    elif kind_half == 1 and p == 0:
                        pe.wait_ge(rows_kept[0].sem, rows_kept[0].after(it, 0))
                    own_wait(pe, t)
                    last = pe.matmul(sO_ps[:, :], sT[0:n, p, :], v_page[0:n, p, 4 * kind_half:4 * kind_half + 4, :],
                                     start=(p == 0), stop=(p == NEW))
                    if p == group_pages(g)[-1]:
                        last.then_inc(applied[kind_half].sem, 1)

                def heads(it, _):
                    pe.wait_ge(rows_kept[1].sem, rows_kept[1].after(it, 0))
                    for b in range(4):
                        cols = slice(16 * b, 16 * b + 16)
                        last = pe.matmul(sO_ps[:, 0:P].rearrange("p (u c) -> p u c", u=2)[:, :, cols],
                                         o_rows_s[:, b * P:(b + 1) * P],
                                         t.ident[:, :].rearrange("p (u c) -> p u c", u=2)[:, :, cols],
                                         start=True, stop=True)
                    last.then_inc(heads_done.sem, 1)

                steps = dict(score=score, out=out, turn_out=turn_out, page=page, page_scores=page_scores,
                             turn=turn, apply=apply, heads=heads)
                pe.wait_ge(zeroed, 3)
                with pe.Fori(0, TURNS) as it:
                    for name, *args in plan:
                        if name in steps:
                            steps[name](it, *args)

            @block.vector
            def _(dve):
                for c in (sc_near, row_max, inv_sum, mixed, s_soft, s_scan, s_sub, o_normed, oT_kept, kT_kept[1],
                          q_spread, snear, smax, ssoft, sscan, ssub, sinv, *rows_kept, so_kept):
                    dve.sem_inc(c.sem, c.per)
                if kind == STICK:
                    for c in (wT_kept,):
                        dve.sem_inc(c.sem, c.per)

                def score(it, i, chunk):
                    if chunk == 0:
                        dve.wait_ge(near_loaded, it * 16 + 16 if kind == DIFF else 16)
                    for g, (ci, u, k0, k1, kn) in enumerate(chunks):
                        if g != chunk or kn >= k1:
                            continue
                        dve.wait_ge(sc_done.sem, sc_done.after(it, g))
                        if kn > k0:
                            dve.wait_ge(sc_far.sem, sc_far.after(it, far_upto[g] - 1))
                        dve.wait_ge(w_turned.sem, w_turned.after(it, groups_upto[i - 2] - 1 if i >= 2 else
                                                                 groups_upto[PT - 2 + i] - 1 - groups_upto[-1]))
                        col = kn - (i - 1) * P
                        dve.tensor_tensor(S[:, i % 2, u, kn:k1], sc_ps[:, g % 2, kn - k0:k1 - k0],
                                          near[:, col:col + k1 - kn], ALU.add).then_inc(sc_near.sem, 1)

                def soft_diff(it, i, n):
                    end = (i + 1) * P
                    last_chunk = max(g for g, c in enumerate(chunks) if c[0] == i)
                    x = stat[:, i % 4, :]
                    if n == 0:
                        dve.wait_ge(sc_far.sem, sc_far.after(it, far_upto[last_chunk] - 1))
                        dve.wait_ge(sc_near.sem, sc_near.after(it, near_upto[last_chunk] - 1))
                        dve.wait_ge(o_normed.sem, o_normed.after(it, i - 4))
                        dve.tensor_reduce(x[:, 0:2], S[:, i % 2, :, 0:end], axis=AX.X, op=ALU.max, negate=True)\
                           .then_inc(row_max.sem, 1)
                    elif n == 2:
                        dve.wait_ge(exps.sem, exps.after(it, 2 * i + 1))
                        dve.reciprocal(x[:, 4:6], x[:, 2:4]).then_inc(inv_sum.sem, 1)
                        dve.wait_ge(inv_sum.sem, inv_sum.after(it, 2 * i))
                        dve.scalar_tensor_tensor(x[:, 1:2], x[:, 5:6], t.neg_lambda[:, 0:1], x[:, 2:3],
                                                 ALU.mult, ALU.mult).then_inc(inv_sum.sem, 1)
                        dve.wait_ge(inv_sum.sem, inv_sum.after(it, 2 * i + 1))
                        dve.wait_ge(w_turned.sem, w_turned.after(it, groups_upto[i - 1] - 1 if i else -1))
                        dve.scalar_tensor_tensor(aux[:, 0, 0:end], S[:, i % 2, 1, 0:end], x[:, 1:2],
                                                 S[:, i % 2, 0, 0:end], ALU.mult, ALU.add).then_inc(mixed.sem, 1)

                def soft_stick(it, i, n):
                    end = (i + 1) * P
                    if n == 3:
                        dve.wait_ge(s_ln.sem, s_ln.after(it, i))
                        dve.scalar_tensor_tensor(aux[:, :, 0:end], S[:, i % 2, :, 0:end], 0.0, aux[:, :, 0:end],
                                                 ALU.max, ALU.add).then_inc(s_soft.sem, 1)
                    elif n == 4:
                        dve.wait_ge(s_soft.sem, s_soft.after(it, i))
                        for u in range(2):
                            dve.tensor_tensor_scan(aux[:, u, 0:end][:, ::-1], aux[:, u, 0:end][:, ::-1],
                                                   aux[:, u, 0:end][:, ::-1], 0.0, ALU.add, ALU.bypass)\
                               .then_inc(s_scan.sem, 1)
                        dve.wait_ge(s_scan.sem, s_scan.after(it, 2 * i + 1))
                        dve.tensor_tensor(S[:, i % 2, :, 0:end], S[:, i % 2, :, 0:end], aux[:, :, 0:end],
                                          ALU.subtract).then_inc(s_sub.sem, 1)

                def out(it, i, n):
                    groups = turned_groups(kind, i)
                    first = groups_upto[i] - n_groups[i]
                    if kind == STICK and n < len(groups):
                        dve.wait_ge(w_turned.sem, w_turned.after(it, first + n))
                        dve.wait_ge(o_done.sem, o_done.after(it, i - 1))
                        m = len(groups[n])
                        dve.tensor_copy(wT[:, 4 * n:4 * n + m, :], wT_ps[:, 0:m, :]).then_inc(wT_kept.sem, 1)

                def turn_out(it, i):
                    if kind == DIFF:
                        dve.wait_ge(sub_rstd.sem, sub_rstd.after(it, i))
                        dve.wait_ge(oT_done.sem, oT_done.after(it, i - 1))
                        dve.tensor_scalar_mul(o_norm[:, :], o_rows[:, i % 2, :], stat[:, i % 4, 7:8])\
                           .then_inc(o_normed.sem, 1)
                    dve.wait_ge(oT_done.sem, oT_done.after(it, i))
                    if i == 0:
                        dve.wait_ge(oT_stored, it * 16 + 16)
                    if kind == DIFF:
                        dve.tensor_scalar_mul(oT[:, i * P:(i + 1) * P], o_ps[:, P:2 * P], t.sub_g[:, 0:1])\
                           .then_inc(oT_kept.sem, 1)
                    else:
                        dve.tensor_copy(oT[:, i * P:(i + 1) * P], o_ps[:, P:2 * P]).then_inc(oT_kept.sem, 1)

                def page(it, p):
                    n = page_keys(p)
                    g = min(p // 2, S_GROUPS - 1)
                    at = p * PAGE - 2 * g * PAGE
                    if p == 0:
                        dve.wait_ge(ps_done.sem, ps_done.after(it, -1))
                        dve.tensor_copy(q_block[:, :].rearrange("p (b c) -> p b c", b=BLOCKS)[:, :, 0:16],
                                        t.q_heads[:, bass.ds(it + TURNS * kind, 1), :, :, :]
                                        .rearrange("p s b u q -> p (s b) (u q)")).then_inc(q_spread.sem, 1)
                    dve.wait_ge(kT_done.sem, kT_done.after(it, 2 * p + 1))
                    dve.wait_ge(ps_done.sem, ps_done.after(it, g - 2))
                    dve.tensor_copy(kT_page[:, g % 2, 4:8, at:at + n], kT_ps[:, 1, :, 0:n]).then_inc(kT_kept[1].sem, 1)

                def page_scores(it, g, part):
                    if part == 1 and g == S_GROUPS - 1:
                        dve.wait_ge(ps_done.sem, ps_done.after(it, g))
                        dve.wait_ge(sfar.sem, sfar.after(it, g))
                        n = PAGE + DEC_SEQ
                        dve.tensor_tensor(sS[:, KEYS - n:KEYS], s_ps[:, PAGE:PAGE + n], t.near_dec[:, 0:n], ALU.add)\
                           .then_inc(snear.sem, 1)

                def weigh(it, n):
                    if n == 0:
                        dve.wait_ge(sfar.sem, sfar.after(it, S_GROUPS - 1))
                        dve.wait_ge(snear.sem, snear.after(it, 0))
                        dve.tensor_reduce(sstat[0:D0, 0:1], sS[0:D0, :], axis=AX.X, op=ALU.max, negate=True)\
                           .then_inc(smax.sem, 1)
                    elif n == 3:
                        dve.wait_ge(sln.sem, sln.after(it, 0))
                        dve.scalar_tensor_tensor(sW[D0:P, :], sS[D0:P, :], 0.0, sW[D0:P, :], ALU.max, ALU.add)\
                           .then_inc(ssoft.sem, 1)
                    elif n == 4:
                        dve.wait_ge(ssoft.sem, ssoft.after(it, 0))
                        dve.tensor_tensor_scan(sW[D0:P, ::-1], sW[D0:P, ::-1], sW[D0:P, ::-1], 0.0, ALU.add,
                                               ALU.bypass).then_inc(sscan.sem, 1)
                    elif n == 5:
                        dve.wait_ge(sscan.sem, sscan.after(it, 0))
                        dve.tensor_tensor(sW[D0:P, :], sS[D0:P, :], sW[D0:P, :], ALU.subtract).then_inc(ssub.sem, 1)
                    elif n == 6:
                        dve.wait_ge(sexp.sem, sexp.after(it, 0))
                        dve.reciprocal(sstat[0:D0, 2:3], sstat[0:D0, 1:2]).then_inc(sinv.sem, 1)
                        dve.wait_ge(sinv.sem, sinv.after(it, 0))
                        dve.tensor_tensor(sstat[0:D0, 3:4], sstat[0:D0, 2:3], t.row_factor[0:D0, :], ALU.mult)\
                           .then_inc(sinv.sem, 1)

                def turn(it, g):
                    if g % 2 == 1:
                        m = len(group_pages(g))
                        dve.wait_ge(kT_done.sem, kT_done.after(it, 2 * D_PAGES + g))
                        dve.wait_ge(applied[1].sem, applied[1].after(it, g - V_GROUPS))
                        dve.tensor_copy(sT[:, 4 * g:4 * g + m, :], kT_ps[:, 1, 0:m, :]).then_inc(kT_kept[1].sem, 1)

                def rows(it, kind_half):
                    dve.wait_ge(applied[kind_half].sem, applied[kind_half].after(it, V_GROUPS - 1))
                    dve.wait_ge(heads_done.sem, heads_done.after(it, -1))
                    if kind_half == 0:
                        dve.wait_ge(sinv.sem, sinv.after(it, 1))
                        dve.tensor_scalar_mul(o_rows_s[0:D0, :], sO_ps[0:D0, :], sstat[0:D0, 3:4])\
                           .then_inc(rows_kept[0].sem, 1)
                    else:
                        dve.tensor_copy(o_rows_s[D0:P, :], sO_ps[D0:P, :]).then_inc(rows_kept[1].sem, 1)

                def heads(it, _):
                    dve.wait_ge(heads_done.sem, heads_done.after(it, 0))
                    dve.tensor_copy(t.sample_o[:, bass.ds(it + TURNS * kind, 1), :].rearrange("p a n -> p (a n)"),
                                    sO_ps[:, 0:P]).then_inc(so_kept.sem, 1)

                steps = dict(score=score, soft=soft_diff if kind == DIFF else soft_stick, out=out, turn_out=turn_out,
                             page=page, page_scores=page_scores, weigh=weigh, turn=turn, rows=rows, heads=heads)
                dve.memset(qT[HEAD:P, 0, :], 0.0).then_inc(zeroed, 1)
                dve.memset(qT[0:HEAD, 1, :], 0.0).then_inc(zeroed, 1)
                dve.memset(q_block[:, :], 0.0).then_inc(zeroed, 1)
                if kind == DIFF:
                    dve.wait_ge(q_in_loaded, 16)
                    for u in range(2):
                        rows_u = slice(HEAD * u, HEAD * u + HEAD)
                        for s in range(DEC_BATCH):
                            dve.tensor_copy(t.q_heads[rows_u, s, :, u, :], q_in[rows_u, :, DEC_SEQ * s:DEC_SEQ * (s + 1)])\
                               .then_inc(zeroed, 1)
                    dve.wait_ge(zeroed, 3 + 2 * DEC_BATCH)
                else:
                    dve.wait_ge(zeroed, 3)
                with dve.Fori(0, TURNS) as it:
                    for name, *args in plan:
                        if name in steps:
                            steps[name](it, *args)

            @block.scalar
            def _(act):
                for c in (sc_far, exps, s_abs, s_expm, s_ln, s_exp, o_kept, o_squared, kT_kept[0], sfar, sexp, sabs,
                          sexpm, sln, sstick):
                    act.sem_inc(c.sem, c.per)
                if kind == DIFF:
                    for c in (wT_kept,):
                        act.sem_inc(c.sem, c.per)

                def score(it, i, chunk):
                    for g, (ci, u, k0, k1, kn) in enumerate(chunks):
                        if g != chunk or kn <= k0:
                            continue
                        act.wait_ge(sc_done.sem, sc_done.after(it, g))
                        act.wait_ge(w_turned.sem, w_turned.after(it, groups_upto[i - 2] - 1 if i >= 2 else
                                                                 groups_upto[PT - 2 + i] - 1 - groups_upto[-1]))
                        act.activation(S[:, i % 2, u, k0:kn], sc_ps[:, g % 2, 0:kn - k0], ACT.Copy)\
                           .then_inc(sc_far.sem, 1)

                def soft_diff(it, i, n):
                    end = (i + 1) * P
                    if n == 1:
                        act.wait_ge(row_max.sem, row_max.after(it, i))
                        for u in range(2):
                            act.activation(S[:, i % 2, u, 0:end], S[:, i % 2, u, 0:end], ACT.Exp,
                                           bias=stat[:, i % 4, u:u + 1],
                                           accum_out=stat[:, i % 4, 2 + u:3 + u]).then_inc(exps.sem, 1)

                def soft_stick(it, i, n):
                    end = (i + 1) * P
                    last_chunk = max(g for g, c in enumerate(chunks) if c[0] == i)
                    if n == 0:
                        act.wait_ge(sc_far.sem, sc_far.after(it, far_upto[last_chunk] - 1))
                        act.wait_ge(sc_near.sem, sc_near.after(it, near_upto[last_chunk] - 1))
                        act.wait_ge(s_sub.sem, s_sub.after(it, i - 1))
                        act.activation(aux[:, :, 0:end], S[:, i % 2, :, 0:end], ACT.Abs).then_inc(s_abs.sem, 1)
                    elif n == 1:
                        act.wait_ge(s_abs.sem, s_abs.after(it, i))
                        act.activation(aux[:, :, 0:end], aux[:, :, 0:end], ACT.Exp, scale=-1.0).then_inc(s_expm.sem, 1)
                    elif n == 2:
                        act.wait_ge(s_expm.sem, s_expm.after(it, i))
                        act.activation(aux[:, :, 0:end], aux[:, :, 0:end], ACT.Ln, bias=1.0).then_inc(s_ln.sem, 1)
                    elif n == 5:
                        act.wait_ge(s_sub.sem, s_sub.after(it, i))
                        act.activation(S[:, i % 2, :, 0:end], S[:, i % 2, :, 0:end], ACT.Exp).then_inc(s_exp.sem, 1)

                def out(it, i, n):
                    groups = turned_groups(kind, i)
                    first = groups_upto[i] - n_groups[i]
                    if n < len(groups):
                        if kind == DIFF:
                            act.wait_ge(w_turned.sem, w_turned.after(it, first + n))
                            act.wait_ge(o_done.sem, o_done.after(it, i - 1))
                            m = len(groups[n])
                            act.activation(wT[:, 4 * n:4 * n + m, :], wT_ps[:, 0:m, :], ACT.Copy)\
                               .then_inc(wT_kept.sem, 1)
                        return
                    act.wait_ge(o_done.sem, o_done.after(it, i))
                    if kind == STICK:
                        act.wait_ge(oT_done.sem, oT_done.after(it, i - 1))
                        act.activation(o_norm[:, :], o_ps[:, 0:P], ACT.Copy).then_inc(o_kept.sem, 1)
                    else:
                        act.wait_ge(o_normed.sem, o_normed.after(it, i - 2))
                        act.activation(o_rows[:, i % 2, :], o_ps[:, 0:P], ACT.Copy, scale=stat[:, i % 4, 4:5])\
                           .then_inc(o_kept.sem, 1)
                        act.wait_ge(o_kept.sem, o_kept.after(it, i))
                        act.wait_ge(o_squared.sem, o_squared.after(it, i - 1))
                        act.activation(o_sq[:, :], o_rows[:, i % 2, :], ACT.Square,
                                       accum_out=stat[:, i % 4, 5:6]).then_inc(o_squared.sem, 1)

                def page(it, p):
                    n = page_keys(p)
                    g = min(p // 2, S_GROUPS - 1)
                    at = p * PAGE - 2 * g * PAGE
                    act.wait_ge(kT_done.sem, kT_done.after(it, 2 * p))
                    act.wait_ge(ps_done.sem, ps_done.after(it, g - 2))
                    act.activation(kT_page[:, g % 2, 0:4, at:at + n], kT_ps[:, 0, :, 0:n], ACT.Copy)\
                       .then_inc(kT_kept[0].sem, 1)

                def page_scores(it, g, part):
                    if part == 0:
                        return
                    n = 2 * PAGE if g + 1 < S_GROUPS else PAGE
                    act.wait_ge(ps_done.sem, ps_done.after(it, g))
                    act.wait_ge(ssub.sem, ssub.after(it, -1))
                    act.wait_ge(sexp.sem, sexp.after(it, -1))
                    act.activation(sS[:, 2 * g * PAGE:2 * g * PAGE + n], s_ps[:, 0:n], ACT.Copy).then_inc(sfar.sem, 1)

                def weigh(it, n):
                    if n == 0:
                        act.wait_ge(sfar.sem, sfar.after(it, S_GROUPS - 1))
                        act.wait_ge(snear.sem, snear.after(it, 0))
                        act.wait_ge(kT_done.sem, kT_done.after(it, -1))
                        act.activation(sW[D0:P, :], sS[D0:P, :], ACT.Abs).then_inc(sabs.sem, 1)
                    elif n == 1:
                        act.wait_ge(sabs.sem, sabs.after(it, 0))
                        act.activation(sW[D0:P, :], sW[D0:P, :], ACT.Exp, scale=-1.0).then_inc(sexpm.sem, 1)
                    elif n == 2:
                        act.wait_ge(sexpm.sem, sexpm.after(it, 0))
                        act.activation(sW[D0:P, :], sW[D0:P, :], ACT.Ln, bias=1.0).then_inc(sln.sem, 1)
                    elif n == 3:
                        act.wait_ge(smax.sem, smax.after(it, 0))
                        act.wait_ge(kT_done.sem, kT_done.after(it, -1))
                        act.wait_ge(rows_kept[0].sem, rows_kept[0].after(it, -1))
                        act.activation(sW[0:D0, :], sS[0:D0, :], ACT.Exp, bias=sstat[0:D0, 0:1],
                                       accum_out=sstat[0:D0, 1:2]).then_inc(sexp.sem, 1)
                    elif n == 6:
                        act.wait_ge(ssub.sem, ssub.after(it, 0))
                        act.activation(sW[D0:P, :], sW[D0:P, :], ACT.Exp).then_inc(sstick.sem, 1)

                def turn(it, g):
                    if g % 2 == 0:
                        m, n = len(group_pages(g)), page_keys(4 * g)
                        act.wait_ge(kT_done.sem, kT_done.after(it, 2 * D_PAGES + g))
                        act.wait_ge(applied[1].sem, applied[1].after(it, g - V_GROUPS))
                        act.activation(sT[0:n, 4 * g:4 * g + m, :], kT_ps[0:n, 0, 0:m, :], ACT.Copy)\
                           .then_inc(kT_kept[0].sem, 1)

                steps = dict(score=score, soft=soft_diff if kind == DIFF else soft_stick, out=out, page=page,
                             page_scores=page_scores, weigh=weigh, turn=turn)
                act.sem_inc(oT_stored, 16)
                with act.Fori(0, TURNS) as it:
                    for name, *args in plan:
                        if name in steps:
                            steps[name](it, *args)
                    act.wait_ge(oT_kept.sem, oT_kept.after(it, PT - 1))
                    act.dma_start(t.oT[:, bass.ds(it + TURNS * kind, 1), 0:SEQ].rearrange("p a n -> p (a n)"), oT[:, :])\
                       .then_inc(oT_stored, 16)
                act.wait_ge(oT_stored, 16 * (TURNS + 1))


        clear(nc, sems)


def sample_heads_out(nc, t):
    with ExitStack() as ctx:
        sems = []

        def sb(name, shape, dt=F32):
            return ctx.enter_context(nc.sbuf_tensor(name, shape, dt))

        def sem(name):
            sems.append(ctx.enter_context(nc.semaphore(name)))
            return sems[-1]

        oT = sb("sample_oT", [P, BLOCKS, P])
        mix = sb("sample_diff", [P, DEC_BATCH, H_DIFF, DEC_SEQ])
        sq = sb("sample_diff_sq", [P, DEC_BATCH * H_DIFF * DEC_SEQ])
        rms = sb("sample_rms", [P, DEC_BATCH * H_DIFF * DEC_SEQ])
        ms_ps = ctx.enter_context(nc.psum_tensor("sample_ms_ps", [P, BANK], F32))
        step, sums, roots, stored = sem("so_step"), sem("so_sums"), sem("so_roots"), sem("so_stored")
        w_raw = sb("w_out_raw", [P, BLOCKS, D_MODEL])
        w_loaded = [sem(f"w_out_loaded{k}") for k in range(BLOCKS)]
        w_hi, w_lo = sem("w_out_hi_done"), sem("w_out_lo_done")
        N = DEC_BATCH * H_DIFF * DEC_SEQ
        with nc.Block() as block:

            @block.vector
            def _(dve):
                o = t.sample_o[:, :, :].rearrange("p s (b u q) -> p s b u q", b=BLOCKS, u=2)
                dve.memset(oT[:, :, :], 0.0).then_inc(step, 1)
                for s in range(DEC_BATCH):
                    dve.tensor_tensor(mix[:, s, :, :], o[:, s, 0:H_DIFF, 0, :], o[:, s, 0:H_DIFF, 1, :], ALU.add)\
                       .then_inc(step, 1)
                dve.wait_ge(step, 1 + DEC_BATCH)
                flat = mix[:, :, :, :].rearrange("p s h q -> p (s h q)")
                dve.tensor_tensor(sq[:, :], flat, flat, ALU.mult).then_inc(step, 1)
                for u in range(2):
                    rows = slice(HEAD * u, HEAD * u + HEAD)
                    for b in range(H_DIFF, BLOCKS):
                        dve.tensor_copy(oT[rows, b, 0:N_SAMPLE].rearrange("p (s q) -> p s q", q=DEC_SEQ),
                                        o[rows, :, b, u, :]).then_inc(step, 1)
                dve.wait_ge(sums, 1)
                dve.tensor_scalar(rms[:, :], ms_ps[:, 0:N], 1.0 / P, SUBLN_EPS, ALU.mult, ALU.add).then_inc(step, 1)
                dve.wait_ge(roots, 1)
                dve.reciprocal(rms[:, :], rms[:, :]).then_inc(step, 1)
                done = 1 + DEC_BATCH + 1 + 2 * (BLOCKS - H_DIFF) + 2
                dve.wait_ge(step, done)
                dve.scalar_tensor_tensor(rms[:, :], rms[:, :], t.sub_g[:, 0:1], flat, ALU.mult, ALU.mult)\
                   .then_inc(step, 1)
                dve.wait_ge(step, done + 1)
                for b in range(H_DIFF):
                    dve.tensor_copy(oT[:, b, 0:N_SAMPLE].rearrange("p (s q) -> p s q", q=DEC_SEQ),
                                    rms[:, :].rearrange("p (s h q) -> p h s q", h=H_DIFF, q=DEC_SEQ)[:, b])\
                       .then_inc(step, 1)
                for k in range(BLOCKS):
                    dve.wait_ge(w_hi, k + 1)
                    dve.tensor_tensor(t.w_out_split[:, 1, k, :], w_raw[:, k, :], t.w_out_split[:, 0, k, :].bitcast(F32),
                                      ALU.subtract).then_inc(w_lo, 1)
                dve.wait_ge(w_lo, BLOCKS)

            @block.tensor
            def _(pe):
                pe.wait_ge(step, 2 + DEC_BATCH)
                pe.matmul(ms_ps[:, 0:N], t.ones[:, :], sq[:, :], start=True, stop=True).then_inc(sums, 1)

            @block.scalar
            def _(act):
                act.wait_ge(step, 1 + DEC_BATCH + 1 + 2 * (BLOCKS - H_DIFF) + 1)
                act.activation(rms[:, :], rms[:, :], ACT.Sqrt).then_inc(roots, 1)
                for k in range(BLOCKS):
                    act.wait_ge(w_loaded[k], 16)
                    act.activation(t.w_out_split[:, 0, k, :], w_raw[:, k, :], ACT.Copy).then_inc(w_hi, 1)

            @block.sync
            def _(sp):
                for k in range(BLOCKS):
                    sp.dma_start(w_raw[:, k, :], t.w_out[k * P:(k + 1) * P, :]).then_inc(w_loaded[k], 16)
                sp.wait_ge(step, 1 + DEC_BATCH + 1 + 2 * (BLOCKS - H_DIFF) + 3 + H_DIFF)
                sp.dma_start(t.oT[:, :, SEQ:TILES * P], oT[:, :, :]).then_inc(stored, 16)
                sp.wait_ge(stored, 16)

        clear(nc, sems)


N_LOGITS = N_GROUPS + N_EXPERTS
N_SLOTS = MOE_TILES * P
ALL = TILES * P


def tile_loop(engine, tile):
    with engine.Fori(0, PT // 2) as it:
        for u in range(2):
            tile(it, u)
    tile(PT // 2, 0)


def ahead_loop(engine, tile):
    with engine.Fori(0, PT // 2 - 1) as it:
        for u in range(2):
            tile(it, u, True)
    tile(PT // 2 - 1, 0, True)
    tile(PT // 2 - 1, 1, False)
    tile(PT // 2, 0, False, final=True)


def row_tile(dram, tile):
    return dram[bass.ds(tile * P, P), :]


def mix_out(nc, t):
    with ExitStack() as ctx:
        sems = []

        def sb(name, shape, dt=F32):
            return ctx.enter_context(nc.sbuf_tensor(name, shape, dt))

        def ps(name, shape):
            return ctx.enter_context(nc.psum_tensor(name, shape, F32))

        def sem(name):
            sems.append(ctx.enter_context(nc.semaphore(name)))
            return sems[-1]

        w_route = sb("w_route", [P, KC, N_LOGITS])
        b_route = sb("b_route", [P, N_LOGITS])
        g_row = sb("g_ffn_row", [P, D_MODEL])
        oT = sb("oT_tile", [P, 2, BLOCKS, P])
        oT_split = sb("oT_split", [P, 2, 2, BLOCKS, P], F32R)
        x = sb("x_again", [P, 2, D_MODEL])
        x1 = sb("x1_tile", [P, 2, D_MODEL])
        h = sb("h2_tile", [P, 2, D_MODEL])
        hT = sb("h2T_tile", [P, KC, P])
        square = sb("square2", [P, D_MODEL])
        ss = sb("sum_squares2", [P, 2, 3])
        y_ps = ps("mix_out_ps", [P, 2, 2, BANK])
        hT_ps = ps("h2T_ps", [P, 2, BANK])
        lg_ps = ps("logits_ps", [P, BANK])

        r_loaded = sem("routers_loaded")
        x_loaded = [sem(f"x_again_loaded{u}") for u in range(2)]
        o_loaded = [sem(f"oT_loaded{u}") for u in range(2)]
        stored = [sem(f"x1_h2_stored{u}") for u in range(2)]
        o_hi, o_lo = Count(sem("oT_hi_done"), 2), Count(sem("oT_lo_done"), 2)
        y_done = Count(sem("mix_out_in_psum"), 4)
        x1_done = Count(sem("x1_done"), 4)
        squares = Count(sem("squares2_done"), 2)
        rstd_step = Count(sem("rstd2_step"), 2)
        rstd = Count(sem("rstd2_done"), 2)
        h_done = Count(sem("h2_done"), 2)
        hT_done = Count(sem("h2T_in_psum"), 4)
        hT_kept = Count(sem("h2T_kept"), 4)
        lg_done = Count(sem("logits_in_psum"), 2)
        lg_kept = Count(sem("logits_kept"), 2)

        with nc.Block() as block:

            @block.sync
            def _(sp):
                def load(it, u, tile):
                    sp.dma_start(oT[:, u, :, :], t.oT[:, :, bass.ds(tile * P, P)]).then_inc(o_loaded[u], 16)
                    sp.dma_start(x[:, u, :], row_tile(t.x, tile)).then_inc(x_loaded[u], 16)

                for u in range(2):
                    load(0, u, u)
                sp.dma_start(w_route[:, :, 0:N_GROUPS], t.w_group.rearrange("(k p) n -> p k n", p=P))\
                  .then_inc(r_loaded, 16)
                sp.dma_start(w_route[:, :, N_GROUPS:N_LOGITS], t.w_erouter.rearrange("(k p) n -> p k n", p=P))\
                  .then_inc(r_loaded, 16)
                sp.dma_start(b_route[:, 0:N_GROUPS], t.b_group.partition_broadcast(P)).then_inc(r_loaded, 16)
                sp.dma_start(b_route[:, N_GROUPS:N_LOGITS], t.b_erouter.partition_broadcast(P)).then_inc(r_loaded, 16)
                sp.dma_start(g_row[:, :], t.g_ffn.partition_broadcast(P)).then_inc(r_loaded, 16)
                for u in range(2):
                    sp.sem_inc(stored[u], 32)

                def tile(it, u, ahead, final=False):
                    sp.wait_ge(x1_done.sem, x1_done.after(it, 2 * u + 1))
                    if ahead:
                        load(it + 1, u, it * 2 + u + 2)
                    sp.dma_start(row_tile(t.x1, it * 2 + u), x1[:, u, :]).then_inc(stored[u], 16)
                    sp.wait_ge(h_done.sem, h_done.after(it, u))
                    sp.dma_start(row_tile(t.h2, it * 2 + u), h[:, u, :]).then_inc(stored[u], 16)

                ahead_loop(sp, tile)
                sp.wait_ge(stored[0], 32 * (2 + PT // 2))
                sp.wait_ge(stored[1], 32 * (1 + PT // 2))

            @block.tensor
            def _(pe):
                for c in (y_done, hT_done, lg_done):
                    pe.sem_inc(c.sem, c.per)

                def out(it, u):
                    pe.wait_ge(o_lo.sem, o_lo.after(it, u))
                    for c in range(2):
                        pe.wait_ge(x1_done.sem, x1_done.after(it, 2 * (u - 2) + c))
                        for k in range(BLOCKS):
                            for m, (a, b) in enumerate(((0, 0), (1, 0), (0, 1))):
                                last = pe.matmul(y_ps[:, u, c, :], oT_split[:, u, a, k, :],
                                                 t.w_out_split[:, b, k, c * BANK:(c + 1) * BANK],
                                                 start=(k == 0 and m == 0), stop=(k == BLOCKS - 1 and m == 2))
                        last.then_inc(y_done.sem, 1)

                def route(it, u):
                    pe.wait_ge(h_done.sem, h_done.after(it, u))
                    for half in range(2):
                        pe.wait_ge(hT_kept.sem, hT_kept.after(it, 2 * (u - 1) + half))
                        for k in range(4):
                            last = pe.transpose(hT_ps[:, half, k * P:(k + 1) * P],
                                                h[:, u, (4 * half + k) * P:(4 * half + k + 1) * P], t.ident[:, :])
                        last.then_inc(hT_done.sem, 1)
                    pe.wait_ge(hT_kept.sem, hT_kept.after(it, 2 * u + 1))
                    pe.wait_ge(lg_kept.sem, lg_kept.after(it, u - 1))
                    for k in range(KC):
                        last = pe.matmul(lg_ps[:, 0:N_LOGITS], hT[:, k, :], w_route[:, k, :],
                                         start=(k == 0), stop=(k == KC - 1))
                    last.then_inc(lg_done.sem, 1)

                out(0, 0)
                pe.wait_ge(r_loaded, 16 * 5)
                with pe.Fori(0, PT // 2) as it:
                    for u in range(2):
                        out(it + u, 1 - u)
                        route(it, u)
                route(PT // 2, 0)

            @block.vector
            def _(dve):
                for c in (o_lo, x1_done, h_done, lg_kept):
                    dve.sem_inc(c.sem, c.per)

                def split(it, u):
                    dve.wait_ge(o_hi.sem, o_hi.after(it, u))
                    dve.tensor_tensor(oT_split[:, u, 1, :, :], oT[:, u, :, :], oT_split[:, u, 0, :, :].bitcast(F32),
                                      ALU.subtract).then_inc(o_lo.sem, 1)

                def residual(it, u):
                    dve.wait_ge(x_loaded[u], it * 16 + 16)
                    dve.wait_ge(stored[u], it * 32 + 32)
                    dve.wait_ge(h_done.sem, h_done.after(it, u - 2))
                    dve.wait_ge(squares.sem, squares.after(it, u - 2))
                    for c in range(2):
                        dve.wait_ge(y_done.sem, y_done.after(it, 2 * u + c))
                        dve.tensor_tensor(x1[:, u, c * BANK:(c + 1) * BANK], y_ps[:, u, c, :],
                                          x[:, u, c * BANK:(c + 1) * BANK], ALU.add).then_inc(x1_done.sem, 1)

                def tile(it, u, ahead, final=False):
                    dve.wait_ge(rstd.sem, rstd.after(it, u))
                    dve.wait_ge(x1_done.sem, x1_done.after(it, 2 * u + 1))
                    dve.wait_ge(hT_done.sem, hT_done.after(it, 2 * (u - 2) + 1))
                    dve.scalar_tensor_tensor(h[:, u, :], x1[:, u, :], ss[:, u, 2:3], g_row[:, :], ALU.mult, ALU.mult)\
                       .then_inc(h_done.sem, 1)
                    if not final:
                        residual(it + u, 1 - u)
                    dve.wait_ge(lg_done.sem, lg_done.after(it, u))
                    dve.tensor_tensor(t.logits[:, bass.ds(it * 2 + u, 1), :].rearrange("p a n -> p (a n)"),
                                      lg_ps[:, 0:N_LOGITS], b_route[:, :], ALU.add).then_inc(lg_kept.sem, 1)
                    if ahead:
                        split(it + 1, u)

                split(0, 0)
                split(0, 1)
                residual(0, 0)
                dve.wait_ge(r_loaded, 16 * 5)
                ahead_loop(dve, tile)

            @block.gpsimd
            def _(pool):
                pool.sem_inc(rstd_step.sem, rstd_step.per)
                pool.sem_inc(rstd.sem, rstd.per)

                def tile(it, u):
                    pool.wait_ge(squares.sem, squares.after(it, u))
                    own_wait(pool, t)
                    pool.tensor_scalar(ss[:, u, 1:2], ss[:, u, 0:1], 1.0 / D_MODEL, NORM_EPS, ALU.mult, ALU.add)\
                        .then_inc(rstd_step.sem, 1)
                    pool.wait_ge(rstd_step.sem, rstd_step.after(it, u))
                    pool.wait_ge(h_done.sem, h_done.after(it, u - 2))
                    pool.tensor_tensor(ss[:, u, 2:3], ss[:, u, 1:2], t.neg_half[:, :], ALU.pow)\
                        .then_inc(rstd.sem, 1)

                tile_loop(pool, tile)

            @block.scalar
            def _(act):
                for c in (o_hi, squares, hT_kept):
                    act.sem_inc(c.sem, c.per)

                def split(it, u):
                    act.wait_ge(o_loaded[u], it * 16 + 16)
                    act.wait_ge(y_done.sem, y_done.after(it, 2 * (u - 2) + 1))
                    act.activation(oT_split[:, u, 0, :, :], oT[:, u, :, :], ACT.Copy).then_inc(o_hi.sem, 1)

                def square_sum(it, u):
                    act.wait_ge(x1_done.sem, x1_done.after(it, 2 * u + 1))
                    act.wait_ge(squares.sem, squares.after(it, u - 1))
                    act.activation(square[:, :], x1[:, u, :], ACT.Square, accum_out=ss[:, u, 0:1])\
                       .then_inc(squares.sem, 1)

                def tile(it, u, ahead, final=False):
                    for half in range(2):
                        act.wait_ge(hT_done.sem, hT_done.after(it, 2 * u + half))
                        act.wait_ge(lg_done.sem, lg_done.after(it, u - 1))
                        act.activation(hT[:, 4 * half:4 * half + 4, :], hT_ps[:, half, :], ACT.Copy)\
                           .then_inc(hT_kept.sem, 1)
                    if not final:
                        square_sum(it + u, 1 - u)
                    if ahead:
                        split(it + 1, u)

                split(0, 0)
                split(0, 1)
                square_sum(0, 0)
                ahead_loop(act, tile)

        clear(nc, sems)


def route(nc, t):
    with ExitStack() as ctx:
        sems = []

        def sb(name, shape, dt=F32):
            return ctx.enter_context(nc.sbuf_tensor(name, shape, dt))

        def sem(name):
            sems.append(ctx.enter_context(nc.semaphore(name)))
            return sems[-1]

        G, J, E = N_GROUPS, PER_GROUP, N_EXPERTS
        rank = sb("first_wins", [P, TILES, G])
        limits = sb("limits", [P, E, TILES])
        tile_no = sb("tile_numbers", [P, MOE_TILES, E])
        spare = sb("spare_slots", [P, TILES])
        before = sb("before", [P, P])
        token = sb("token_ids", [P, TILES])
        column = sb("column_numbers", [P, P])
        part_i = sb("slot_parts_i", [P, 2, TOP_K * TILES], I32)
        part = sb("slot_parts", [P, 2, TOP_K * TILES])
        place = sb("place_hot", [P, 2, P])
        tile_token = sb("token_by_tile", [P, 2, MOE_TILES])
        g_max = sb("g_max", [P, TILES, 1])
        g_exp = sb("g_exp", [P, TILES, G])
        g_hot = sb("g_hot", [P, TILES, G])
        one = sb("one_hot", [P, 2, TILES, J])
        tmp = sb("tmp4", [P, TILES, G])
        top = sb("top", [P, 4, TILES, 1])
        el = sb("group_logits", [P, TILES, J])
        prod = sb("group_products", [P, TILES, J, G])
        hot = sb("expert_hot", [P, 2, TILES, G, J])
        member = sb("member", [P, TILES, E])
        pos = sb("positions", [P, TILES, E])
        total = sb("tile_counts", [P, TILES, E])
        carry = sb("carried", [P, TILES + 1, E])
        filled = sb("filled", [P, E, TILES])
        n_tiles = sb("n_tiles", [P, E])
        ends = sb("tile_ends", [P, E])
        base = sb("slot_bases", [P, E])
        passed = sb("passed", [P, MOE_TILES, E])
        te = sb("tile_expert_f", [P, MOE_TILES])
        slot_f = sb("slot_f", [P, 2, TILES])
        picked = sb("picked", [P, 2, TILES, E])
        zero_y = sb("zero_y", [P, D_MODEL])
        cnt_ps = ctx.enter_context(nc.psum_tensor("counts_ps", [P, 2, BANK], F32))
        loaded, step, gexp, wexp = sem("route_loaded"), sem("route_step"), sem("g_exp_done"), sem("w_exp_done")
        counted, zeroed, spare_stored, placed = sem("counted"), sem("zeroed_y"), sem("spare_rows_stored"), sem("placed")

        with nc.Block() as block:

            @block.vector
            def _(dve):
                done = [0]

                def link(ins):
                    done[0] += 1
                    ins.then_inc(step, 1)
                    dve.wait_ge(step, done[0])

                def wide(ap, shape):
                    return ap.broadcast_to(shape)

                S3 = [P, TILES, G]

                def first_max(values, maximum, out):
                    link(dve.tensor_tensor(tmp[:, :, :], values, wide(maximum, S3), ALU.is_equal))
                    link(dve.tensor_tensor(tmp[:, :, :], tmp[:, :, :], rank[:, :, :], ALU.mult))
                    link(dve.tensor_reduce(top[:, 3, :, :], tmp[:, :, :], axis=AX.X, op=ALU.max))
                    link(dve.tensor_tensor(out, tmp[:, :, :], wide(top[:, 3, :, :], S3), ALU.is_equal))

                gl = t.logits[:, :, 0:G]
                dve.wait_ge(loaded, 16 * 7)
                link(dve.tensor_reduce(g_max[:, :, :], gl, axis=AX.X, op=ALU.max))
                link(dve.tensor_tensor(g_exp[:, :, :], gl, wide(g_max[:, :, :], S3), ALU.subtract))
                t.n_gdiff = done[0]
                first_max(gl, g_max[:, :, :], g_hot[:, :, :])
                for g in range(G):
                    link(dve.tensor_tensor(prod[:, :, :, g], t.logits[:, :, G + J * g:G + J * g + J],
                                           wide(g_hot[:, :, g:g + 1], [P, TILES, J]), ALU.mult))
                link(dve.tensor_reduce(el[:, :, :], prod[:, :, :, :], axis=AX.X, op=ALU.add))
                link(dve.tensor_reduce(top[:, 0, :, :], el[:, :, :], axis=AX.X, op=ALU.max))
                first_max(el[:, :, :], top[:, 0, :, :], one[:, 0, :, :])
                link(dve.scalar_tensor_tensor(el[:, :, :], one[:, 0, :, :], NEG, el[:, :, :], ALU.mult, ALU.add))
                link(dve.tensor_reduce(top[:, 1, :, :], el[:, :, :], axis=AX.X, op=ALU.max))
                first_max(el[:, :, :], top[:, 1, :, :], one[:, 1, :, :])
                link(dve.tensor_tensor(top[:, 2, :, :], top[:, 1, :, :], top[:, 0, :, :], ALU.subtract))
                t.n_wdiff = done[0]
                for k in range(TOP_K):
                    for g in range(G):
                        link(dve.tensor_tensor(hot[:, k, :, g, :], one[:, k, :, :],
                                               wide(g_hot[:, :, g:g + 1], [P, TILES, J]), ALU.mult))
                link(dve.memset(hot[N_SAMPLE:P, :, PT, :, :], 0.0))
                link(dve.tensor_tensor(member[:, :, :], hot[:, 0, :, :, :].rearrange("p t g j -> p t (g j)"),
                                       hot[:, 1, :, :, :].rearrange("p t g j -> p t (g j)"), ALU.add))
                t.n_member = done[0]
                dve.wait_ge(gexp, 1)
                link(dve.tensor_reduce(g_max[:, :, :], g_exp[:, :, :], axis=AX.X, op=ALU.add))
                dve.wait_ge(wexp, 1)
                link(dve.tensor_scalar_add(top[:, 3, :, :], top[:, 2, :, :], 1.0))
                link(dve.tensor_tensor(g_max[:, :, :], g_max[:, :, :], top[:, 3, :, :], ALU.mult))
                link(dve.reciprocal(t.gates[:, 0, :], g_max[:, :, 0]))
                link(dve.tensor_tensor(t.gates[:, 1, :], t.gates[:, 0, :], top[:, 2, :, 0], ALU.mult))
                dve.wait_ge(counted, 1)
                flat = "p t e -> p (t e)"
                link(dve.tensor_copy(pos[:, :, :].rearrange(flat), cnt_ps[:, 0, 0:TILES * E]))
                link(dve.tensor_copy(total[:, :, :].rearrange(flat), cnt_ps[:, 1, 0:TILES * E]))
                link(dve.memset(carry[:, 0, :], 0.0))
                for n in range(TILES):
                    link(dve.tensor_tensor(carry[:, n + 1, :], carry[:, n, :], total[:, n, :], ALU.add))
                link(dve.tensor_tensor(filled[:, :, :],
                                       wide(carry[:, TILES, :].unsqueeze(2), [P, E, TILES]), limits[:, :, :], ALU.is_gt))
                link(dve.tensor_reduce(n_tiles[:, :], filled[:, :, :], axis=AX.X, op=ALU.add))
                link(dve.tensor_tensor_scan(ends[:, :], n_tiles[:, :], n_tiles[:, :], 0.0, ALU.add, ALU.bypass))
                link(dve.tensor_tensor(base[:, :], ends[:, :], n_tiles[:, :], ALU.subtract))
                link(dve.tensor_scalar_mul(base[:, :], base[:, :], float(P)))
                link(dve.tensor_tensor(passed[:, :, :], tile_no[:, :, :],
                                       wide(ends[:, :].unsqueeze(1), [P, MOE_TILES, E]), ALU.is_ge))
                link(dve.tensor_reduce(te[:, :], passed[:, :, :], axis=AX.X, op=ALU.add))
                link(dve.tensor_scalar_min(te[:, :], te[:, :], float(E - 1)))
                link(dve.tensor_copy(t.tile_expert[:, :], te[0:1, :]))
                link(dve.tensor_tensor(pos[:, :, :], pos[:, :, :], carry[:, 0:TILES, :], ALU.add))
                link(dve.tensor_tensor(pos[:, :, :], pos[:, :, :],
                                       wide(base[:, :].unsqueeze(1), [P, TILES, E]), ALU.add))
                for k in range(TOP_K):
                    link(dve.tensor_tensor(picked[:, k, :, :], hot[:, k, :, :, :].rearrange("p t g j -> p t (g j)"),
                                           pos[:, :, :], ALU.mult))
                    link(dve.tensor_reduce(slot_f[:, k, :], picked[:, k, :, :], axis=AX.X, op=ALU.add))
                    link(dve.tensor_tensor(slot_f[:, k, :], slot_f[:, k, :], spare[:, :], ALU.add))
                    link(dve.tensor_copy(t.slots[:, :].rearrange("p (t k) -> p k t", k=2)[:, k], slot_f[:, k, :]))
                link(dve.tensor_scalar(part_i[:, 0, :], t.slots[:, :], P.bit_length() - 1, None, ALU.logical_shift_right))
                link(dve.tensor_scalar(part_i[:, 1, :], t.slots[:, :], P - 1, None, ALU.bitwise_and))
                link(dve.tensor_copy(part[:, :, :], part_i[:, :, :]))
                t.n_first_place = done[0] + 2
                for n in range(TOP_K * TILES):
                    if n >= 2:
                        dve.wait_ge(placed, n - 1)
                    done[0] += 2
                    dve.tensor_scalar(place[:, n % 2, :], column[:, :], part[:, 1, n:n + 1], None, ALU.is_equal)\
                       .then_inc(step, 1)
                    dve.tensor_scalar(tile_token[:, n % 2, :], column[:, 0:MOE_TILES], part[:, 0, n:n + 1],
                                      token[:, n // TOP_K:n // TOP_K + 1], ALU.is_equal, ALU.mult).then_inc(step, 1)
                dve.wait_ge(placed, TOP_K * TILES)
                link(dve.tensor_copy(t.slot_tok[:, :], cnt_ps[:, 0, 0:MOE_TILES]))

            @block.sync
            def _(sp):
                for dst, src in ((rank, t.rank_const), (limits, t.limits_const), (tile_no, t.tile_no_const)):
                    sp.dma_start(dst[:, :, :], src.partition_broadcast(P)).then_inc(loaded, 16)
                sp.dma_start(column[:, :], t.column_const.partition_broadcast(P)).then_inc(loaded, 16)
                for dst, src in ((spare, t.spare_const), (before, t.before_const), (token, t.token_const)):
                    sp.dma_start(dst[:, :], src).then_inc(loaded, 16)
                sp.wait_ge(zeroed, 1)
                sp.dma_start(t.moe_out[N_SLOTS:N_SLOTS + P, :], zero_y[:, :]).then_inc(spare_stored, 16)
                sp.wait_ge(spare_stored, 16)

            @block.tensor
            def _(pe):
                pe.wait_ge(step, t.n_member)
                pe.matmul(cnt_ps[:, 0, 0:TILES * E], before[:, :], member[:, :, :], start=True, stop=True)
                pe.matmul(cnt_ps[:, 1, 0:TILES * E], t.ones[:, :], member[:, :, :], start=True, stop=True)\
                  .then_inc(counted, 1)
                for n in range(TOP_K * TILES):
                    pe.wait_ge(step, t.n_first_place + 2 * n)
                    pe.matmul(cnt_ps[:, 0, 0:MOE_TILES], place[:, n % 2, :], tile_token[:, n % 2, :], start=(n == 0),
                              stop=(n == TOP_K * TILES - 1)).then_inc(placed, 1)

            @block.scalar
            def _(act):
                act.wait_ge(step, t.n_gdiff)
                act.activation(g_exp[:, :, :], g_exp[:, :, :], ACT.Exp).then_inc(gexp, 1)
                act.wait_ge(step, t.n_wdiff)
                act.activation(top[:, 2, :, :], top[:, 2, :, :], ACT.Exp).then_inc(wexp, 1)

            @block.gpsimd
            def _(pool):
                pool.memset(zero_y[:, :], 0.0).then_inc(zeroed, 1)

        clear(nc, sems)


GU = 2 * D_EXPERT


def experts(nc, t):
    with ExitStack() as ctx:
        sems = []

        def sb(name, shape, dt=F32):
            return ctx.enter_context(nc.sbuf_tensor(name, shape, dt))

        def ps(name, shape):
            return ctx.enter_context(nc.psum_tensor(name, shape, F32))

        def sem(name):
            sems.append(ctx.enter_context(nc.semaphore(name)))
            return sems[-1]

        class TileCount:

            def __init__(self, name, per):
                self.sem, self.per = sem(name), per

            def after(self, tile, k):
                return tile * self.per + (2 * self.per + k + 1)

        FK = D_EXPERT // P
        w_gu = sb("w_gate_up", [P, 2, KC, 2, D_EXPERT])
        w_dn = sb("w_down", [P, 2, FK, D_MODEL])
        rows = sb("slot_rows", [P, 2, D_MODEL])
        idx = sb("slot_index", [P, 2], I32)
        gu_split = sb("w_gate_up_split", [P, 2, 2, KC, GU], F32R)
        dn_split = sb("w_down_split", [P, 2, 2, FK, D_MODEL], F32R)
        xT = sb("slot_rows_T", [P, 2, 2, KC, P], F32R)
        gate = sb("silu_gate", [P, 2, D_EXPERT])
        act_rows = sb("expert_act", [P, 2, D_EXPERT])
        aT = sb("expert_act_T", [P, 2, 2, FK, P], F32R)
        y = sb("expert_out", [P, 2, D_MODEL])
        gu_ps = ps("gate_up_ps", [P, 2, GU])
        xT_ps = ps("slot_rows_T_ps", [P, 2, BANK])
        aT_ps = ps("act_T_ps", [P, BANK])
        y_ps = ps("expert_out_ps", [P, 2, BANK])

        gu_loaded = [sem(f"w_gate_up_loaded{u}") for u in range(2)]
        dn_loaded = [sem(f"w_down_loaded{u}") for u in range(2)]
        rows_loaded = [sem(f"slot_rows_loaded{u}") for u in range(2)]
        y_stored = [sem(f"expert_out_stored{u}") for u in range(2)]
        idx_done = TileCount("slot_index_done", 1)
        xT_done, xT_hi, xT_kept = TileCount("xT_in_psum", 2), TileCount("xT_hi_kept", 2), TileCount("xT_kept", 2)
        gu_hi, gu_lo = TileCount("w_gate_up_hi", 2), TileCount("w_gate_up_lo", 2)
        dn_hi, dn_lo = TileCount("w_down_hi", 1), TileCount("w_down_lo", 1)
        gu_done, silu = TileCount("gate_up_in_psum", 1), TileCount("silu_done", 1)
        a_done, aT_done = TileCount("act_done", 1), TileCount("aT_in_psum", 1)
        aT_hi, aT_kept = TileCount("aT_hi_kept", 1), TileCount("aT_kept", 1)
        y_done = TileCount("y_in_psum", 2)
        y_kept = [TileCount("y_half0_kept", 1), TileCount("y_half1_kept", 1)]

        def tiles(engine, step):
            with engine.Fori(0, MOE_TILES // 2 - 1) as it:
                for u in range(2):
                    step(it * 2 + (1 + u), (1 + u) % 2, it + u)

        PRODUCTS = ((0, 0), (1, 0), (0, 1))
        LAST = MOE_TILES - 1
        assert LAST % 2 == 1

        with nc.Block() as block:

            @block.sync
            def _(sp):
                def load(tile, u):
                    e = sp.value_load(t.tile_expert[0:1, bass.ds(tile, 1)], min_val=0, max_val=N_EXPERTS - 1)
                    sp.wait_ge(gu_lo.sem, gu_lo.after(tile, -3))
                    for n, w in enumerate((t.w_gate, t.w_up)):
                        sp.dma_start(w_gu[:, u, :, n, :], w[bass.ds(e, 1), :, :].rearrange("e (k p) n -> p (e k) n", p=P))\
                          .then_inc(gu_loaded[u], 16)
                    sp.wait_ge(dn_lo.sem, dn_lo.after(tile, -2))
                    sp.dma_start(w_dn[:, u, :, :], t.w_down[bass.ds(e, 1), :, :].rearrange("e (k p) n -> p (e k) n", p=P))\
                      .then_inc(dn_loaded[u], 16)

                with sp.Fori(0, MOE_TILES // 2) as it:
                    for u in range(2):
                        load(it * 2 + u, u)

            @block.gpsimd
            def _(pool):
                pool.sem_inc(idx_done.sem, 2)
                pool.sem_inc(dn_lo.sem, 2)

                def gather(tile, u):
                    pool.wait_ge(xT_done.sem, xT_done.after(tile, -3))
                    pool.tensor_copy(idx[:, u:u + 1], t.slot_tok[:, bass.ds(tile, 1)]).then_inc(idx_done.sem, 1)
                    pool.wait_ge(idx_done.sem, idx_done.after(tile, 0))
                    own_wait(pool, t)
                    pool.indirect_dma_start(rows[:, u, :], None, t.h2[:, :],
                                            bass.IndirectOffsetOnAxis(ap=idx[:, u:u + 1], axis=0))\
                        .then_inc(rows_loaded[u], 16)

                def split_dn(tile, u):
                    pool.wait_ge(dn_hi.sem, dn_hi.after(tile, 0))
                    pool.tensor_tensor(dn_split[:, u, 1, :, :], w_dn[:, u, :, :], dn_split[:, u, 0, :, :].bitcast(F32),
                                       ALU.subtract).then_inc(dn_lo.sem, 1)

                gather(0, 0)
                gather(1, 1)
                split_dn(0, 0)

                def step(tile, u, turn):
                    gather(tile + 1, 1 - u)
                    split_dn(tile, u)

                tiles(pool, step)
                split_dn(LAST, 1)

            @block.tensor
            def _(pe):
                for c in (xT_done, gu_done, aT_done, y_done):
                    pe.sem_inc(c.sem, 2 * c.per)

                def turn_rows(tile, u, turn):
                    pe.wait_ge(rows_loaded[u], turn * 16 + 16)
                    for half in range(2):
                        pe.wait_ge(xT_kept.sem, xT_kept.after(tile, half - 2))
                        for k in range(4):
                            last = pe.transpose(xT_ps[:, half, k * P:(k + 1) * P],
                                                rows[:, u, (4 * half + k) * P:(4 * half + k + 1) * P], t.ident[:, :])
                        last.then_inc(xT_done.sem, 1)

                def gate_up(tile, u, turn):
                    pe.wait_ge(xT_kept.sem, xT_kept.after(tile, 1))
                    pe.wait_ge(a_done.sem, a_done.after(tile, -2))
                    for k in range(KC):
                        if k % 4 == 0:
                            pe.wait_ge(gu_lo.sem, gu_lo.after(tile, k // 4))
                        for m, (a, b) in enumerate(PRODUCTS):
                            last = pe.matmul(gu_ps[:, u, :], xT[:, u, a, k, :], gu_split[:, u, b, k, :],
                                             start=(k == 0 and m == 0), stop=(k == KC - 1 and m == 2))
                    last.then_inc(gu_done.sem, 1)

                def turn_act(tile, u):
                    pe.wait_ge(a_done.sem, a_done.after(tile, 0))
                    pe.wait_ge(aT_kept.sem, aT_kept.after(tile, -1))
                    for k in range(FK):
                        last = pe.transpose(aT_ps[:, k * P:(k + 1) * P], act_rows[:, u, k * P:(k + 1) * P], t.ident[:, :])
                    last.then_inc(aT_done.sem, 1)

                def down(tile, u, turn):
                    pe.wait_ge(aT_kept.sem, aT_kept.after(tile, 0))
                    pe.wait_ge(dn_lo.sem, dn_lo.after(tile, 0))
                    for c in range(2):
                        pe.wait_ge(y_kept[c].sem, y_kept[c].after(tile, -1))
                        for k in range(FK):
                            for m, (a, b) in enumerate(PRODUCTS):
                                last = pe.matmul(y_ps[:, c, :], aT[:, u, a, k, :],
                                                 dn_split[:, u, b, k, c * BANK:(c + 1) * BANK],
                                                 start=(k == 0 and m == 0), stop=(k == FK - 1 and m == 2))
                        last.then_inc(y_done.sem, 1)

                turn_rows(0, 0, 0)
                gate_up(0, 0, 0)
                turn_rows(1, 1, 0)
                turn_act(0, 0)

                def step(tile, u, turn):
                    gate_up(tile, u, turn)
                    turn_rows(tile + 1, 1 - u, turn if u == 0 else turn + 1)
                    down(tile - 1, 1 - u, turn if u == 1 else turn - 1)
                    turn_act(tile, u)

                tiles(pe, step)
                half = MOE_TILES // 2
                gate_up(LAST, 1, half - 1)
                down(LAST - 1, 0, half - 1)
                turn_act(LAST, 1)
                down(LAST, 1, half - 1)

            @block.vector
            def _(dve):
                for c in (a_done, xT_kept, gu_lo, aT_kept, y_kept[1]):
                    dve.sem_inc(c.sem, 2 * c.per)

                def split_gu(tile, u):
                    for half in range(2):
                        at = slice(4 * half, 4 * half + 4)
                        dve.wait_ge(gu_hi.sem, gu_hi.after(tile, half))
                        dve.tensor_tensor(gu_split[:, u, 1, at, :], w_gu[:, u, at, :, :].rearrange("p k c n -> p k (c n)"),
                                          gu_split[:, u, 0, at, :].bitcast(F32), ALU.subtract).then_inc(gu_lo.sem, 1)

                def split_rows(tile, u):
                    for half in range(2):
                        at = slice(4 * half, 4 * half + 4)
                        dve.wait_ge(xT_hi.sem, xT_hi.after(tile, half))
                        dve.tensor_tensor(xT[:, u, 1, at, :], xT_ps[:, half, :].rearrange("p (k c) -> p k c", c=P),
                                          xT[:, u, 0, at, :].bitcast(F32), ALU.subtract).then_inc(xT_kept.sem, 1)

                def split_act(tile, u):
                    dve.wait_ge(aT_hi.sem, aT_hi.after(tile, 0))
                    dve.tensor_tensor(aT[:, u, 1, :, :], aT_ps[:, 0:FK * P].rearrange("p (k c) -> p k c", c=P),
                                      aT[:, u, 0, :, :].bitcast(F32), ALU.subtract).then_inc(aT_kept.sem, 1)

                def multiply(tile, u):
                    dve.wait_ge(silu.sem, silu.after(tile, 0))
                    dve.wait_ge(aT_done.sem, aT_done.after(tile, -2))
                    dve.tensor_tensor(act_rows[:, u, :], gu_ps[:, u, D_EXPERT:GU], gate[:, u, :], ALU.mult)\
                       .then_inc(a_done.sem, 1)

                def keep_y(tile, u, turn):
                    dve.wait_ge(y_done.sem, y_done.after(tile, 1))
                    dve.wait_ge(y_stored[u], turn * 16 + 16)
                    dve.tensor_copy(y[:, u, BANK:D_MODEL], y_ps[:, 1, :]).then_inc(y_kept[1].sem, 1)

                split_gu(0, 0)
                split_rows(0, 0)
                split_gu(1, 1)
                multiply(0, 0)
                split_rows(1, 1)
                split_act(0, 0)

                def step(tile, u, turn):
                    split_gu(tile + 1, 1 - u)
                    multiply(tile, u)
                    split_rows(tile + 1, 1 - u)
                    keep_y(tile - 1, 1 - u, turn if u == 1 else turn - 1)
                    split_act(tile, u)

                tiles(dve, step)
                half = MOE_TILES // 2
                multiply(LAST, 1)
                keep_y(LAST - 1, 0, half - 1)
                split_act(LAST, 1)
                keep_y(LAST, 1, half - 1)

            @block.scalar
            def _(act):
                for c in (silu, gu_hi, dn_hi, xT_hi, aT_hi, y_kept[0]):
                    act.sem_inc(c.sem, 2 * c.per)
                for u in range(2):
                    act.sem_inc(y_stored[u], 16)

                def split_gu(tile, u, turn):
                    for half in range(2):
                        at = slice(4 * half, 4 * half + 4)
                        if half == 0:
                            act.wait_ge(gu_loaded[u], turn * 32 + 32)
                            act.wait_ge(gu_done.sem, gu_done.after(tile, -2))
                        act.activation(gu_split[:, u, 0, at, :], w_gu[:, u, at, :, :].rearrange("p k c n -> p k (c n)"),
                                       ACT.Copy).then_inc(gu_hi.sem, 1)

                def split_dn(tile, u, turn):
                    act.wait_ge(dn_loaded[u], turn * 16 + 16)
                    act.wait_ge(y_done.sem, y_done.after(tile, -3))
                    act.activation(dn_split[:, u, 0, :, :], w_dn[:, u, :, :], ACT.Copy).then_inc(dn_hi.sem, 1)

                def split_rows(tile, u):
                    for half in range(2):
                        act.wait_ge(xT_done.sem, xT_done.after(tile, half))
                        act.wait_ge(gu_done.sem, gu_done.after(tile, -2))
                        act.activation(xT[:, u, 0, 4 * half:4 * half + 4, :],
                                       xT_ps[:, half, :].rearrange("p (k c) -> p k c", c=P), ACT.Copy)\
                           .then_inc(xT_hi.sem, 1)

                def swish(tile, u):
                    act.wait_ge(gu_done.sem, gu_done.after(tile, 0))
                    act.wait_ge(a_done.sem, a_done.after(tile, -2))
                    act.activation(gate[:, u, :], gu_ps[:, u, 0:D_EXPERT], ACT.Silu).then_inc(silu.sem, 1)

                def keep_act(tile, u):
                    act.wait_ge(aT_done.sem, aT_done.after(tile, 0))
                    act.wait_ge(y_done.sem, y_done.after(tile, -3))
                    act.activation(aT[:, u, 0, :, :], aT_ps[:, 0:FK * P].rearrange("p (k c) -> p k c", c=P), ACT.Copy)\
                       .then_inc(aT_hi.sem, 1)

                def keep_y(tile, u, turn):
                    act.wait_ge(y_done.sem, y_done.after(tile, 0))
                    act.wait_ge(y_stored[u], turn * 16 + 16)
                    act.activation(y[:, u, 0:BANK], y_ps[:, 0, :], ACT.Copy).then_inc(y_kept[0].sem, 1)

                def store_y(tile, u):
                    act.wait_ge(y_kept[0].sem, y_kept[0].after(tile, 0))
                    act.wait_ge(y_kept[1].sem, y_kept[1].after(tile, 0))
                    act.dma_start(row_tile(t.moe_out, tile), y[:, u, :]).then_inc(y_stored[u], 16)

                split_gu(0, 0, 0)
                split_rows(0, 0)
                split_gu(1, 1, 0)
                split_dn(0, 0, 0)
                swish(0, 0)
                split_rows(1, 1)
                keep_act(0, 0)

                def step(tile, u, turn):
                    split_gu(tile + 1, 1 - u, turn if u == 0 else turn + 1)
                    split_dn(tile, u, turn)
                    swish(tile, u)
                    split_rows(tile + 1, 1 - u)
                    keep_y(tile - 1, 1 - u, turn if u == 1 else turn - 1)
                    keep_act(tile, u)
                    store_y(tile - 1, 1 - u)

                tiles(act, step)
                half = MOE_TILES // 2
                split_dn(LAST, 1, half - 1)
                swish(LAST, 1)
                keep_y(LAST - 1, 0, half - 1)
                keep_act(LAST, 1)
                store_y(LAST - 1, 0)
                keep_y(LAST, 1, half - 1)
                store_y(LAST, 1)
                for u in range(2):
                    act.wait_ge(y_stored[u], 16 * (half + 1))

        clear(nc, sems)


def combine(nc, t):
    with ExitStack() as ctx:
        sems = []

        def sb(name, shape, dt=F32):
            return ctx.enter_context(nc.sbuf_tensor(name, shape, dt))

        def sem(name):
            sems.append(ctx.enter_context(nc.semaphore(name)))
            return sems[-1]

        U = 3
        TURNS3 = TILES // U
        assert TILES % U == 0
        x = sb("x1_again", [P, U, D_MODEL])
        rows = sb("expert_rows", [P, U, TOP_K, D_MODEL])
        g_row = sb("g_final_row", [P, D_MODEL])
        square = sb("square3", [P, D_MODEL])
        out = sb("out_rows", [P, U, D_MODEL])
        ss = sb("sum_squares3", [P, U, 3])
        g_loaded = sem("g_final_loaded")
        x_loaded = [sem(f"x1_loaded{u}") for u in range(U)]
        rows_loaded = [sem(f"expert_rows_loaded{u}") for u in range(U)]
        stored = [sem(f"out_stored{u}") for u in range(U)]
        sums = Count(sem("expert_rows_added"), 2 * U)
        squares = Count(sem("squares3_done"), U)
        rstd_step = Count(sem("rstd3_step"), U)
        rstd = Count(sem("rstd3_done"), U)
        normed = Count(sem("out_done"), U)

        with nc.Block() as block:

            @block.sync
            def _(sp):
                for u in range(U):
                    sp.dma_start(x[:, u, :], row_tile(t.x1, u)).then_inc(x_loaded[u], 16)
                sp.dma_start(g_row[:, :], t.g_final.partition_broadcast(P)).then_inc(g_loaded, 16)
                for u in range(U):
                    sp.sem_inc(stored[u], 16)

                def tile(it, u, final=False):
                    sp.wait_ge(normed.sem, normed.after(it, u))
                    sp.dma_start(row_tile(t.y, it * U + u), out[:, u, :]).then_inc(stored[u], 16)
                    if not final:
                        sp.dma_start(x[:, u, :], row_tile(t.x1, (it + 1) * U + u)).then_inc(x_loaded[u], 16)

                with sp.Fori(0, TURNS3 - 1) as it:
                    for u in range(U):
                        tile(it, u)
                for u in range(U):
                    tile(TURNS3 - 1, u, final=True)
                for u in range(U):
                    sp.wait_ge(stored[u], 16 * (1 + TURNS3))

            @block.gpsimd
            def _(pool):
                for c in (rstd_step, rstd):
                    pool.sem_inc(c.sem, c.per)

                def gather(n):
                    u, it = n % U, n // U
                    if it:
                        pool.wait_ge(sums.sem, sums.after(it, 2 * (u - U) + 1))
                    for k in range(TOP_K):
                        pool.indirect_dma_start(rows[:, u, k, :], None, t.moe_out[:, :],
                                                bass.IndirectOffsetOnAxis(ap=t.slots[:, n * TOP_K + k:n * TOP_K + k + 1],
                                                                          axis=0))\
                            .then_inc(rows_loaded[u], 16)

                for n in range(U - 1):
                    gather(n)
                for n in range(TILES):
                    it, u = n // U, n % U
                    if n + U - 1 < TILES:
                        gather(n + U - 1)
                    pool.wait_ge(squares.sem, squares.after(it, u))
                    pool.tensor_scalar(ss[:, u, 1:2], ss[:, u, 0:1], 1.0 / D_MODEL, NORM_EPS, ALU.mult, ALU.add)\
                        .then_inc(rstd_step.sem, 1)
                    pool.wait_ge(rstd_step.sem, rstd_step.after(it, u))
                    pool.wait_ge(normed.sem, normed.after(it, u - U))
                    pool.tensor_tensor(ss[:, u, 2:3], ss[:, u, 1:2], t.neg_half[:, :], ALU.pow).then_inc(rstd.sem, 1)

            @block.vector
            def _(dve):
                for c in (sums, normed):
                    dve.sem_inc(c.sem, c.per)
                dve.wait_ge(g_loaded, 16)

                def add(it, u):
                    dve.wait_ge(x_loaded[u], it * 16 + 16)
                    dve.wait_ge(rows_loaded[u], it * 32 + 32)
                    for k in range(TOP_K):
                        if k:
                            dve.wait_ge(sums.sem, sums.after(it, 2 * u + k - 1))
                        dve.scalar_tensor_tensor(x[:, u, :], rows[:, u, k, :], t.gates[:, k, bass.ds(it * U + u, 1)],
                                                 x[:, u, :], ALU.mult, ALU.add).then_inc(sums.sem, 1)

                def tile(it, u, final=False):
                    if not final:
                        add(it + (u + 1) // U, (u + 1) % U)
                    dve.wait_ge(rstd.sem, rstd.after(it, u))
                    dve.wait_ge(stored[u], it * 16 + 16)
                    dve.wait_ge(sums.sem, sums.after(it, 2 * u + 1))
                    dve.scalar_tensor_tensor(out[:, u, :], x[:, u, :], ss[:, u, 2:3], g_row[:, :], ALU.mult, ALU.mult)\
                       .then_inc(normed.sem, 1)

                add(0, 0)
                with dve.Fori(0, TURNS3 - 1) as it:
                    for u in range(U):
                        tile(it, u)
                for u in range(U):
                    tile(TURNS3 - 1, u, final=u == U - 1)

            @block.scalar
            def _(act):
                act.sem_inc(squares.sem, squares.per)
                with act.Fori(0, TURNS3) as it:
                    for u in range(U):
                        act.wait_ge(sums.sem, sums.after(it, 2 * u + 1))
                        act.wait_ge(squares.sem, squares.after(it, u - 1))
                        act.activation(square[:, :], x[:, u, :], ACT.Square, accum_out=ss[:, u, 0:1])\
                           .then_inc(squares.sem, 1)

        clear(nc, sems)


def buckets_of(n):
    exact = N_BUCKETS // 2
    ratio = np.maximum(n, 1).astype(np.float32) / np.float32(exact)
    large = exact + (np.log(ratio) / np.float32(math.log(MAX_DISTANCE / exact)) * np.float32(N_BUCKETS - exact))\
        .astype(np.int32)
    return np.where(n < exact, n, np.minimum(large, N_BUCKETS - 1))


def host_constants():
    n = 2 * P - 1 - np.arange(DIST)
    table = np.zeros((N_BUCKETS + 2, DIST), np.float32)
    seen = n >= 0
    table[buckets_of(np.maximum(n, 0))[seen], np.arange(DIST)[seen]] += 1
    table[N_BUCKETS - 1, seen] -= 1
    table[N_BUCKETS, n < 0] = NEG
    table[N_BUCKETS + 1, n <= 0] = NEG
    mask_rows = np.zeros((2, H_DIFF + 1), np.float32)
    mask_rows[0, :H_DIFF] = 1
    mask_rows[1, H_DIFF] = 1
    half = np.arange(P) // DEC_SEQ % 2
    half_map = np.stack([1 - half, half], 1).astype(np.float32)
    e = N_EXPERTS
    rank = np.tile(np.arange(N_GROUPS, 0, -1, dtype=np.float32), (TILES, 1))
    limits = np.tile(P * np.arange(TILES, dtype=np.float32), (e, 1))
    tile_no = np.repeat(np.arange(MOE_TILES, dtype=np.float32)[:, None], e, 1)
    spare = np.zeros((P, TILES), np.float32)
    spare[N_SAMPLE:, PT] = N_SLOTS + np.arange(N_SAMPLE, P)
    before = np.triu(np.ones((P, P), np.float32), 1)
    token = (np.arange(TILES)[None] * P + np.arange(P)[:, None]).astype(np.float32)
    more = {"rank_const": rank, "limits_const": limits, "tile_no_const": tile_no, "spare_const": spare,
            "before_const": before, "token_const": token,
            "column_const": np.arange(P, dtype=np.float32)}
    return more | {"bucket_table": table, "mask_rows": mask_rows, "half_map": half_map, "eye": np.eye(P, dtype=np.float32)}


INPUTS = ["x", "cache_d", "cache_s", "page_table", "rel_bias", "g_mix", "w_in", "lambda_q1", "lambda_k1", "lambda_q2",
          "lambda_k2", "subln_g", "w_out", "g_ffn", "w_group", "b_group", "w_erouter", "b_erouter", "w_gate", "w_up",
          "w_down", "g_final", "eye", "bucket_table", "mask_rows", "half_map", "rank_const", "limits_const",
          "tile_no_const", "column_const", "spare_const", "before_const", "token_const"]
OUTPUTS = ["y", "new_kvd", "new_kvs"]


def step_kernel(nc, t):
    def scratch(name, shape, dt=F32):
        return nc.dram_tensor(name, shape, dt).ap()

    t.n_pool = t.cache_d.shape[0]
    t.qT = scratch("scratch_qT", (P, BLOCKS, ALL))
    t.kT = scratch("scratch_kT", (P, BLOCKS, ALL))
    t.oT = scratch("scratch_oT", (P, BLOCKS, ALL))
    t.bias_dram = scratch("scratch_bias", (H_DIFF + 1, P, DIST))
    t.near_dram = scratch("scratch_near", (H_DIFF, P, NEAR))
    t.x1 = scratch("scratch_x1", (ALL, D_MODEL))
    t.h2 = scratch("scratch_h2", (ALL, D_MODEL))
    t.moe_out = scratch("scratch_moe_out", (N_SLOTS + P, D_MODEL))
    with ExitStack() as ctx:
        constants(nc, ctx, t)
        t.logits = ctx.enter_context(nc.sbuf_tensor("logits", [P, TILES, N_LOGITS], F32))
        with ExitStack() as att:
            table_places(nc, att, t)
            project(nc, t)
            t.sample_o = att.enter_context(nc.sbuf_tensor("sample_o", [P, DEC_BATCH, P], F32))
            attention(nc, t, DIFF)
            attention(nc, t, STICK)
            t.w_out_split = att.enter_context(nc.sbuf_tensor("w_out_split", [P, 2, BLOCKS, D_MODEL], F32R))
            sample_heads_out(nc, t)
            mix_out(nc, t)
        t.gates = ctx.enter_context(nc.sbuf_tensor("gates", [P, TOP_K, TILES], F32))
        t.slots = ctx.enter_context(nc.sbuf_tensor("slots", [P, TOP_K * TILES], I32))
        t.slot_tok = ctx.enter_context(nc.sbuf_tensor("slot_tok", [P, MOE_TILES], I32))
        t.tile_expert = ctx.enter_context(nc.sbuf_tensor("tile_expert", [1, MOE_TILES], I32))
        route(nc, t)
        experts(nc, t)
        combine(nc, t)


def kernel(**inputs):
    import concourse.bacc as bacc
    from types import SimpleNamespace
    from concourse.bass_utils import run_bass_kernel_spmd

    a = {k: np.asarray(v) for k, v in inputs.items()}
    n_pool = a["cache_kv_diff"].shape[0]
    host = host_constants()
    host["x"] = np.concatenate([a["x_prompt"].reshape(SEQ, D_MODEL), a["x_sample"].reshape(N_SAMPLE, D_MODEL),
                                np.zeros((ALL - SEQ - N_SAMPLE, D_MODEL), a["x_prompt"].dtype)])
    host["cache_d"] = a["cache_kv_diff"].reshape(n_pool, PAGE, 2 * HALF_W)
    host["cache_s"] = a["cache_kv_sb"].reshape(n_pool, PAGE, 2 * HALF_W)
    host["w_erouter"] = a["w_erouter"][0].reshape(D_MODEL, N_EXPERTS)
    host["b_erouter"] = a["b_erouter"][0].reshape(N_EXPERTS)
    for name in ("w_gate", "w_up"):
        host[name] = a[name][0].reshape(N_EXPERTS, D_MODEL, D_EXPERT)
    host["w_down"] = a["w_down"][0].reshape(N_EXPERTS, D_EXPERT, D_MODEL)
    for name in ("page_table", "rel_bias", "g_final"):
        host[name] = a[name]
    for name in ("g_mix", "w_in", "lambda_q1", "lambda_k1", "lambda_q2", "lambda_k2", "subln_g", "w_out", "g_ffn",
                 "w_group", "b_group"):
        host[name] = a[name][0]

    nc = bacc.Bacc("TRN2", target_bir_lowering=False, num_devices=1)
    arrays, dram = {}, {}
    for name in INPUTS:
        arrays[f"in_{name}"] = np.ascontiguousarray(host[name])
        dram[name] = nc.dram_tensor(f"in_{name}", host[name].shape, mybir.dt.from_np(host[name].dtype),
                                    kind="ExternalInput").ap()
    for name in OUTPUTS:
        dram[name] = nc.dram_tensor(f"out_{name}", (ALL, D_MODEL), F32, kind="ExternalOutput").ap()
    step_kernel(nc, SimpleNamespace(**dram))
    r = run_bass_kernel_spmd(nc, [arrays], core_ids=[0]).results[0]

    def rows(name, *shape):
        out = r[f"out_{name}"]
        return out[0:SEQ].reshape(1, SEQ, *shape), out[SEQ:SEQ + N_SAMPLE].reshape(DEC_BATCH, DEC_SEQ, *shape)

    y_p, y_s = rows("y", D_MODEL)
    kvd_p, kvd_s = rows("new_kvd", 1, 2, H_DIFF, 2 * HEAD)
    kvs_p, kvs_s = rows("new_kvs", 1, 2, H_SB, HEAD)
    return y_p, y_s, kvd_p, kvs_p, kvd_s, kvs_s
```
